# Optimizing a Trainium2 kernel written in Bass

```python
import jax, jax.numpy as jnp
from jax import lax
import numpy as np

D_MODEL = 1024
BATCH = 1
SEQ = 512
DEPTH = 2

CHUNK = 64
QBLOCK = 128
N_A = DEPTH // 2
N_B = DEPTH - N_A
FOX_HEADS = 16
FOX_HEAD_DIM = 64
FOX_WIDTH = FOX_HEADS * FOX_HEAD_DIM
MLA_HEADS = 16
MLA_NOPE = 128
MLA_ROPE = 64
MLA_V = 128
KV_LORA = 256
Q_LORA = 768
ROPE_THETA = 10000.0
D_FF = 2816
CONV_W = 3
EPS = 1e-6


def rmsnorm(x, g):
    xf = x.astype(jnp.float32)
    y = xf * lax.rsqrt(jnp.mean(xf * xf, axis=-1, keepdims=True) + EPS)
    return (y * g.astype(jnp.float32)).astype(x.dtype)

def rope_tables(seq, dtype):
    pos = jnp.arange(seq, dtype=jnp.float32)
    inv = ROPE_THETA ** (-jnp.arange(0, MLA_ROPE, 2, dtype=jnp.float32) / MLA_ROPE)
    ang = pos[:, None] * inv[None, :]
    return jnp.cos(ang).astype(dtype), jnp.sin(ang).astype(dtype)

def apply_rope(x, cos, sin):
    x1, x2 = jnp.split(x, 2, axis=-1)
    return jnp.concatenate([x1 * cos - x2 * sin, x1 * sin + x2 * cos], axis=-1)

def to_blocks(a):
    b, s = a.shape[:2]
    a = a.reshape((b, s // QBLOCK, QBLOCK) + a.shape[2:])
    return jnp.moveaxis(a, 1, 0)

def from_blocks(a):
    a = jnp.moveaxis(a, 0, 1)
    return a.reshape((a.shape[0], a.shape[1] * a.shape[2]) + a.shape[3:])

def fox_mixer(h, w_in, b_f, w_out):
    b, s_len, _ = h.shape
    proj = h @ w_in
    qkv = proj[..., :3 * FOX_WIDTH].reshape(b, s_len, 3, FOX_HEADS, FOX_HEAD_DIM)
    q, k, v = qkv[:, :, 0], qkv[:, :, 1], qkv[:, :, 2]
    logf = jax.nn.log_sigmoid((proj[..., 3 * FOX_WIDTH:] + b_f).astype(jnp.float32))
    cum = jnp.cumsum(logf, axis=1)
    cum_k = jnp.transpose(cum, (0, 2, 1))
    kpos = jnp.arange(s_len)
    scale = FOX_HEAD_DIM ** -0.5

    def block(args):
        i, qi, ci = args
        sc = jnp.einsum('bqhd,bkhd->bhqk', qi, k, preferred_element_type=jnp.float32) * scale
        sc = sc + (jnp.transpose(ci, (0, 2, 1))[..., :, None] - cum_k[:, :, None, :])
        qpos = i * QBLOCK + jnp.arange(QBLOCK)
        sc = jnp.where(kpos[None, :] <= qpos[:, None], sc, -jnp.inf)
        p = jax.nn.softmax(sc, axis=-1).astype(v.dtype)
        return jnp.einsum('bhqk,bkhd->bqhd', p, v)

    o = lax.map(block, (jnp.arange(s_len // QBLOCK), to_blocks(q), to_blocks(cum)))
    return from_blocks(o).reshape(b, s_len, FOX_WIDTH) @ w_out

def mla_shared_kv(x, kv_in_g, w_dkv, kv_norm_g, w_uk, w_uv, cos, sin):
    b, s_len, _ = x.shape
    ckv = rmsnorm(x, kv_in_g) @ w_dkv
    latent = rmsnorm(ckv[..., :KV_LORA], kv_norm_g)
    k_rope = apply_rope(ckv[..., KV_LORA:], cos, sin)
    k_nope = (latent @ w_uk).reshape(b, s_len, MLA_HEADS, MLA_NOPE)
    v = (latent @ w_uv).reshape(b, s_len, MLA_HEADS, MLA_V)
    return k_nope, k_rope, v

def mla_mixer(h, w_dq, q_norm_g, w_uq, w_out, k_nope, k_rope, v, cos, sin):
    b, s_len, _ = h.shape
    q = (rmsnorm(h @ w_dq, q_norm_g) @ w_uq).reshape(b, s_len, MLA_HEADS, MLA_NOPE + MLA_ROPE)
    q_nope = q[..., :MLA_NOPE]
    q_rope = apply_rope(q[..., MLA_NOPE:], cos[:, None, :], sin[:, None, :])
    kpos = jnp.arange(s_len)
    scale = (MLA_NOPE + MLA_ROPE) ** -0.5

    def block(args):
        i, qn, qr = args
        sc = (jnp.einsum('bqhd,bkhd->bhqk', qn, k_nope, preferred_element_type=jnp.float32)
              + jnp.einsum('bqhr,bkr->bhqk', qr, k_rope, preferred_element_type=jnp.float32)) * scale
        qpos = i * QBLOCK + jnp.arange(QBLOCK)
        visible = kpos[None, :] < (qpos[:, None] // CHUNK + 1) * CHUNK
        sc = jnp.where(visible, sc, -jnp.inf)
        p = jax.nn.softmax(sc, axis=-1).astype(v.dtype)
        return jnp.einsum('bhqk,bkhd->bqhd', p, v)

    o = lax.map(block, (jnp.arange(s_len // QBLOCK), to_blocks(q_nope), to_blocks(q_rope)))
    return from_blocks(o).reshape(b, s_len, MLA_HEADS * MLA_V) @ w_out

def conv_ffn(h, w_in, conv_w, conv_b, w_out):
    s_len = h.shape[1]
    u = h @ w_in
    up = jnp.pad(u, ((0, 0), (CONV_W - 1, 0), (0, 0)))
    u = conv_b + sum(up[:, j:j + s_len] * conv_w[j] for j in range(CONV_W))
    gate, val = jnp.split(u, 2, axis=-1)
    return (jax.nn.silu(gate) * val) @ w_out

def first_inputs(seed: int = 0) -> dict:
    key = jax.random.key(seed)
    ks = jax.random.split(key, 24)
    f32 = jnp.float32
    res = (2.0 * DEPTH) ** -0.5

    def nrm(k, shape, scale):
        return jax.random.normal(k, shape, f32) * scale

    def gain(k, shape):
        return 1.0 + 0.02 * jax.random.normal(k, shape, f32)

    w_fox_in = jnp.concatenate([
        nrm(ks[2], (N_A, D_MODEL, 3 * FOX_WIDTH), D_MODEL ** -0.5),
        nrm(ks[3], (N_A, D_MODEL, FOX_HEADS), 0.1 * D_MODEL ** -0.5)], axis=-1)
    return {
        'x': jax.random.normal(ks[0], (BATCH, SEQ, D_MODEL), f32),
        'fox_norm': gain(ks[1], (N_A, D_MODEL)),
        'w_fox_in': w_fox_in,
        'b_fox_f': jax.random.uniform(ks[4], (N_A, FOX_HEADS), f32, 1.0, 6.0),
        'w_fox_out': nrm(ks[5], (N_A, FOX_WIDTH, D_MODEL), FOX_WIDTH ** -0.5 * res),
        'kv_in_norm': gain(ks[6], (D_MODEL,)),
        'w_dkv': nrm(ks[7], (D_MODEL, KV_LORA + MLA_ROPE), D_MODEL ** -0.5),
        'kv_norm': gain(ks[8], (KV_LORA,)),
        'w_uk': nrm(ks[9], (KV_LORA, MLA_HEADS * MLA_NOPE), KV_LORA ** -0.5),
        'w_uv': nrm(ks[10], (KV_LORA, MLA_HEADS * MLA_V), KV_LORA ** -0.5),
        'mla_norm': gain(ks[11], (N_B, D_MODEL)),
        'w_dq': nrm(ks[12], (N_B, D_MODEL, Q_LORA), D_MODEL ** -0.5),
        'q_norm': gain(ks[13], (N_B, Q_LORA)),
        'w_uq': nrm(ks[14], (N_B, Q_LORA, MLA_HEADS * (MLA_NOPE + MLA_ROPE)), Q_LORA ** -0.5),
        'w_mla_out': nrm(ks[15], (N_B, MLA_HEADS * MLA_V, D_MODEL), (MLA_HEADS * MLA_V) ** -0.5 * res),
        'ffn_norm': gain(ks[16], (DEPTH, D_MODEL)),
        'w_ffn_in': nrm(ks[17], (DEPTH, D_MODEL, 2 * D_FF), D_MODEL ** -0.5),
        'ffn_conv_w': nrm(ks[18], (DEPTH, CONV_W, 2 * D_FF), CONV_W ** -0.5),
        'ffn_conv_b': nrm(ks[19], (DEPTH, 2 * D_FF), 0.01),
        'w_ffn_out': nrm(ks[20], (DEPTH, D_FF, D_MODEL), D_FF ** -0.5 * res),
        'final_norm': gain(ks[21], (D_MODEL,)),
    }

def first_block(x, fox_norm, w_fox_in, b_fox_f, w_fox_out, kv_in_norm, w_dkv, kv_norm, w_uk, w_uv,
              mla_norm, w_dq, q_norm, w_uq, w_mla_out, ffn_norm, w_ffn_in, ffn_conv_w, ffn_conv_b,
              w_ffn_out, final_norm):
    cos, sin = rope_tables(x.shape[1], x.dtype)
    k_nope = k_rope = v = None
    for layer in range(DEPTH):
        if layer < N_A:
            x = x + fox_mixer(rmsnorm(x, fox_norm[layer]), w_fox_in[layer], b_fox_f[layer],
                              w_fox_out[layer])
        else:
            if layer == N_A:
                k_nope, k_rope, v = mla_shared_kv(x, kv_in_norm, w_dkv, kv_norm, w_uk, w_uv, cos, sin)
            j = layer - N_A
            x = x + mla_mixer(rmsnorm(x, mla_norm[j]), w_dq[j], q_norm[j], w_uq[j], w_mla_out[j],
                              k_nope, k_rope, v, cos, sin)
        x = x + conv_ffn(rmsnorm(x, ffn_norm[layer]), w_ffn_in[layer], ffn_conv_w[layer],
                         ffn_conv_b[layer], w_ffn_out[layer])
    return rmsnorm(x, final_norm)


N_EVEN = (DEPTH + 1) // 2
N_ODD = DEPTH // 2

NSA_HEADS = 8
HEAD_DIM = 64
KV_GROUPS = 2
HEADS_PER_GROUP = NSA_HEADS // KV_GROUPS
N_BRANCH = 3
CMP_BLOCK = 32
CMP_STRIDE = 16
CMP_HIDDEN = 128
SEL_BLOCK = 64
SEL_TOPK = 8
WINDOW = 512
Q_BLOCK = 128
FORCE_BONUS = 1e4
NEG = -1e30

POOL_WIDTH = D_MODEL // 2
POOL_WINDOWS = (2, 4, 8, 16)
POOL_GROUPS = len(POOL_WINDOWS)
POOL_GROUP_DIM = POOL_WIDTH // POOL_GROUPS

NSA_WIDTH = NSA_HEADS * HEAD_DIM
KV_WIDTH = KV_GROUPS * HEAD_DIM
GATE_WIDTH = NSA_HEADS * N_BRANCH
IN_WIDTH = NSA_WIDTH + N_BRANCH * 2 * KV_WIDTH + GATE_WIDTH + POOL_WIDTH
MIX_WIDTH = NSA_WIDTH + POOL_WIDTH

CONV_WIDTH = 31

FFN_HIDDEN = -(-8 * D_MODEL // (3 * 256)) * 256


def rmsnorm_2(x, g, eps=1e-6):
    xf = x.astype(jnp.float32)
    y = xf * lax.rsqrt(jnp.mean(xf * xf, axis=-1, keepdims=True) + eps)
    return (y * g.astype(jnp.float32)).astype(x.dtype)

def layernorm(x, g, b, eps=1e-5):
    xf = x.astype(jnp.float32)
    mu = jnp.mean(xf, axis=-1, keepdims=True)
    xc = xf - mu
    var = jnp.mean(xc * xc, axis=-1, keepdims=True)
    y = xc * lax.rsqrt(var + eps) * g.astype(jnp.float32) + b.astype(jnp.float32)
    return y.astype(x.dtype)

def alibi_slopes():
    h = jnp.arange(1, NSA_HEADS + 1, dtype=jnp.float32)
    return jnp.exp2(-8.0 * h / NSA_HEADS).reshape(KV_GROUPS, HEADS_PER_GROUP)

def compress_blocks(kv, pos, w1, w2):
    b, g, s, dh = kv.shape
    r = CMP_BLOCK // CMP_STRIDE
    n_cmp = s // CMP_STRIDE - r + 1
    sub = kv.reshape(b, g, s // CMP_STRIDE, CMP_STRIDE, dh)
    blocks = jnp.concatenate([sub[:, :, j:j + n_cmp] for j in range(r)], axis=3)
    blocks = (blocks + pos).reshape(b, g, n_cmp, CMP_BLOCK * dh)
    return jax.nn.gelu(blocks @ w1) @ w2

def compressed_branch(q, kc, vc, slopes):
    s = q.shape[3]
    n_cmp = kc.shape[2]
    t = jnp.arange(s, dtype=jnp.int32)[:, None]
    end = jnp.arange(n_cmp, dtype=jnp.int32)[None, :] * CMP_STRIDE + (CMP_BLOCK - 1)
    dist = (t - end).astype(jnp.float32)
    valid = dist >= 0
    logits = jnp.einsum('bgrtd,bgnd->bgrtn', q, kc).astype(jnp.float32)
    logits = logits - slopes[:, :, None, None] * dist
    logits = jnp.where(valid, logits, NEG)
    p = jax.nn.softmax(logits, axis=-1) * valid
    o = jnp.einsum('bgrtn,bgnd->bgrtd', p.astype(vc.dtype), vc)
    return o, p

def selection_indices(p_cmp, s):
    n_cmp = p_cmp.shape[-1]
    n_sel = s // SEL_BLOCK
    c0 = np.arange(n_cmp)[:, None] * CMP_STRIDE
    s0 = np.arange(n_sel)[None, :] * SEL_BLOCK
    overlap = np.clip(np.minimum(c0 + CMP_BLOCK, s0 + SEL_BLOCK) - np.maximum(c0, s0), 0, None) / CMP_BLOCK
    imp = jnp.einsum('bgtn,nj->bgtj', p_cmp.sum(axis=2), jnp.asarray(overlap, jnp.float32))
    t_blk = (jnp.arange(s, dtype=jnp.int32) // SEL_BLOCK)[:, None]
    j = jnp.arange(n_sel, dtype=jnp.int32)[None, :]
    forced = (j == 0) | (j == t_blk) | (j == t_blk - 1)
    imp = jnp.where(forced, imp + FORCE_BONUS, imp)
    imp = jnp.where(j > t_blk, NEG, imp)
    _, idx = lax.top_k(imp, min(SEL_TOPK, n_sel))
    return idx

def selected_branch(q, ks, vs, idx, slopes):
    b, g, r, s, dh = q.shape
    k = idx.shape[-1]
    n_sel = s // SEL_BLOCK
    nq = s // Q_BLOCK
    kb = ks.reshape(b, g, n_sel, SEL_BLOCK, dh)
    vb = vs.reshape(b, g, n_sel, SEL_BLOCK, dh)
    qc = jnp.moveaxis(q.reshape(b, g, r, nq, Q_BLOCK, dh), 3, 0)
    ic = jnp.moveaxis(idx.reshape(b, g, nq, Q_BLOCK, k), 2, 0)
    tc = jnp.arange(s, dtype=jnp.int32).reshape(nq, Q_BLOCK)
    bi = jnp.arange(b)[:, None, None, None]
    gi = jnp.arange(g)[None, :, None, None]
    offs = jnp.arange(SEL_BLOCK, dtype=jnp.int32)

    def one_block(args):
        qq, ii, tt = args
        k_sel = kb[bi, gi, ii].reshape(b, g, Q_BLOCK, k * SEL_BLOCK, dh)
        v_sel = vb[bi, gi, ii].reshape(b, g, Q_BLOCK, k * SEL_BLOCK, dh)
        pos = (ii[..., None] * SEL_BLOCK + offs).reshape(b, g, Q_BLOCK, k * SEL_BLOCK)
        dist = (tt[None, None, :, None] - pos).astype(jnp.float32)[:, :, None]
        logits = jnp.einsum('bgrqd,bgqkd->bgrqk', qq, k_sel).astype(jnp.float32)
        logits = logits - slopes[None, :, :, None, None] * dist
        logits = jnp.where(dist >= 0, logits, NEG)
        p = jax.nn.softmax(logits, axis=-1)
        return jnp.einsum('bgrqk,bgqkd->bgrqd', p.astype(v_sel.dtype), v_sel)

    o = lax.map(one_block, (qc, ic, tc))
    return jnp.moveaxis(o, 0, 3).reshape(b, g, r, s, dh)

def window_branch(q, kw, vw, slopes):
    b, g, r, s, dh = q.shape
    nq = s // Q_BLOCK
    nw = WINDOW // Q_BLOCK
    pad = ((0, 0), (0, 0), (WINDOW, 0), (0, 0))
    kp = jnp.pad(kw, pad).reshape(b, g, nq + nw, Q_BLOCK, dh)
    vp = jnp.pad(vw, pad).reshape(b, g, nq + nw, Q_BLOCK, dh)
    k_band = jnp.concatenate([kp[:, :, j:j + nq] for j in range(nw + 1)], axis=3)
    v_band = jnp.concatenate([vp[:, :, j:j + nq] for j in range(nw + 1)], axis=3)
    qb = q.reshape(b, g, r, nq, Q_BLOCK, dh)
    t = jnp.arange(s, dtype=jnp.int32).reshape(nq, Q_BLOCK)
    kpos = (jnp.arange(nq, dtype=jnp.int32)[:, None] - nw) * Q_BLOCK + jnp.arange((nw + 1) * Q_BLOCK, dtype=jnp.int32)[None, :]
    dist = t[:, :, None] - kpos[:, None, :]
    valid = (dist >= 0) & (dist < WINDOW) & (kpos[:, None, :] >= 0)
    logits = jnp.einsum('bgrnqd,bgnkd->bgrnqk', qb, k_band).astype(jnp.float32)
    logits = logits - slopes[:, :, None, None, None] * dist.astype(jnp.float32)
    logits = jnp.where(valid, logits, NEG)
    p = jax.nn.softmax(logits, axis=-1)
    o = jnp.einsum('bgrnqk,bgnkd->bgrnqd', p.astype(v_band.dtype), v_band)
    return o.reshape(b, g, r, s, dh)

def multiscale_pool(u, w_pool, scale):
    b, s, c = u.shape
    uf = u.astype(jnp.float32)
    cs = jnp.pad(jnp.cumsum(uf, axis=1), ((0, 0), (1, 0), (0, 0)))
    t = jnp.arange(s, dtype=jnp.float32)
    outs = []
    for gi, w in enumerate(POOL_WINDOWS):
        sl = slice(gi * POOL_GROUP_DIM, (gi + 1) * POOL_GROUP_DIM)
        csg = cs[:, :, sl]
        start = jnp.pad(csg, ((0, 0), (w - 1, 0), (0, 0)))[:, :s]
        mean = (csg[:, 1:] - start) / jnp.minimum(t + 1.0, float(w))[None, :, None]
        outs.append(mean - uf[:, :, sl])
    d = jnp.stack(outs, axis=2).astype(u.dtype)
    y = jnp.einsum('bsgc,gce->bsge', d, w_pool).reshape(b, s, c)
    return y * scale

def nsa_pool_mixer(h, w_in, pos_k, pos_v, k_w1, k_w2, v_w1, v_w2, w_pool, pool_scale, w_out):
    b, s, _ = h.shape
    proj = h @ w_in
    sizes = [NSA_WIDTH] + [KV_WIDTH] * (2 * N_BRANCH) + [GATE_WIDTH]
    cuts = [int(c) for c in np.cumsum(sizes)]
    q, kc, vc, ks, vs, kw, vw, gate, u = jnp.split(proj, cuts, axis=-1)

    def kv_heads(z):
        return z.reshape(b, s, KV_GROUPS, HEAD_DIM).transpose(0, 2, 1, 3)

    q = q.reshape(b, s, KV_GROUPS, HEADS_PER_GROUP, HEAD_DIM).transpose(0, 2, 3, 1, 4) * (HEAD_DIM ** -0.5)
    slopes = alibi_slopes()

    kcmp = compress_blocks(kv_heads(kc), pos_k, k_w1, k_w2)
    vcmp = compress_blocks(kv_heads(vc), pos_v, v_w1, v_w2)
    o_cmp, p_cmp = compressed_branch(q, kcmp, vcmp, slopes)
    idx = selection_indices(p_cmp, s)
    o_sel = selected_branch(q, kv_heads(ks), kv_heads(vs), idx, slopes)
    o_win = window_branch(q, kv_heads(kw), kv_heads(vw), slopes)

    g = jax.nn.sigmoid(gate.reshape(b, s, KV_GROUPS, HEADS_PER_GROUP, N_BRANCH)).transpose(0, 2, 3, 1, 4)
    o = g[..., 0:1] * o_cmp + g[..., 1:2] * o_sel + g[..., 2:3] * o_win
    o = o.transpose(0, 3, 1, 2, 4).reshape(b, s, NSA_WIDTH)
    y_pool = multiscale_pool(u, w_pool, pool_scale)
    return jnp.concatenate([o, y_pool], axis=-1) @ w_out

def conformer_conv(h, w_pw1, b_pw1, w_dw, b_dw, ln_g, ln_b, w_pw2, b_pw2):
    a, gt = jnp.split(h @ w_pw1 + b_pw1, 2, axis=-1)
    z = a * jax.nn.sigmoid(gt)
    z = lax.conv_general_dilated(
        z, w_dw[:, None, :], window_strides=(1,), padding=[(CONV_WIDTH - 1, 0)],
        dimension_numbers=('NWC', 'WIO', 'NWC'), feature_group_count=D_MODEL) + b_dw
    z = jax.nn.silu(layernorm(z, ln_g, ln_b))
    return z @ w_pw2 + b_pw2

def swiglu(h, w_gate, w_up, w_down):
    return (jax.nn.silu(h @ w_gate) * (h @ w_up)) @ w_down

def second_inputs(seed: int = 0) -> dict:
    key = jax.random.key(seed)
    keys = iter(jax.random.split(key, 32))

    def nrm(shape, scale):
        return jax.random.normal(next(keys), shape, jnp.float32) * scale

    def gain(shape):
        return 1.0 + nrm(shape, 0.05)

    dh = HEAD_DIM
    return {
        "x": nrm((BATCH, SEQ, D_MODEL), 1.0),
        "mix_norm": gain((DEPTH, D_MODEL)),
        "ffn_norm": gain((DEPTH, D_MODEL)),
        "nsa_w_in": nrm((N_EVEN, D_MODEL, IN_WIDTH), D_MODEL ** -0.5),
        "cmp_pos_k": nrm((N_EVEN, CMP_BLOCK, dh), 0.1),
        "cmp_pos_v": nrm((N_EVEN, CMP_BLOCK, dh), 0.1),
        "cmp_k_w1": nrm((N_EVEN, CMP_BLOCK * dh, CMP_HIDDEN), (CMP_BLOCK * dh) ** -0.5),
        "cmp_k_w2": nrm((N_EVEN, CMP_HIDDEN, dh), CMP_HIDDEN ** -0.5),
        "cmp_v_w1": nrm((N_EVEN, CMP_BLOCK * dh, CMP_HIDDEN), (CMP_BLOCK * dh) ** -0.5),
        "cmp_v_w2": nrm((N_EVEN, CMP_HIDDEN, dh), CMP_HIDDEN ** -0.5),
        "pool_w": nrm((N_EVEN, POOL_GROUPS, POOL_GROUP_DIM, POOL_GROUP_DIM), POOL_GROUP_DIM ** -0.5),
        "pool_scale": gain((N_EVEN, POOL_WIDTH)),
        "mix_w_out": nrm((N_EVEN, MIX_WIDTH, D_MODEL), MIX_WIDTH ** -0.5),
        "conv_w_pw1": nrm((N_ODD, D_MODEL, 2 * D_MODEL), D_MODEL ** -0.5),
        "conv_b_pw1": nrm((N_ODD, 2 * D_MODEL), 0.02),
        "conv_w_dw": nrm((N_ODD, CONV_WIDTH, D_MODEL), CONV_WIDTH ** -0.5),
        "conv_b_dw": nrm((N_ODD, D_MODEL), 0.02),
        "conv_ln_g": gain((N_ODD, D_MODEL)),
        "conv_ln_b": nrm((N_ODD, D_MODEL), 0.02),
        "conv_w_pw2": nrm((N_ODD, D_MODEL, D_MODEL), D_MODEL ** -0.5),
        "conv_b_pw2": nrm((N_ODD, D_MODEL), 0.02),
        "ffn_w_gate": nrm((DEPTH, D_MODEL, FFN_HIDDEN), D_MODEL ** -0.5),
        "ffn_w_up": nrm((DEPTH, D_MODEL, FFN_HIDDEN), D_MODEL ** -0.5),
        "ffn_w_down": nrm((DEPTH, FFN_HIDDEN, D_MODEL), FFN_HIDDEN ** -0.5),
        "final_norm": gain((D_MODEL,)),
    }

def second_block(x, mix_norm, ffn_norm, nsa_w_in, cmp_pos_k, cmp_pos_v, cmp_k_w1, cmp_k_w2,
              cmp_v_w1, cmp_v_w2, pool_w, pool_scale, mix_w_out, conv_w_pw1, conv_b_pw1,
              conv_w_dw, conv_b_dw, conv_ln_g, conv_ln_b, conv_w_pw2, conv_b_pw2,
              ffn_w_gate, ffn_w_up, ffn_w_down, final_norm):
    for layer in range(DEPTH):
        h = rmsnorm_2(x, mix_norm[layer])
        i = layer // 2
        if layer % 2 == 0:
            x = x + nsa_pool_mixer(h, nsa_w_in[i], cmp_pos_k[i], cmp_pos_v[i], cmp_k_w1[i], cmp_k_w2[i],
                                   cmp_v_w1[i], cmp_v_w2[i], pool_w[i], pool_scale[i], mix_w_out[i])
        else:
            x = x + conformer_conv(h, conv_w_pw1[i], conv_b_pw1[i], conv_w_dw[i], conv_b_dw[i],
                                   conv_ln_g[i], conv_ln_b[i], conv_w_pw2[i], conv_b_pw2[i])
        h = rmsnorm_2(x, ffn_norm[layer])
        x = x + swiglu(h, ffn_w_gate[layer], ffn_w_up[layer], ffn_w_down[layer])
    return rmsnorm_2(x, final_norm)


def setup_inputs(seed=0):
    out = dict(first_inputs(seed))
    for name, value in second_inputs(seed + 1).items():
        if name != "x":
            out[name + "_2"] = value
    return out


def reference(
    x, fox_norm, w_fox_in, b_fox_f, w_fox_out, kv_in_norm, w_dkv, kv_norm, w_uk, w_uv, mla_norm,
    w_dq, q_norm, w_uq, w_mla_out, ffn_norm, w_ffn_in, ffn_conv_w, ffn_conv_b, w_ffn_out,
    final_norm, mix_norm_2, ffn_norm_2, nsa_w_in_2, cmp_pos_k_2, cmp_pos_v_2, cmp_k_w1_2,
    cmp_k_w2_2, cmp_v_w1_2, cmp_v_w2_2, pool_w_2, pool_scale_2, mix_w_out_2, conv_w_pw1_2,
    conv_b_pw1_2, conv_w_dw_2, conv_b_dw_2, conv_ln_g_2, conv_ln_b_2, conv_w_pw2_2,
    conv_b_pw2_2, ffn_w_gate_2, ffn_w_up_2, ffn_w_down_2, final_norm_2,
):
    x = first_block(
        x, fox_norm, w_fox_in, b_fox_f, w_fox_out, kv_in_norm, w_dkv, kv_norm, w_uk, w_uv,
        mla_norm, w_dq, q_norm, w_uq, w_mla_out, ffn_norm, w_ffn_in, ffn_conv_w, ffn_conv_b,
        w_ffn_out, final_norm,
    )
    return second_block(
        x, mix_norm_2, ffn_norm_2, nsa_w_in_2, cmp_pos_k_2, cmp_pos_v_2, cmp_k_w1_2, cmp_k_w2_2,
        cmp_v_w1_2, cmp_v_w2_2, pool_w_2, pool_scale_2, mix_w_out_2, conv_w_pw1_2, conv_b_pw1_2,
        conv_w_dw_2, conv_b_dw_2, conv_ln_g_2, conv_ln_b_2, conv_w_pw2_2, conv_b_pw2_2,
        ffn_w_gate_2, ffn_w_up_2, ffn_w_down_2, final_norm_2,
    )


_drawn_inputs = setup_inputs


def setup_inputs(seed=0):
    import zlib

    import numpy as np

    out = dict(_drawn_inputs(seed))
    spreads = {}
    factors = {'fox_norm': 8.0,
     'kv_in_norm': 8.0,
     'kv_norm': 8.0,
     'mla_norm': 8.0,
     'q_norm': 8.0,
     'ffn_norm': 4.072,
     'ffn_conv_b': 8.0,
     'cmp_pos_k_2': 22.455,
     'conv_b_pw1_2': 5.916,
     'conv_b_dw_2': 3.107,
     'conv_ln_b_2': 6.224,
     'conv_b_pw2_2': 3.853}
    for name, (base, spread) in spreads.items():
        noise = np.random.default_rng([zlib.crc32(name.encode()), seed]).standard_normal(out[name].shape)
        drawn = base * np.exp(spread * noise) if base else spread * noise
        out[name] = __import__('jax').numpy.asarray(drawn.astype(out[name].dtype))
    for name, factor in factors.items():
        out[name] = (out[name] * factor).astype(out[name].dtype)
    return out
```

```python
from contextlib import ExitStack

import numpy as np

import concourse.bass as bass
from concourse import mybir

F = mybir.dt.float32
R = mybir.dt.float32r
ALU = mybir.AluOpType
ACT = mybir.ActivationFunctionType
AX = mybir.AxisListType.X

P = 128
T = 512
TT = T // P
D = 1024
KD = D // P
SLAB = KD * P
RAW = 2
RING = 4
HID = 2816
KH = HID // P
FOX_H, DH = 16, 64
FOX_PAIRS = FOX_H // 2
MLA_H, NOPE, ROPE, LAT, QLAT = 16, 128, 64, 256, 768
KL, KQ = LAT // P, QLAT // P
NSA_H = 8
CMP, STRIDE, SEL = 32, 16, 64
NCMP = T // STRIDE - 1
TAPS = 31
PE_TAPS = 9
EPS = 1e-6
NEG = -1e30

SLABS = [
    ("fox_v", 8), ("fox_qk", 16), ("fox_out", 8), ("ffn0_in", 44), ("ffn0_out", 24),
    ("mla_kvq", 12), ("mla_a", 16), ("mla_out_a", 8), ("mla_b", 16), ("mla_out_b", 8),
    ("ffn1_in", 44), ("ffn1_out", 24),
    ("nsa_misc", 12), ("nsa_attn", 8), ("nsa_out", 8), ("sw0_in", 44), ("sw0_out", 24),
    ("pw1", 16), ("pw2", 8), ("sw1_in", 44), ("sw1_out", 24),
]
SLAB_AT = {}
NSLABS = 0
for _name, _n in SLABS:
    SLAB_AT[_name] = NSLABS
    NSLABS += _n

HID_SPLIT = (8, 7, 7)

COLS = {}
NCOLS = 0
for _name, _n in [
    ("fox_norm", KD), ("kv_in_norm", KD), ("kv_norm", KL), ("mla_norm", KD), ("q_norm", KQ),
    ("ffn_norm0", KD), ("ffn_norm1", KD), ("final_norm", KD), ("b_fox", 1), ("rope_pick", 2),
    ("mix_norm0", KD), ("mix_norm1", KD), ("ffn2_norm0", KD), ("ffn2_norm1", KD), ("final2", KD),
    ("pool_scale", 4), ("b_pw1", 2 * KD), ("b_dw", KD), ("ln_g", KD), ("ln_b", KD), ("b_pw2", KD),
    ("w_dw", TAPS * KD), ("conv0", 4 * 2 * KH), ("conv1", 4 * 2 * KH), ("alibi", TT * NSA_H),
    ("pool_inv", 4 * STRIDE), ("eps", 1), ("eps_ln", 1), ("cmp_pos_k", 16), ("cmp_pos_v", 16),
]:
    COLS[_name] = NCOLS
    NCOLS += _n

SIDE = {"w_f": 0, "w_gate": 128, "w2": 320}
NSIDE = 512
NGATE = 3 * NSA_H
NCMPCOL = 32
NCMPTAB = NSA_H * TT * NCMPCOL
ALIBI_W = T + STRIDE


class Plan:

    def __init__(self):
        self.base, self.steps, self.reps, self.total = {}, {}, {}, 0

    def stage(self, name, steps, reps=1):
        assert name not in self.base and len(set(steps)) == len(steps), name
        self.base[name], self.steps[name], self.reps[name] = self.total, list(steps), reps
        self.total += len(steps) * reps

    def after(self, name, step, turn=0):
        return turn * len(self.steps[name]) + (self.base[name] + self.steps[name].index(step) + 1)

    def before(self, name):
        return self.base[name]

    def end(self, name):
        return self.base[name] + len(self.steps[name]) * self.reps[name]


SLOT = ((2, 3, 4), (5, 6, 7))
MAX_TILES = [(2, 1, 0), (0, 1, 384), (3, 0, 0), (1, 2, 0)]
SCORE_TILES = [(1, 1, 0), (3, 1, 384), (0, 0, 0), (2, 2, 0)]
PROB_AT = [0, 512, 896, 1152]
NPROB = 1280
MAX_STEPS = ["mx1", "mx0", "mx2"]


def attn_pe(h):
    return [f"max{h}b1", f"max{h}b0", f"max{h}b2"]


def score_pe(h):
    return [f"sc{h}b1", f"sc{h}b0", f"sc{h}b2"]


def max_vec(h):
    return [f"mx{h}t{n}" for n, _, _ in MAX_TILES] + [f"dg{h}"]


def exp_act(h):
    return [f"exp{h}t{n}" for n, _, _ in SCORE_TILES]


def make_plans():
    act, vec, pool, pe = Plan(), Plan(), Plan(), Plan()

    def norm_stats(name, cols=False):
        pe.stage(name + ".stat", ["sum"] + (["cols"] if cols else []))
        act.stage(name + ".stat", ["root"] + (["root_cols"] if cols else []))
        vec.stage(name + ".stat", ["rstd"] + (["rstd_cols"] if cols else []))

    def units(name, reps, n, full=True):
        act.stage(name, [f"{s}{c}" for c in range(n) for s in (["hi", "sq"] if full else ["sq"])], reps)
        vec.stage(name, [f"{s}{c}" for c in range(n) for s in (["x", "lo"] if full else ["x"])], reps)
        pool.stage(name, [f"acc{c}" for c in range(n)], reps)

    def out_layer(name, full=True):
        pool.stage(name + ".zero", ["zero"])
        pe.stage(name, [], 2)
        units(name, 2, 4, full)

    def glu_in(name, conv):
        pe.stage(name, [], KH // 2)
        a = ["tapg", "tapv", "silu", "hi"] if conv else ["silu", "hi"]
        v = ["ug", "uv", "c1g", "c1v", "c2g", "c2v", "mul", "lo"] if conv else ["ug", "uv", "mul", "lo"]
        act.stage(name, [f"{s}{c}" for c in range(2) for s in a], KH // 2)
        vec.stage(name, [f"{s}{c}" for c in range(2) for s in v], KH // 2)

    pool.stage("init", ["ones", "ones_r", "zero_negc"])
    act.stage("init", ["ident", "mask0", "mask1", "side"])
    vec.stage("init", ["side"])
    pool.stage("x_in.zero", ["zero"])
    act.stage("x_in", [f"{s}{c}" for c in range(KD) for s in ("hi", "sq")])
    vec.stage("x_in", [f"lo{c}" for c in range(KD)])
    pool.stage("x_in", [f"acc{c}" for c in range(KD)])

    norm_stats("fox", cols=True)
    pe.stage("fox_v", ["f", "negc_cols"])
    act.stage("fox_v", [f"v0t{t}" for t in range(TT)] + ["e", "ln"] + [f"v1t{t}" for t in range(TT)])
    vec.stage("fox_v", ["z0", "z", "na", "logf", "scan", "negc_r", "negc_cols"])
    pool.stage("fox_v", ["vones", "ones_row", "zk0l", "zk1l", "zk0h", "zk1h"])
    v_proj = ["qt", "qlo", "sel0", "sel1", "kt", "klo0", "klo1"]
    a_proj = ["qhi", "khi0", "khi1"]
    v_max = max_vec(0) + max_vec(1)
    v_norm = ["rc0", "on0", "rc1", "on1", "olo"]
    pe_max = attn_pe(0) + attn_pe(1)
    pe_sc = score_pe(0) + score_pe(1)
    pe_body = ["pv0"] + pe_max + ["pv1"] + pe_sc
    pe.stage("fox_first", pe_max + pe_sc)
    act.stage("fox_first", a_proj + exp_act(0) + exp_act(1))
    vec.stage("fox_first", v_proj + v_max)
    pool.stage("fox_first", ["vp0", "vp1"])

    def twice(steps):
        return [f"{s}.{c}" for c in range(2) for s in steps]

    for name, reps, two in (("fox_loop", 3, twice), ("fox_peel", 1, lambda s: [f"{x}.0" for x in s])):
        pe.stage(name, two(pe_body), reps)
        act.stage(name, two(a_proj + exp_act(0) + exp_act(1) + ["ohi"]), reps)
        vec.stage(name, two(v_proj + v_max + v_norm), reps)
        pool.stage(name, two(["vp0", "vp1"]), reps)
    pe.stage("fox_last", ["pv0", "pv1"])
    act.stage("fox_last", ["ohi"])
    vec.stage("fox_last", v_norm)
    out_layer("fox_out")

    norm_stats("ffn0")
    pool.stage("pad0", ["pad0", "pad1"])
    glu_in("ffn0_in", True)
    out_layer("ffn0_out")

    norm_stats("mla")
    pe.stage("mla_kvq", ["t0", "t1", "lat_sum", "t3", "t4", "t6", "t7"] + [f"q_sum{j}" for j in range(KQ)])
    act.stage("mla_kvq", [f"h_hi{n}" for n in range(KD)] + ["sq_l0", "sq_l1", "kr_hi0", "kr_hi1", "root_l", "hi_l0", "hi_l1"]
              + [f"{s}{j}" for j in range(KQ) for s in ("q_hi", "q_sq")] + ["root_q"])
    vec.stage("mla_kvq", [f"h_lo{n}" for n in range(KD)] + ["l0", "l1", "kra", "krb0", "krb1", "krs", "krn", "kr_lo0", "kr_lo1",
              "rstd_l", "ln0", "ln1", "lo_l0", "lo_l1"] + [f"{s}{j}" for j in range(KQ) for s in ("q", "q_lo")]
              + ["rstd_q", "cos_q", "sin_q"])
    m_pe = attn_pe(0) + attn_pe(1)
    m_v = ["n0", "n0lo", "n1", "n1lo", "ra", "rb0", "rb1", "rs", "rlo", "k0lo", "k1lo"]
    m_a = ["n0hi", "n1hi", "rhi", "k0hi", "k1hi"]
    m_sum = [f"s{h}{c}" for h in range(2) for c in "abcd"]
    for half in "ab":
        n = "mla_" + half
        pe.stage(n + "_first", ["k0", "k1"] + m_pe + pe_sc)
        act.stage(n + "_first", m_a + ["v0", "v1"] + exp_act(0) + exp_act(1))
        vec.stage(n + "_first", m_v + max_vec(0) + max_vec(1))
        pool.stage(n + "_first", m_sum)
        pe.stage(n + "_loop", ["k0", "k1", "pv0", "sum0"] + m_pe + ["pv1", "sum1"] + pe_sc, 3)
        act.stage(n + "_loop", m_a + ["ohi0", "ohi1", "v0", "v1"] + exp_act(0) + exp_act(1), 3)
        vec.stage(n + "_loop", m_v + ["rc0", "on0", "olo0"] + max_vec(0) + ["rc1", "on1", "olo1"] + max_vec(1), 3)
        pool.stage(n + "_loop", m_sum, 3)
        pe.stage(n + "_last", ["pv0", "sum0", "pv1", "sum1"])
        act.stage(n + "_last", ["ohi0", "ohi1"])
        vec.stage(n + "_last", ["rc0", "on0", "olo0", "rc1", "on1", "olo1"])
        if half == "a":
            vec.stage("mla_out_a", [f"x{c}" for c in range(4)], 2)
        else:
            out_layer("mla_out_b")

    norm_stats("ffn1")
    pool.stage("pad1", ["pad0", "pad1"])
    glu_in("ffn1_in", True)
    out_layer("ffn1_out", False)

    norm_stats("x2")
    pool.stage("x2.zero", ["zero"])
    act.stage("x2", [f"{s}{c}" for c in range(KD) for s in ("hi", "sq")])
    vec.stage("x2", [f"{s}{c}" for c in range(KD) for s in ("x", "lo")])
    pool.stage("x2", [f"acc{c}" for c in range(KD)])
    norm_stats("nsa", cols=True)

    pool.stage("nsa_misc", ["pad0", "pad1", "pad2", "pad3", "pad4", "pad5", "gates0"])
    pe.stage("nsa_misc", ["gate", "kcmp", "vcmp"])
    act.stage("nsa_misc", ["hik", "hiv"] + [f"d_hi{g}" for g in range(4)]
              + ["sig", "gelu_k", "gelu_v", "kc0", "kc1", "vc0"] + [f"p_hi{g}" for g in range(4)])
    vec.stage("nsa_misc", [f"{z}{g}{h}" for z in ["bk"] for g in range(2) for h in range(2)]
              + [f"blk{g}{h}" for g in range(2) for h in range(2)] + ["lok"]
              + [f"bv{g}{h}" for g in range(2) for h in range(2)]
              + [f"blv{g}{h}" for g in range(2) for h in range(2)] + ["lov"]
              + [f"{z}{g}" for g in range(4) for z in ["u"] + [f"sum{n}_" for n in range(g + 1)] + ["d", "early", "first", "d_lo"]]
              + ["gz", "kcl0", "kcl1"] + [f"p_lo{g}" for g in range(4)])
    vec.stage("nsa_proj", [f"{z}{g}" for g in range(2) for z in ("q0", "q1", "k00", "k01", "k10", "k11")])
    act.stage("nsa_proj", [f"v{g}{t}" for g in range(2) for t in range(TT)])
    pool.stage("nsa_attn.zero", [f"k{n}" for n in range(8)] + ["vones", "vcg"])
    act.stage("nsa_attn.zero", ["table"])
    def unit(steps, u):
        return [f"{z}.{u}" for z in steps]

    pe.stage("nsa_attn", ["g", "cs", "tr", "cpv0", "cpv1"] + unit(pe_max + pe_sc, 0)
             + [z for u in range(1, 4) for z in unit(["pv0"] + pe_max + ["pv1"] + pe_sc, u)] + ["pv0.4", "pv1.4"], 2)
    a = ["ghi", "q0hi", "q1hi", "khi00", "khi01", "khi10", "khi11", "vcg", "bias"] + [f"g{n}" for n in range(6)] + ["cexp"]         + [f"pt{n}" for n in range(4)]
    for u in range(4):
        a += unit(exp_act(0) + exp_act(1), u)
        if u == 2:
            a += ["ohi0"]
    act.stage("nsa_attn", a + ["ohi1"], 2)
    v = [f"gs{n}{h}" for n in range(6) for h in range(2)] + ["glo", "q0lo", "q1lo", "cs", "cm", "cmin", "csub", "csum", "cmax",
         "crec", "cp", "klo00", "klo01", "klo10", "klo11", "acc0", "acc1"]
    for u in range(4):
        v += unit((["sel0", "sel1"] if u % 2 == 0 else []) + max_vec(0) + max_vec(1), u)
        if u:
            v += unit(["rc0", "on0", "rc1", "on1"], u)
        if u == 3:
            v += ["olo0"]
    vec.stage("nsa_attn", v + unit(["rc0", "on0", "rc1", "on1"], 4) + ["olo1"], 2)
    pool.stage("nsa_attn", ["vz0", "vz1"] + [f"{z}.{u}" for u in range(4) for z in ("gm", "ga")], 2)
    out_layer("nsa_out")
    norm_stats("sw0")
    glu_in("sw0_in", False)
    out_layer("sw0_out")

    norm_stats("pw1")
    pool.stage("pw1.zero", ["zero", "zpad0", "zpad1"])
    pe.stage("pw1", ["y0", "y1"], KD // 2)
    act.stage("pw1", [f"{s}{c}" for c in range(2) for s in ["w", "sg"] + [f"diag{k}_" for k in range(PE_TAPS)] + ["t"]], KD // 2)
    vec.stage("pw1", [f"{s}{c}" for c in range(2) for s in ["ua", "ug", "z"]
                      + [f"t{k}_" for k in range(1, TAPS - PE_TAPS)] + ["y"]], KD // 2)
    pool.stage("pw1", ["acc0", "acc1"], KD // 2)
    pe.stage("ln", ["mean"] + [f"v{n}" for n in range(KD)])
    act.stage("ln", ["mean"] + [f"sq{n}" for n in range(KD)] + ["root"] + [f"{s}{n}" for n in range(KD) for s in ("s", "hi")])
    vec.stage("ln", [f"xc{n}" for n in range(KD)] + ["rstd"] + [f"yn{n}" for n in range(KD)] + [f"lo{n}" for n in range(KD)])
    out_layer("pw2")
    norm_stats("sw1")
    glu_in("sw1_in", False)
    out_layer("sw1_out", False)
    norm_stats("final")
    vec.stage("final", [f"y{n}" for n in range(KD)])
    return act, vec, pool, pe


def build(nc, stream, xt_dram, cols_dram, mats_dram, side_dram, rows_dram, tab_dram, out_dram):
    ctx = ExitStack()
    with ctx:
        def sb(name, shape, dt=F, scope=ctx):
            return scope.enter_context(nc.sbuf_tensor(name, shape, dt))

        def sem(name):
            return ctx.enter_context(nc.semaphore(name))

        A, V, G, M = make_plans()

        x = sb("x", [P, KD, T])
        raw = [sb(f"raw{n}", [P, SLAB]) for n in range(RAW)]
        w_hi = [sb(f"w_hi{n}", [P, SLAB], R) for n in range(RING)]
        w_lo = [sb(f"w_lo{n}", [P, SLAB], R) for n in range(RING)]
        rstd = sb("rstd", [P, T])
        root = sb("root", [P, T])
        rstd_col = sb("rstd_col", [P, TT])
        root_col = sb("root_col", [P, TT])
        sq = [sb(f"sq{n}", [P, T]) for n in range(2)]
        sq_sum = sb("sq_sum", [P, T])
        cols = sb("cols", [P, NCOLS])
        mats = sb("mats", [P, 3, P])
        ident = mats[:, 0, :]
        ident_r = sb("ident_r", [P, P], R)
        mask_r = [sb(f"mask_r{n}", [P, P], R) for n in range(2)]
        ones = sb("ones", [P, P])
        ones_r = sb("ones_r", [P, P], R)
        side_raw = root
        side_hi = sb("side_hi", [P, NSIDE], R)
        side_lo = sb("side_lo", [P, NSIDE], R)
        h_scope = ctx.enter_context(ExitStack())
        h_hi = sb("h_hi", [P, KD, T], R, h_scope)
        h_lo = sb("h_lo", [P, KD, T], R, h_scope)

        with ExitStack() as fox:
            o_hi = sb("fox_o_hi", [P, KD, T], R, fox)
            o_lo = sb("fox_o_lo", [P, KD, T], R, fox)
            fx = dict(
                v=sb("fox_v", [P, TT, D], F, fox),
                q_raw=sb("fox_q_raw", [P, T], F, fox), k_raw=sb("fox_k_raw", [P, T], F, fox),
                q_hi=sb("fox_q_hi", [P, T], R, fox), q_lo=sb("fox_q_lo", [P, T], R, fox),
                k_hi=[sb(f"fox_k_hi{h}", [P, T], R, fox) for h in range(2)],
                k_lo=[sb(f"fox_k_lo{h}", [P, T], R, fox) for h in range(2)],
                vp=sb("fox_vp", [P, TT, 2, P], F, fox),
                prob=[sb(f"fox_prob{h}", [P, NPROB], F, fox) for h in range(2)],
                diag=[sb(f"fox_diag{h}", [P, TT, P], R, fox) for h in range(2)],
                sel=[sb(f"fox_sel{h}", [P, P], R, fox) for h in range(2)],
                negm=[sb(f"fox_negm{h}", [P, TT], F, fox) for h in range(2)],
                rec=sb("fox_rec", [P, T], F, fox), o=sb("fox_o", [P, T], F, fox),
                negc=sb("fox_negc", [P, T], F, fox), negc_r=sb("fox_negc_r", [P, T], R, fox),
                negc_col=sb("fox_negc_col", [P, TT, FOX_H], F, fox),
            )
            fx.update(z=fx["rec"], ones_row=fx["o"], na=fx["prob"][0])
            fox_o = (o_hi, o_lo)
        with ExitStack() as ffn:
            act_hi = sb("glu_hi", [P, KH, T], R, ffn)
            act_lo = sb("glu_lo", [P, KH, T], R, ffn)
            u = [sb(f"glu_u{n}", [P, T + 2], F, ffn) for n in range(2)]
            tap = [sb(f"glu_tap{n}", [P, T], F, ffn) for n in range(2)]

        h_scope.close()
        with ExitStack() as mla:
            ml = dict(
                qn_hi=[sb(f"mla_qn_hi{h}", [P, T], R, mla) for h in range(2)],
                qn_lo=[sb(f"mla_qn_lo{h}", [P, T], R, mla) for h in range(2)],
                qr_hi=sb("mla_qr_hi", [P, T], R, mla), qr_lo=sb("mla_qr_lo", [P, T], R, mla),
                v=sb("mla_v", [P, TT, 2, P], F, mla),
                q_raw=sb("mla_q_raw", [P, T], F, mla), rot=sb("mla_rot", [P, T], F, mla),
                rec=sb("mla_rec", [P, T], F, mla), o=sb("mla_o", [P, T], F, mla),
                psum=[sb(f"mla_psum{h}", [P, T], F, mla) for h in range(2)],
                k_hi=[sb(f"mla_k_hi{h}", [P, T], R, mla) for h in range(2)],
            )
            sb("mla_pad", [P, (KD * 2 - 16) * T or 1], F, mla)
            ml["o_hi"] = sb("mla_o_hi", [P, KD, T], R, mla)
            ml["o_lo"] = sb("mla_o_lo", [P, KD, T], R, mla)
            ml.update(
                ql_hi=sb("mla_ql_hi", [P, KQ, T], R, mla), ql_lo=sb("mla_ql_lo", [P, KQ, T], R, mla),
                l_hi=sb("mla_l_hi", [P, KL, T], R, mla), l_lo=sb("mla_l_lo", [P, KL, T], R, mla),
                kr_hi=[sb(f"mla_kr_hi{h}", [P, T], R, mla) for h in range(2)],
                kr_lo=[sb(f"mla_kr_lo{h}", [P, T], R, mla) for h in range(2)],
                k_lo=[sb(f"mla_k_lo{h}", [P, T], R, mla) for h in range(2)],
                cos=sb("mla_cos", [P, T], F, mla), sin=sb("mla_sin", [P, T], F, mla),
                prob=[sb(f"mla_prob{h}", [P, NPROB], F, mla) for h in range(2)],
                diag=[sb(f"mla_diag{h}", [P, TT, P], R, mla) for h in range(2)],
                negm=[sb(f"mla_negm{h}", [P, TT], F, mla) for h in range(2)],
            )

        with ExitStack() as nsa:
            sb("nsa_under", [P, 2 * KD * T], F, nsa)
            ns = dict(
                o_hi=sb("nsa_o_hi", [P, KD, T], R, nsa), o_lo=sb("nsa_o_lo", [P, KD, T], R, nsa),
                q_raw=sb("nsa_q_raw", [P, NSA_H // 2, T], F, nsa),
                k_raw=sb("nsa_k_raw", [P, 2, 2, T], F, nsa),
                v_raw=sb("nsa_v_raw", [P, TT, 2, P], F, nsa),
                kc_hi=sb("nsa_kc_hi", [P, 2, 2, NCMPCOL], R, nsa),
                kc_lo=sb("nsa_kc_lo", [P, 2, 2, NCMPCOL], R, nsa),
                vc=sb("nsa_vc", [NCMPCOL, 2, DH], F, nsa),
                w2=sb("nsa_w2", [P, P + DH], F, nsa),
                tab=sb("nsa_tab", [P, 2, 2 * 2 * TT * NCMPCOL], F, nsa),
                table=sb("nsa_table", [P, T], R, nsa),
                gates=sq_sum, cmp=root, rec=sq[0], o=sq[1],
            )
            misc = nsa.enter_context(ExitStack())
            ns.update(
                bk=sb("nsa_bk", [P, 2, T + STRIDE], F, misc), blk=sb("nsa_blk", [P, 16, 2, NCMPCOL], F, misc),
                b_hi=[sb(f"nsa_b_hi{n}", [P, 16, 2, NCMPCOL], R, misc) for n in range(2)],
                b_lo=[sb(f"nsa_b_lo{n}", [P, 16, 2, NCMPCOL], R, misc) for n in range(2)],
                run=[sb(f"nsa_run{n}", [P, STRIDE + T], F, misc) for n in range(3)],
                gh=[sb(f"nsa_gh{n}", [P, 2, NCMPCOL], F, misc) for n in range(2)],
            )
            misc.close()
            ns.update(
                prob=[sb(f"nsa_prob{h}", [P, NPROB], F, nsa) for h in range(2)],
                sel=[sb(f"nsa_sel{h}", [P, P], R, nsa) for h in range(2)],
                negm=[sb(f"nsa_negm{h}", [P, TT], F, nsa) for h in range(2)],
                bias=sb("nsa_bias", [P, TT * NSA_H // 2], F, nsa),
                cmp_m=sb("nsa_cmp_m", [P, 16], F, nsa),
                q_lo=[sb(f"nsa_q_lo{j}", [P, T], R, nsa) for j in range(2)],
                gsel=sb("nsa_gsel", [P, 6 * P], R, nsa),
                g=sb("nsa_g", [P, 6, T], F, nsa), vcg=sb("nsa_vcg", [NCMPCOL, 2, P], F, nsa),
            )
        with ExitStack() as nsa2:
            ns.update(
                k_hi=[[sb(f"nsa_k_hi{b}{h}", [P, T], R, nsa2) for h in range(2)] for b in range(2)],
                k_lo=[[sb(f"nsa_k_lo{b}{h}", [P, T], R, nsa2) for h in range(2)] for b in range(2)],
                v=sb("nsa_v", [P, TT, 2, 2, P], F, nsa2),
                diag=[sb(f"nsa_diag{h}", [P, TT, P], R, nsa2) for h in range(2)],
                q_hi=[sb(f"nsa_q_hi{j}", [P, T], R, nsa2) for j in range(2)],
            )

        with ExitStack() as conf:
            sb("conf_under", [P, 2 * KD * T], F, conf)
            cf = dict(
                o_hi=sb("conf_o_hi", [P, KD, T], R, conf), o_lo=sb("conf_o_lo", [P, KD, T], R, conf),
                y=sb("conf_y", [P, KD, T], F, conf),
                a=sb("conf_a", [P, T], F, conf), gate=sb("conf_gate", [P, T], F, conf),
                z=[sb(f"conf_z{c}", [P, TAPS - 1 + T], F, conf) for c in range(2)],
                acc=[sb(f"conf_acc{c}", [P, T], F, conf) for c in range(2)],
                w=[sb(f"conf_w{c}", [P, TAPS], F, conf) for c in range(2)],
                diag=[sb(f"conf_diag{c}", [P, PE_TAPS, P], F, conf) for c in range(2)],
            )

        bank = [ctx.enter_context(nc.psum_tensor(f"bank{n}", [P, T], F)) for n in range(8)]

        const_loaded = sem("const_loaded")
        x_loaded = sem("x_loaded")
        raw_loaded = [sem(f"raw_loaded{n}") for n in range(RAW)]
        hi_ready = sem("hi_ready")
        lo_ready = sem("lo_ready")
        slab_used = sem("slab_used")
        act_done = sem("act_done")
        vec_done = sem("vec_done")
        pool_done = sem("pool_done")
        pe_done = sem("pe_done")
        out_stored = sem("out_stored")
        tables_loaded = sem("tables_loaded")

        def kvq_slabs(t):
            return KD * (t + 1) // 6

        def kvq_done(t):
            if KD * (t + 1) % 6 == 0:
                return slab_used, SLAB_AT["mla_kvq"] + kvq_slabs(t)
            return pe_done, M.after("mla_kvq", f"t{t}")

        KVQ_BANK = (0, 1, 2, 3, 4, 5, 6, 0, 1)

        def col(name, n=0, count=1):
            return cols[:, bass.ds(COLS[name] + n, count)]

        block = ctx.enter_context(nc.Block())

        @block.sync
        def _(sp):
            for n in range(RAW):
                sp.dma_start(raw[n][:, :], stream[n, :, :]).then_inc(raw_loaded[n], 16)
                if n == 0:
                    sp.dma_start(x[:, :, :], xt_dram).then_inc(x_loaded, 16)
                    sp.dma_start(cols[:, :], cols_dram).then_inc(const_loaded, 16)
                    sp.dma_start(mats[:, :, :], mats_dram).then_inc(const_loaded, 16)
                    sp.dma_start(side_raw[:, :], side_dram).then_inc(const_loaded, 16)
            last = NSLABS
            with sp.Fori(1, last // RAW) as i:
                for n in range(RAW):
                    sp.wait_ge(lo_ready, RAW * i + (n - RAW + 1))
                    sp.dma_start(raw[n][:, :], stream[bass.ds(RAW * i + n, 1), :, :].rearrange("a p n -> (a p) n"))\
                        .then_inc(raw_loaded[n], 16)
            for n in range(0, KD, 2):
                sp.wait_ge(vec_done, V.after("final", f"y{n + 1}"))
                sp.dma_start(out_dram[:, n:n + 2, :], x[:, n:n + 2, :]).then_inc(out_stored, 16)
            sp.wait_ge(out_stored, 16 * KD // 2)

        @block.gpsimd
        def _(pool):
            order = [0]

            def own(plan_stage, step, turn=0):
                n = G.after(plan_stage, step, turn) - 1
                if isinstance(n, int) and n == 0:
                    return
                pool.wait_ge(pool_done, n)

            def zero_sum(name, read):
                own(name + ".zero", "zero")
                if read:
                    pool.wait_ge(pe_done, M.end(read + ".stat"))
                nc.gpsimd.memset(sq_sum[:, :], 0.0).then_inc(pool_done, 1)

            def sum_squares(name, n, turn=0):
                for c in range(n):
                    own(name, f"acc{c}", turn)
                    pool.wait_ge(act_done, A.after(name, f"sq{c}", turn))
                    nc.gpsimd.tensor_tensor(sq_sum[:, :], sq_sum[:, :], sq[c % 2][:, :], ALU.add)\
                        .then_inc(pool_done, 1)

            def out_layer(name, read):
                zero_sum(name, read)
                with pool.Fori(0, 2) as i:
                    sum_squares(name, 4, i)

            own("init", "ones")
            nc.gpsimd.memset(ones[:, :], 1.0).then_inc(pool_done, 1)
            own("init", "ones_r")
            nc.gpsimd.memset(ones_r[:, :].bitcast(F), 1.0).then_inc(pool_done, 1)
            own("init", "zero_negc")
            nc.gpsimd.memset(fx["negc_r"][:, :].bitcast(F), 0.0).then_inc(pool_done, 1)
            zero_sum("x_in", None)
            sum_squares("x_in", KD)

            own("fox_v", "vones")
            nc.gpsimd.memset(fx["vp"][:, :, :, :], 1.0).then_inc(pool_done, 1)
            own("fox_v", "ones_row")
            nc.gpsimd.memset(fx["ones_row"][:, :], 1.0).then_inc(pool_done, 1)
            for name, buf, lo in (("zk0l", fx["k_lo"][0], 64), ("zk1l", fx["k_lo"][1], 0),
                                  ("zk0h", fx["k_hi"][0], 64), ("zk1h", fx["k_hi"][1], 0)):
                own("fox_v", name)
                nc.gpsimd.memset(buf[lo:lo + 64, :].bitcast(F), 0.0).then_inc(pool_done, 1)

            def fox_values(name, sfx, turn, pair):
                for h in range(2):
                    own(name, f"vp{h}{sfx}", turn)
                    src = fx["v"][:, :, bass.ds(pair * P + h * DH, DH)]
                    nc.gpsimd.tensor_copy(fx["vp"][:, :, h, h * DH:(h + 1) * DH], src).then_inc(pool_done, 1)

            pool.wait_ge(act_done, A.after("fox_v", f"v1t{TT - 1}"))
            fox_values("fox_first", "", 0, 0)
            with pool.Fori(0, 3) as i:
                for c in range(2):
                    pool.wait_ge(pe_done, M.after("fox_loop", f"pv1.{c}", i))
                    fox_values("fox_loop", f".{c}", i, 2 * i + (c + 1))
            pool.wait_ge(pe_done, M.after("fox_peel", "pv1.0"))
            fox_values("fox_peel", ".0", 0, FOX_PAIRS - 1)
            out_layer("fox_out", "fox")
            for n in range(2):
                own("pad0", f"pad{n}")
                nc.gpsimd.memset(u[n][:, 0:2], 0.0).then_inc(pool_done, 1)
            out_layer("ffn0_out", "ffn0")

            def prob_sums(name, turn):
                for h in range(2):
                    p, total = ml["prob"][h], ml["psum"][h]
                    own(name, f"s{h}a", turn)
                    pool.wait_ge(act_done, A.after(name, f"exp{h}t2", turn))
                    nc.gpsimd.tensor_tensor(total[:, 0:P], p[:, 0:P], ones[:, :], ALU.mult).then_inc(pool_done, 1)
                    own(name, f"s{h}b", turn)
                    nc.gpsimd.tensor_tensor(total[:, P:T], p[:, P:T], p[:, PROB_AT[1]:PROB_AT[1] + T - P], ALU.add)\
                        .then_inc(pool_done, 1)
                    for n, c in ((2, "c"), (3, "d")):
                        own(name, f"s{h}{c}", turn)
                        nc.gpsimd.tensor_tensor(total[:, n * P:T], total[:, n * P:T],
                                                p[:, PROB_AT[n]:PROB_AT[n] + T - n * P], ALU.add).then_inc(pool_done, 1)

            for half in "ab":
                prob_sums(f"mla_{half}_first", 0)
                with pool.Fori(0, 3) as i:
                    prob_sums(f"mla_{half}_loop", i)
            out_layer("mla_out_b", "mla")
            for n in range(2):
                own("pad1", f"pad{n}")
                pool.wait_ge(slab_used, SLAB_AT["ffn1_in"])
                nc.gpsimd.memset(u[n][:, 0:2], 0.0).then_inc(pool_done, 1)
            out_layer("ffn1_out", "ffn1")
            zero_sum("x2", "x2")
            sum_squares("x2", KD)
            s = SLAB_AT["nsa_misc"]
            for n, dst in enumerate([ns["bk"][:, :, T:T + STRIDE]] + [r[:, 0:STRIDE] for r in ns["run"]]
                                     + [ns[z][:, :, :, :].bitcast(F) for z in ("kc_hi", "kc_lo")]):
                own("nsa_misc", f"pad{n}")
                pool.wait_ge(slab_used, s)
                nc.gpsimd.memset(dst, 0.0).then_inc(pool_done, 1)
            own("nsa_misc", "gates0")
            pool.wait_ge(pe_done, M.end("nsa.stat"))
            nc.gpsimd.memset(ns["gates"][:, :], 0.0).then_inc(pool_done, 1)
            for n in range(8):
                b, h, kind = n // 4, n // 2 % 2, ("k_hi", "k_lo")[n % 2]
                own("nsa_attn.zero", f"k{n}")
                pool.wait_ge(slab_used, SLAB_AT["nsa_out"])
                nc.gpsimd.memset(ns[kind][b][h][(1 - h) * DH:(2 - h) * DH, :].bitcast(F), 0.0).then_inc(pool_done, 1)
            own("nsa_attn.zero", "vones")
            nc.gpsimd.memset(ns["v"][:, :, :, :, :], 1.0).then_inc(pool_done, 1)
            own("nsa_attn.zero", "vcg")
            nc.gpsimd.memset(ns["vcg"][:, :, :], 0.0).then_inc(pool_done, 1)
            with pool.Fori(0, 2) as i:
                pool.wait_ge(pe_done, M.after("nsa_attn", "g", i) - 1)
                for b in range(2):
                    own("nsa_attn", f"vz{b}", i)
                    pool.wait_ge(act_done, A.end("nsa_proj"))
                    nc.gpsimd.tensor_copy(
                        ns["v"][:, :, b, :, :].rearrange("p t h (a d) -> p t (h a) d", a=2)[:, :, 0:4:3, :],
                        ns["v_raw"][:, :, bass.ds(i, 1), b * DH:(b + 1) * DH].broadcast_to([P, TT, 2, DH]))\
                        .then_inc(pool_done, 1)
                for n in range(4):
                    j, b = n // 2, n % 2
                    g = ns["g"][:, 3 * j + 1 + b, :]
                    own("nsa_attn", f"gm.{n}", i)
                    pool.wait_ge(vec_done, V.after("nsa_attn", f"on1.{n + 1}", i))
                    nc.gpsimd.tensor_tensor(g, g, ns["o"][:, :], ALU.mult).then_inc(pool_done, 1)
                    own("nsa_attn", f"ga.{n}", i)
                    nc.gpsimd.tensor_tensor(ns["g"][:, 3 * j, :], ns["g"][:, 3 * j, :], g, ALU.add).then_inc(pool_done, 1)
            out_layer("nsa_out", None)
            out_layer("sw0_out", "sw0")
            zero_sum("pw1", "pw1")
            for c in range(2):
                own("pw1.zero", f"zpad{c}")
                pool.wait_ge(slab_used, SLAB_AT["pw1"])
                nc.gpsimd.memset(cf["z"][c][:, 0:TAPS - 1], 0.0).then_inc(pool_done, 1)
            with pool.Fori(0, KD // 2) as i:
                for c in range(2):
                    own("pw1", f"acc{c}", i)
                    pool.wait_ge(vec_done, V.after("pw1", f"y{c}", i))
                    nc.gpsimd.tensor_tensor(sq_sum[:, :], sq_sum[:, :], cf["y"][:, bass.ds(2 * i + c, 1), :], ALU.add)\
                        .then_inc(pool_done, 1)
            own("pw2.zero", "zero")
            pool.wait_ge(pe_done, M.after("ln", "mean"))
            nc.gpsimd.memset(sq_sum[:, :], 0.0).then_inc(pool_done, 1)
            with pool.Fori(0, 2) as i:
                sum_squares("pw2", 4, i)
            out_layer("sw1_out", "sw1")

        @block.scalar
        def _(act):
            def own(plan_stage, step, turn=0):
                n = A.after(plan_stage, step, turn) - 1
                if isinstance(n, int) and n == 0:
                    return
                act.wait_ge(act_done, n)

            def split_hi(s0, turn=0, per=0):
                if isinstance(turn, int) and s0 + per * turn >= NSLABS:
                    return
                act.wait_ge(raw_loaded[s0 % RAW], 16 * (s0 // RAW + 1) + turn * (16 * per // RAW))
                if s0 >= RING:
                    act.wait_ge(slab_used, s0 - RING + 1 + turn * per)
                nc.scalar.activation(w_hi[s0 % RING][:, :], raw[s0 % RAW][:, :], ACT.Copy).then_inc(hi_ready, 1)

            def norm_unit(name, c, n, gain, turn=0, full=True, need=None):
                own(name, f"hi{c}" if full else f"sq{c}", turn)
                if need:
                    act.wait_ge(*need)
                if name != "x_in" or c >= 2:
                    act.wait_ge(pool_done, G.after(name, f"acc{c}", turn) - 2)
                if full:
                    nc.scalar.activation(h_hi[:, bass.ds(n, 1), :], x[:, bass.ds(n, 1), :], ACT.Copy,
                                         scale=col(gain, n)).then_inc(act_done, 1)
                nc.scalar.activation(sq[c % 2][:, :], x[:, bass.ds(n, 1), :], ACT.Square).then_inc(act_done, 1)

            def stats(name, width, cols_too=False):
                own(name + ".stat", "root")
                act.wait_ge(pe_done, M.after(name + ".stat", "sum"))
                nc.scalar.activation(root[:, :], bank[7][:, :], ACT.Sqrt, bias=col("eps"),
                                     scale=1.0 / width).then_inc(act_done, 1)
                if cols_too:
                    own(name + ".stat", "root_cols")
                    act.wait_ge(pe_done, M.after(name + ".stat", "cols"))
                    nc.scalar.activation(root_col[:, :], bank[6][:, 0:TT], ACT.Sqrt, bias=col("eps"),
                                         scale=1.0 / width).then_inc(act_done, 1)

            def out_layer(name, gain, full=True):
                def half(i):
                    s = SLAB_AT[name]
                    for c in range(4):
                        for _k in OUT[name]:
                            split_hi(s + RING, i, 4 * len(OUT[name]))
                            s += 1
                        norm_unit(name, c, 4 * i + c, gain, i, full, (vec_done, V.after(name, f"x{c}", i)))

                if name == "sw1_out":
                    half(0)
                    half(1)
                else:
                    with act.Fori(0, 2) as i:
                        half(i)

            for s in range(RING):
                split_hi(s)
            act.wait_ge(const_loaded, 48)
            for step, dst, src in (("ident", ident_r[:, :], ident), ("mask0", mask_r[0][:, :], mats[:, 1, :]),
                                   ("mask1", mask_r[1][:, :], mats[:, 2, :]),
                                   ("side", side_hi[:, :], side_raw[:, :])):
                own("init", step)
                nc.scalar.activation(dst, src, ACT.Copy).then_inc(act_done, 1)
            act.wait_ge(x_loaded, 16)
            for n in range(KD):
                norm_unit("x_in", n, n, "fox_norm")
            act.wait_ge(vec_done, V.after("init", "side"))
            stats("fox", D, True)

            act.wait_ge(vec_done, V.after("fox.stat", "rstd_cols"))
            s = SLAB_AT["fox_v"]

            def fox_v_half(half):
                for c in range(4):
                    split_hi(s + 4 * half + c + RING)
                for t in range(TT):
                    own("fox_v", f"v{half}t{t}")
                    act.wait_ge(slab_used, s + 4 * half + 4)
                    nc.scalar.activation(fx["v"][:, t, half * T:(half + 1) * T], bank[t][:, :], ACT.Copy,
                                         scale=rstd_col[:, t:t + 1]).then_inc(act_done, 1)

            fox_v_half(0)
            own("fox_v", "e")
            act.wait_ge(vec_done, V.after("fox_v", "na"))
            nc.scalar.activation(fx["q_raw"][0:FOX_H, :], fx["na"][0:FOX_H, 0:T], ACT.Exp).then_inc(act_done, 1)
            own("fox_v", "ln")
            nc.scalar.activation(fx["k_raw"][0:FOX_H, :], fx["q_raw"][0:FOX_H, :], ACT.Ln, bias=1.0)\
                .then_inc(act_done, 1)
            fox_v_half(1)

            def fox_proj(name, sfx, turn, s0, per):
                split_hi(s0 + RING, turn, per)
                own(name, "qhi" + sfx, turn)
                act.wait_ge(vec_done, V.after(name, "qt" + sfx, turn))
                nc.scalar.activation(fx["q_hi"][:, :], fx["q_raw"][:, :], ACT.Copy).then_inc(act_done, 1)
                split_hi(s0 + 1 + RING, turn, per)
                for h in range(2):
                    own(name, f"khi{h}{sfx}", turn)
                    act.wait_ge(vec_done, V.after(name, "kt" + sfx, turn))
                    nc.scalar.activation(fx["k_hi"][h][h * DH:(h + 1) * DH, :], fx["k_raw"][h * DH:(h + 1) * DH, :],
                                         ACT.Copy).then_inc(act_done, 1)

            def fox_exps(name, sfx, turn, pair):
                for h in range(2):
                    for n, b, at in SCORE_TILES:
                        own(name, f"exp{h}t{n}{sfx}", turn)
                        act.wait_ge(pe_done, M.after(name, f"sc{h}b{b}{sfx}", turn))
                        w = (TT - n) * P
                        nc.scalar.activation(fx["prob"][h][:, PROB_AT[n]:PROB_AT[n] + w],
                                             bank[SLOT[h][b]][:, at:at + w], ACT.Exp,
                                             bias=fx["negc_col"][:, n, bass.ds(2 * pair + h, 1)]).then_inc(act_done, 1)

            def fox_out_hi(name, sfx, turn, pair):
                own(name, "ohi" + sfx, turn)
                act.wait_ge(vec_done, V.after(name, "on1" + sfx, turn))
                nc.scalar.activation(fox_o[0][:, bass.ds(pair, 1), :], fx["o"][:, :], ACT.Copy).then_inc(act_done, 1)

            s = SLAB_AT["fox_qk"]
            fox_proj("fox_first", "", 0, s, 0)
            act.wait_ge(vec_done, V.after("fox_v", "negc_cols"))
            fox_exps("fox_first", "", 0, 0)
            with act.Fori(0, 3) as i:
                for c in range(2):
                    fox_proj("fox_loop", f".{c}", i, s + 2 + 2 * c, 4)
                    fox_exps("fox_loop", f".{c}", i, 2 * i + (c + 1))
                    fox_out_hi("fox_loop", f".{c}", i, 2 * i + c)
            fox_proj("fox_peel", ".0", 0, s + 14, 0)
            fox_exps("fox_peel", ".0", 0, FOX_PAIRS - 1)
            fox_out_hi("fox_peel", ".0", 0, FOX_PAIRS - 2)
            fox_out_hi("fox_last", "", 0, FOX_PAIRS - 1)
            out_layer("fox_out", "ffn_norm0")

            def glu_in(name, conv):
                with act.Fori(0, KH // 2) as i:
                    for c in range(2):
                        s = SLAB_AT[name] + 2 * c
                        split_hi(s + RING, i, 4)
                        if conv:
                            for n, step, need in ((0, "tapg", "ug"), (1, "tapv", "uv")):
                                own(name, f"{step}{c}", i)
                                act.wait_ge(vec_done, V.after(name, f"{need}{c}", i))
                                at = (2 * i + (c + KH * n)) * 4
                                nc.scalar.activation(tap[n][:, :], u[n][:, 2:T + 2], ACT.Identity,
                                                     bias=col(conv, at + 3), scale=col(conv, at + 2))\
                                    .then_inc(act_done, 1)
                        split_hi(s + 1 + RING, i, 4)
                        own(name, f"silu{c}", i)
                        act.wait_ge(vec_done, V.after(name, ("c2g" if conv else "ug") + str(c), i))
                        nc.scalar.activation(tap[0][:, :], tap[0][:, :], ACT.Silu).then_inc(act_done, 1)
                        own(name, f"hi{c}", i)
                        act.wait_ge(vec_done, V.after(name, f"mul{c}", i))
                        nc.scalar.activation(act_hi[:, bass.ds(2 * i + c, 1), :], tap[0][:, :], ACT.Copy)\
                            .then_inc(act_done, 1)

            stats("ffn0", D)
            glu_in("ffn0_in", "conv0")
            out_layer("ffn0_out", "kv_in_norm")

            act.wait_ge(slab_used, SLAB_AT["mla_kvq"])
            act.dma_start(ml["cos"][:, :], rows_dram[:, 0, 0:T]).then_inc(tables_loaded, 16)
            act.dma_start(ml["sin"][:, :], rows_dram[:, 1, 0:T]).then_inc(tables_loaded, 16)
            stats("mla", D)
            for n in range(KD):
                own("mla_kvq", f"h_hi{n}")
                nc.scalar.activation(ml["o_hi"][:, n, :], x[:, n, :], ACT.Copy, scale=col("mla_norm", n))\
                    .then_inc(act_done, 1)
            tl = [ml["prob"][0][:, j * T:(j + 1) * T] for j in range(2)]

            def kvq_splits(split, t):
                for j in range(kvq_slabs(t - 1), kvq_slabs(t)):
                    split(SLAB_AT["mla_kvq"] + j + RING)

            for t in range(2):
                kvq_splits(split_hi, t)
                own("mla_kvq", f"sq_l{t}")
                act.wait_ge(vec_done, V.after("mla_kvq", f"l{t}"))
                nc.scalar.activation(sq[t][:, :], tl[t], ACT.Square).then_inc(act_done, 1)
            kvq_splits(split_hi, 2)
            for h in range(2):
                own("mla_kvq", f"kr_hi{h}")
                act.wait_ge(vec_done, V.after("mla_kvq", "krn"))
                nc.scalar.activation(ml["kr_hi"][h][:, :], ml["prob"][1][:, 0:T], ACT.Copy, scale=col("rope_pick", h))\
                    .then_inc(act_done, 1)
            own("mla_kvq", "root_l")
            act.wait_ge(pe_done, M.after("mla_kvq", "lat_sum"))
            nc.scalar.activation(root[:, :], bank[7][:, :], ACT.Sqrt, bias=col("eps"), scale=1.0 / LAT)\
                .then_inc(act_done, 1)
            for j in range(KL):
                own("mla_kvq", f"hi_l{j}")
                act.wait_ge(vec_done, V.after("mla_kvq", f"ln{j}"))
                nc.scalar.activation(ml["l_hi"][:, j, :], tl[j], ACT.Copy).then_inc(act_done, 1)
            for j in range(KQ):
                kvq_splits(split_hi, 3 + j)
                own("mla_kvq", f"q_hi{j}")
                act.wait_ge(vec_done, V.after("mla_kvq", f"q{j}"))
                nc.scalar.activation(ml["ql_hi"][:, j, :], tl[j % 2], ACT.Copy, scale=col("q_norm", j))\
                    .then_inc(act_done, 1)
                own("mla_kvq", f"q_sq{j}")
                if j >= 2:
                    act.wait_ge(pe_done, M.after("mla_kvq", f"q_sum{j - 2}"))
                nc.scalar.activation(sq[j % 2][:, :], tl[j % 2], ACT.Square).then_inc(act_done, 1)
            own("mla_kvq", "root_q")
            act.wait_ge(pe_done, M.after("mla_kvq", f"q_sum{KQ - 1}"))
            nc.scalar.activation(root[:, :], bank[7][:, :], ACT.Sqrt, bias=col("eps"), scale=1.0 / QLAT)\
                .then_inc(act_done, 1)

            def mla_step(name, turn, s0, per, n_out):
                for step, need, dst, src in (("n0hi", "n0", ml["qn_hi"][0], ml["q_raw"]),
                                             ("n1hi", "n1", ml["qn_hi"][1], ml["rot"]),
                                             ("rhi", "rs", ml["qr_hi"], ml["q_raw"])):
                    own(name, step, turn)
                    act.wait_ge(vec_done, V.after(name, need, turn))
                    nc.scalar.activation(dst[:, :], src[:, :], ACT.Copy).then_inc(act_done, 1)
                    split_hi(s0 + ("n0hi", "n1hi", "rhi").index(step) + RING, turn, per)
                for h in range(2):
                    own(name, f"k{h}hi", turn)
                    act.wait_ge(pe_done, M.after(name, f"k{h}", turn))
                    nc.scalar.activation(ml["k_hi"][h][:, :], bank[1 - h][:, :], ACT.Copy).then_inc(act_done, 1)
                if n_out is not None:
                    mla_out_hi(name, turn, n_out)
                for j in range(2):
                    own(name, f"v{j}", turn)
                    act.wait_ge(slab_used, s0 + 4 + turn * per)
                    nc.scalar.activation(ml["v"][:, 2 * j:2 * j + 2, :, :].rearrange("p t h d -> p (t h d)"),
                                         bank[j][:, :], ACT.Copy).then_inc(act_done, 1)
                split_hi(s0 + 3 + RING, turn, per)
                for h in range(2):
                    for n, b, at in SCORE_TILES:
                        own(name, f"exp{h}t{n}", turn)
                        act.wait_ge(pe_done, M.after(name, f"sc{h}b{b}", turn))
                        w = (TT - n) * P
                        nc.scalar.activation(ml["prob"][h][:, PROB_AT[n]:PROB_AT[n] + w],
                                             bank[SLOT[h][b]][:, at:at + w], ACT.Exp).then_inc(act_done, 1)

            def mla_out_hi(name, turn, n):
                for h in range(2):
                    own(name, f"ohi{h}", turn)
                    act.wait_ge(vec_done, V.after(name, f"on{h}", turn))
                    nc.scalar.activation(ml["o_hi"][:, bass.ds(n + h, 1), :], ml["o"][:, :], ACT.Copy)\
                        .then_inc(act_done, 1)

            for half in "ab":
                s = SLAB_AT["mla_" + half]
                mla_step(f"mla_{half}_first", 0, s, 0, None)
                with act.Fori(0, 3) as i:
                    mla_step(f"mla_{half}_loop", i, s + 4, 4, 2 * i)
                mla_out_hi(f"mla_{half}_last", 0, 6)
                if half == "a":
                    for n in range(KD):
                        split_hi(SLAB_AT["mla_out_a"] + n + RING)
            out_layer("mla_out_b", "ffn_norm1")
            stats("ffn1", D)
            glu_in("ffn1_in", "conv1")
            out_layer("ffn1_out", None, False)

            act.wait_ge(slab_used, SLAB_AT["nsa_misc"])
            act.dma_start(ns["w2"][:, :], side_dram[:, SIDE["w2"]:SIDE["w2"] + P + DH]).then_inc(tables_loaded, 16)
            act.dma_start(ns["tab"][:, :, :].rearrange("p g n -> p (g n)"), tab_dram).then_inc(tables_loaded, 16)
            stats("x2", D)
            for n in range(KD):
                norm_unit("x2", n, n, "mix_norm0", 0, True, (vec_done, V.after("x2", f"x{n}")))
            stats("nsa", D, True)
            s = SLAB_AT["nsa_misc"]
            for n, kv in enumerate("kv"):
                split_hi(s + n + RING)
                own("nsa_misc", "hi" + kv)
                act.wait_ge(vec_done, V.after("nsa_misc", f"bl{kv}11"))
                nc.scalar.activation(ns["b_hi"][n][:, :, :, :], ns["blk"][:, :, :, :], ACT.Copy).then_inc(act_done, 1)
            for g in range(4):
                split_hi(s + 2 + g + RING)
                own("nsa_misc", f"d_hi{g}")
                act.wait_ge(vec_done, V.after("nsa_misc", f"first{g}"))
                nc.scalar.activation(ns["o_hi"][:, 4 + g, :], ns["run"][1 + (g + 1) % 2][:, STRIDE:], ACT.Copy)\
                    .then_inc(act_done, 1)
            own("nsa_misc", "sig")
            act.wait_ge(vec_done, V.after("nsa_misc", "gz"))
            nc.scalar.activation(ns["gates"][0:NGATE, :], ns["gates"][0:NGATE, :], ACT.Sigmoid).then_inc(act_done, 1)
            for n, kv in enumerate("kv"):
                split_hi(s + 6 + 2 * n + RING)
                split_hi(s + 7 + 2 * n + RING)
                own("nsa_misc", "gelu_" + kv)
                nc.scalar.activation(ns["gh"][n][:, :, :].rearrange("p g n -> p (g n)"), bank[7 - 7 * n][:, 0:64],
                                     ACT.Gelu_apprx_tanh).then_inc(act_done, 1)
            for h in range(2):
                own("nsa_misc", f"kc{h}")
                act.wait_ge(pe_done, M.after("nsa_misc", "kcmp"))
                act.wait_ge(pool_done, G.after("nsa_misc", "pad5"))
                hs = slice(h * DH, (h + 1) * DH)
                nc.scalar.activation(ns["kc_hi"][hs, :, h, :], bank[1][hs, 0:64].rearrange("p (g n) -> p g n", g=2),
                                     ACT.Copy).then_inc(act_done, 1)
            own("nsa_misc", "vc0")
            act.wait_ge(pe_done, M.after("nsa_misc", "vcmp"))
            nc.scalar.activation(ns["vc"][:, :, :].rearrange("p g d -> p (g d)"), bank[6][0:NCMPCOL, 0:P], ACT.Copy)\
                .then_inc(act_done, 1)
            split_hi(s + 10 + RING)
            split_hi(s + 11 + RING)
            for g in range(4):
                own("nsa_misc", f"p_hi{g}")
                act.wait_ge(slab_used, s + 11 + g // 2)
                nc.scalar.activation(ns["o_hi"][:, 4 + g, :], bank[2 + g][:, :], ACT.Copy, scale=col("pool_scale", g))\
                    .then_inc(act_done, 1)
            s = SLAB_AT["nsa_attn"]
            for g in range(2):
                for c in range(4):
                    split_hi(s + 4 * g + c + RING)
                for t in range(TT):
                    own("nsa_proj", f"v{g}{t}")
                    act.wait_ge(slab_used, s + 4 * g + 4)
                    nc.scalar.activation(ns["v_raw"][:, t, g, :], bank[4 * g + 3][:, t * P:(t + 1) * P], ACT.Copy,
                                         scale=rstd_col[:, t:t + 1]).then_inc(act_done, 1)
            act.dma_start(ns["o"][:, :], rows_dram[:, 2, :]).then_inc(tables_loaded, 16)
            own("nsa_attn.zero", "table")
            act.wait_ge(tables_loaded, 80)
            nc.scalar.activation(ns["table"][:, :], ns["o"][:, :], ACT.Copy).then_inc(act_done, 1)

            def nsa_group(i):
                name = "nsa_attn"

                def step(what, dst, src, *waits, **kw):
                    own(name, what, i)
                    for w in waits:
                        act.wait_ge(*w)
                    nc.scalar.activation(dst, src, ACT.Copy, **kw).then_inc(act_done, 1)

                act.wait_ge(vec_done, V.after(name, "gs00", i) - 1)
                act.wait_ge(pool_done, G.end("nsa_attn.zero"))
                step("ghi", ns["diag"][0][:, :, :].rearrange("p t n -> p (t n)"), ns["gates"][:, :])
                for j in range(2):
                    step(f"q{j}hi", ns["q_hi"][j][:, :], ns["q_raw"][:, bass.ds(2 * i + j, 1), :])
                for b in range(2):
                    for h in range(2):
                        hs = slice(h * DH, (h + 1) * DH)
                        step(f"khi{b}{h}", ns["k_hi"][b][h][hs, :], ns["k_raw"][hs, bass.ds(i, 1), b, :])
                step("vcg", ns["vcg"][:, :, :].rearrange("p h (a d) -> p (h a) d", a=2)[:, 0:4:3, :],
                     ns["vc"][:, bass.ds(i, 1), :].broadcast_to([NCMPCOL, 2, DH]))
                step("bias", ns["bias"][:, :], col("alibi", 16 * i, 16))
                for n in range(6):
                    step(f"g{n}", ns["g"][:, n, :], bank[2 + n][:, :], (pe_done, M.after(name, "g", i)))
                own(name, "cexp", i)
                act.wait_ge(vec_done, V.after(name, "csub", i))
                nc.scalar.activation(ns["cmp"][:, :], ns["cmp"][:, :], ACT.Exp).then_inc(act_done, 1)
                for n in range(4):
                    step(f"pt{n}", ns["prob"][n // 2][0:NCMPCOL, (n % 2) * T:(n % 2 + 1) * T],
                         bank[2 + n][0:NCMPCOL, :], (pe_done, M.after(name, "tr", i)))

                def out_hi(j):
                    step(f"ohi{j}", ns["o_hi"][:, bass.ds(2 * i + j, 1), :], ns["g"][:, 3 * j, :],
                         (pool_done, G.after(name, f"ga.{2 * j + 1}", i)))

                for u in range(4):
                    for h in range(2):
                        for n, b, at in SCORE_TILES:
                            own(name, f"exp{h}t{n}.{u}", i)
                            act.wait_ge(pe_done, M.after(name, f"sc{h}b{b}.{u}", i))
                            w = (TT - n) * P
                            nc.scalar.activation(ns["prob"][h][:, PROB_AT[n]:PROB_AT[n] + w],
                                                 bank[SLOT[h][b]][:, at:at + w], ACT.Exp,
                                                 bias=ns["bias"][:, 4 * n + 2 * (u // 2) + h:4 * n + 2 * (u // 2) + h + 1]).then_inc(act_done, 1)
                    if u == 2:
                        out_hi(0)
                out_hi(1)

            with act.Fori(0, 2) as i:
                nsa_group(i)
            out_layer("nsa_out", "ffn2_norm0")
            stats("sw0", D)
            glu_in("sw0_in", None)
            out_layer("sw0_out", "mix_norm1")

            stats("pw1", D)
            s = SLAB_AT["pw1"]
            with act.Fori(0, KD // 2) as i:
                for c in range(2):
                    split_hi(s + 2 * c + RING, i, 4)
                    own("pw1", f"w{c}", i)
                    act.wait_ge(vec_done, V.after("pw1", f"ua{c}", i) - 1)
                    nc.scalar.activation(cf["w"][c][:, :], col("w_dw", 2 * TAPS * i + TAPS * c, TAPS), ACT.Copy)\
                        .then_inc(act_done, 1)
                    own("pw1", f"sg{c}", i)
                    act.wait_ge(vec_done, V.after("pw1", f"ug{c}", i))
                    nc.scalar.activation(cf["gate"][:, :], cf["gate"][:, :], ACT.Sigmoid,
                                         bias=col("b_pw1", 2 * i + (KD + c))).then_inc(act_done, 1)
                    for k in range(PE_TAPS):
                        own("pw1", f"diag{k}_{c}", i)
                        t = TAPS - PE_TAPS + k
                        nc.scalar.activation(cf["diag"][c][:, k, :], ident, ACT.Copy, scale=cf["w"][c][:, t:t + 1])\
                            .then_inc(act_done, 1)
                    split_hi(s + 2 * c + 1 + RING, i, 4)
                    own("pw1", f"t{c}", i)
                    act.wait_ge(vec_done, V.after("pw1", f"z{c}", i))
                    nc.scalar.activation(cf["acc"][c][:, :], cf["z"][c][:, 0:T], ACT.Identity,
                                         bias=col("b_dw", 2 * i + c), scale=cf["w"][c][:, 0:1]).then_inc(act_done, 1)
            own("ln", "mean")
            act.wait_ge(pe_done, M.after("ln", "mean"))
            nc.scalar.activation(root[:, :], bank[7][:, :], ACT.Copy, scale=1.0 / D).then_inc(act_done, 1)
            for n in range(KD):
                own("ln", f"sq{n}")
                act.wait_ge(vec_done, V.after("ln", f"xc{n}"))
                if n >= 2:
                    act.wait_ge(pe_done, M.after("ln", f"v{n - 2}"))
                nc.scalar.activation(sq[n % 2][:, :], cf["y"][:, n, :], ACT.Square).then_inc(act_done, 1)
            own("ln", "root")
            act.wait_ge(pe_done, M.after("ln", f"v{KD - 1}"))
            nc.scalar.activation(root[:, :], bank[7][:, :], ACT.Sqrt, bias=col("eps_ln"), scale=1.0 / D)\
                .then_inc(act_done, 1)
            for n in range(KD):
                own("ln", f"s{n}")
                act.wait_ge(vec_done, V.after("ln", f"yn{n}"))
                nc.scalar.activation(cf["y"][:, n, :], cf["y"][:, n, :], ACT.Silu, bias=col("ln_b", n),
                                     scale=col("ln_g", n)).then_inc(act_done, 1)
                own("ln", f"hi{n}")
                nc.scalar.activation(cf["o_hi"][:, n, :], cf["y"][:, n, :], ACT.Copy).then_inc(act_done, 1)
            out_layer("pw2", "ffn2_norm1")
            stats("sw1", D)
            glu_in("sw1_in", None)
            out_layer("sw1_out", None, False)
            stats("final", D)

        @block.vector
        def _(dve):
            def own(plan_stage, step, turn=0):
                n = V.after(plan_stage, step, turn) - 1
                if isinstance(n, int) and n == 0:
                    return
                dve.wait_ge(vec_done, n)

            def split_lo(s0, turn=0, per=0):
                if isinstance(turn, int) and s0 + per * turn >= NSLABS:
                    return
                dve.wait_ge(hi_ready, s0 + 1 + turn * per)
                nc.vector.tensor_tensor(w_lo[s0 % RING][:, :], raw[s0 % RAW][:, :],
                                        w_hi[s0 % RING][:, :].bitcast(F), ALU.subtract).then_inc(lo_ready, 1)

            def norm_lo(name, c, n, gain, turn=0):
                own(name, f"lo{c}", turn)
                dve.wait_ge(act_done, A.after(name, f"hi{c}", turn))
                nc.vector.scalar_tensor_tensor(h_lo[:, bass.ds(n, 1), :], x[:, bass.ds(n, 1), :], col(gain, n),
                                               h_hi[:, bass.ds(n, 1), :].bitcast(F), ALU.mult, ALU.subtract)\
                    .then_inc(vec_done, 1)

            def stats(name, cols_too=False):
                own(name + ".stat", "rstd")
                dve.wait_ge(act_done, A.after(name + ".stat", "root"))
                nc.vector.reciprocal(rstd[:, :], root[:, :]).then_inc(vec_done, 1)
                if cols_too:
                    own(name + ".stat", "rstd_cols")
                    dve.wait_ge(act_done, A.after(name + ".stat", "root_cols"))
                    nc.vector.reciprocal(rstd_col[:, :], root_col[:, :]).then_inc(vec_done, 1)

            def out_layer(name, gain, full=True, bias=None):
                parts = OUT[name]

                def half(i):
                    s = SLAB_AT[name]
                    for c in range(4):
                        for _k in parts:
                            split_lo(s + RING, i, 4 * len(parts))
                            s += 1
                        own(name, f"x{c}", i)
                        dve.wait_ge(slab_used, s + i * (4 * len(parts)))
                        n = 4 * i + c
                        if bias:
                            nc.vector.scalar_tensor_tensor(x[:, bass.ds(n, 1), :], bank[4 + c % 2][:, :], col(bias, n),
                                                           x[:, bass.ds(n, 1), :], ALU.add, ALU.add).then_inc(vec_done, 1)
                        else:
                            nc.vector.tensor_tensor(x[:, bass.ds(n, 1), :], x[:, bass.ds(n, 1), :],
                                                    bank[4 + c % 2][:, :], ALU.add).then_inc(vec_done, 1)
                        if full:
                            norm_lo(name, c, n, gain, i)

                if name == "sw1_out":
                    half(0)
                    half(1)
                else:
                    with dve.Fori(0, 2) as i:
                        half(i)

            for s in range(RING):
                split_lo(s)
            own("init", "side")
            dve.wait_ge(act_done, A.after("init", "side"))
            nc.vector.tensor_tensor(side_lo[:, :], side_raw[:, :], side_hi[:, :].bitcast(F), ALU.subtract)\
                .then_inc(vec_done, 1)
            for n in range(KD):
                norm_lo("x_in", n, n, "fox_norm")
            stats("fox", True)

            s = SLAB_AT["fox_v"]
            for c in range(4):
                split_lo(s + c + RING)
            hs = slice(0, FOX_H)
            own("fox_v", "z0")
            dve.wait_ge(pe_done, M.after("fox_v", "f"))
            nc.vector.tensor_tensor(fx["z"][hs, :], rstd[hs, :], bank[4][hs, :], ALU.mult).then_inc(vec_done, 1)
            own("fox_v", "z")
            nc.vector.tensor_scalar(fx["z"][hs, :], fx["z"][hs, :], cols[hs, COLS["b_fox"]:COLS["b_fox"] + 1], None,
                                    ALU.add).then_inc(vec_done, 1)
            own("fox_v", "na")
            nc.vector.scalar_tensor_tensor(fx["na"][hs, 0:T], fx["z"][hs, :], -1.0, fx["z"][hs, :], ALU.mult, ALU.min)\
                .then_inc(vec_done, 1)
            own("fox_v", "logf")
            dve.wait_ge(act_done, A.after("fox_v", "ln"))
            nc.vector.scalar_tensor_tensor(fx["na"][hs, 0:T], fx["z"][hs, :], 0.0, fx["k_raw"][hs, :], ALU.min,
                                           ALU.subtract).then_inc(vec_done, 1)
            own("fox_v", "scan")
            dve.wait_ge(pool_done, G.after("fox_v", "ones_row"))
            nc.vector.tensor_tensor_scan(fx["negc"][hs, :], fx["ones_row"][hs, :], fx["na"][hs, 0:T], 0.0, ALU.mult,
                                         ALU.subtract).then_inc(vec_done, 1)
            own("fox_v", "negc_r")
            nc.vector.tensor_copy(fx["negc_r"][hs, :], fx["negc"][hs, :]).then_inc(vec_done, 1)
            own("fox_v", "negc_cols")
            dve.wait_ge(pe_done, M.after("fox_v", "negc_cols"))
            nc.vector.tensor_copy(fx["negc_col"][:, :, :].rearrange("p t h -> p (t h)"), bank[5][:, 0:TT * FOX_H])\
                .then_inc(vec_done, 1)
            for c in range(4):
                split_lo(s + 4 + c + RING)

            def fox_proj(name, sfx, turn, s0, per, pair):
                split_lo(s0 + RING, turn, per)
                own(name, "qt" + sfx, turn)
                dve.wait_ge(slab_used, s0 + 1 + turn * per)
                nc.vector.scalar_tensor_tensor(fx["q_raw"][:, :], bank[0][:, :], DH ** -0.5, rstd[:, :], ALU.mult,
                                               ALU.mult).then_inc(vec_done, 1)
                own(name, "qlo" + sfx, turn)
                dve.wait_ge(act_done, A.after(name, "qhi" + sfx, turn))
                nc.vector.tensor_tensor(fx["q_lo"][:, :], fx["q_raw"][:, :], fx["q_hi"][:, :].bitcast(F),
                                        ALU.subtract).then_inc(vec_done, 1)
                for h in range(2):
                    own(name, f"sel{h}{sfx}", turn)
                    nc.vector.tensor_scalar(fx["sel"][h][:, :], ones[:, :], mats[:, 0, bass.ds(2 * pair + h, 1)], None,
                                            ALU.mult).then_inc(vec_done, 1)
                split_lo(s0 + 1 + RING, turn, per)
                own(name, "kt" + sfx, turn)
                dve.wait_ge(slab_used, s0 + 2 + turn * per)
                nc.vector.tensor_tensor(fx["k_raw"][:, :], rstd[:, :], bank[1][:, :], ALU.mult).then_inc(vec_done, 1)
                for h in range(2):
                    own(name, f"klo{h}{sfx}", turn)
                    dve.wait_ge(act_done, A.after(name, f"khi{h}{sfx}", turn))
                    hs = slice(h * DH, (h + 1) * DH)
                    nc.vector.tensor_tensor(fx["k_lo"][h][hs, :], fx["k_raw"][hs, :], fx["k_hi"][h][hs, :].bitcast(F),
                                            ALU.subtract).then_inc(vec_done, 1)

            def head_max(b, name, h, sfx, turn):
                for n, bk, at in MAX_TILES:
                    own(name, f"mx{h}t{n}{sfx}", turn)
                    dve.wait_ge(pe_done, M.after(name, f"max{h}b{bk}{sfx}", turn))
                    nc.vector.tensor_reduce(b["negm"][h][:, n:n + 1], bank[SLOT[h][bk]][:, at:at + (n + 1) * P], AX,
                                            ALU.max, negate=True).then_inc(vec_done, 1)
                own(name, f"dg{h}{sfx}", turn)
                nc.vector.tensor_tensor(
                    b["diag"][h][:, :, :], mats[:, 0:1, :].broadcast_to([P, TT, P]),
                    b["negm"][h][:, :].rearrange("p (t o) -> p t o", o=1).broadcast_to([P, TT, P]),
                    ALU.mult).then_inc(vec_done, 1)

            def fox_max(name, sfx, turn):
                for h in range(2):
                    head_max(fx, name, h, sfx, turn)

            def fox_norm(name, sfx, turn, pair):
                for h in range(2):
                    hs = slice(h * DH, (h + 1) * DH)
                    sums = slice((1 - h) * DH, (2 - h) * DH)
                    own(name, f"rc{h}{sfx}", turn)
                    dve.wait_ge(pe_done, M.after(name, f"pv{h}{sfx}", turn))
                    nc.vector.reciprocal(fx["rec"][hs, :], bank[h][sums, :]).then_inc(vec_done, 1)
                    own(name, f"on{h}{sfx}", turn)
                    nc.vector.tensor_tensor(fx["o"][hs, :], fx["rec"][hs, :], bank[h][hs, :], ALU.mult)\
                        .then_inc(vec_done, 1)
                own(name, "olo" + sfx, turn)
                dve.wait_ge(act_done, A.after(name, "ohi" + sfx, turn))
                nc.vector.tensor_tensor(fox_o[1][:, bass.ds(pair, 1), :], fx["o"][:, :],
                                        fox_o[0][:, bass.ds(pair, 1), :].bitcast(F), ALU.subtract).then_inc(vec_done, 1)

            s = SLAB_AT["fox_qk"]
            fox_proj("fox_first", "", 0, s, 0, 0)
            fox_max("fox_first", "", 0)
            with dve.Fori(0, 3) as i:
                for c in range(2):
                    fox_proj("fox_loop", f".{c}", i, s + 2 + 2 * c, 4, 2 * i + (c + 1))
                    fox_max("fox_loop", f".{c}", i)
                    fox_norm("fox_loop", f".{c}", i, 2 * i + c)
            fox_proj("fox_peel", ".0", 0, s + 14, 0, FOX_PAIRS - 1)
            fox_max("fox_peel", ".0", 0)
            fox_norm("fox_peel", ".0", 0, FOX_PAIRS - 2)
            fox_norm("fox_last", "", 0, FOX_PAIRS - 1)
            out_layer("fox_out", "ffn_norm0")

            def glu_in(name, conv):
                if conv:
                    dve.wait_ge(pool_done, G.end("pad" + name[3]))
                with dve.Fori(0, KH // 2) as i:
                    for c in range(2):
                        s = SLAB_AT[name] + 2 * c
                        for n, step in ((0, "ug"), (1, "uv")):
                            own(name, f"{step}{c}", i)
                            dve.wait_ge(slab_used, s + 1 + n + i * 4)
                            dst = u[n][:, 2:T + 2] if conv else tap[n][:, :]
                            nc.vector.tensor_tensor(dst, rstd[:, :], bank[2 * c + n][:, :], ALU.mult)\
                                .then_inc(vec_done, 1)
                        split_lo(s + RING, i, 4)
                        if conv:
                            for k in (1, 2):
                                for n, g in ((0, "g"), (1, "v")):
                                    own(name, f"c{k}{g}{c}", i)
                                    dve.wait_ge(act_done, A.after(name, f"tap{g}{c}", i))
                                    at = (2 * i + (c + KH * n)) * 4
                                    nc.vector.scalar_tensor_tensor(tap[n][:, :], u[n][:, 2 - k:T + 2 - k],
                                                                   col(conv, at + 2 - k), tap[n][:, :], ALU.mult,
                                                                   ALU.add).then_inc(vec_done, 1)
                        split_lo(s + 1 + RING, i, 4)
                        own(name, f"mul{c}", i)
                        dve.wait_ge(act_done, A.after(name, f"silu{c}", i))
                        nc.vector.tensor_tensor(tap[0][:, :], tap[0][:, :], tap[1][:, :], ALU.mult).then_inc(vec_done, 1)
                        own(name, f"lo{c}", i)
                        dve.wait_ge(act_done, A.after(name, f"hi{c}", i))
                        nc.vector.tensor_tensor(act_lo[:, bass.ds(2 * i + c, 1), :], tap[0][:, :],
                                                act_hi[:, bass.ds(2 * i + c, 1), :].bitcast(F), ALU.subtract)\
                            .then_inc(vec_done, 1)

            stats("ffn0")
            glu_in("ffn0_in", "conv0")
            out_layer("ffn0_out", "kv_in_norm")

            stats("mla")
            for n in range(KD):
                own("mla_kvq", f"h_lo{n}")
                dve.wait_ge(act_done, A.after("mla_kvq", f"h_hi{n}"))
                nc.vector.scalar_tensor_tensor(ml["o_lo"][:, n, :], x[:, n, :], col("mla_norm", n),
                                               ml["o_hi"][:, n, :].bitcast(F), ALU.mult, ALU.subtract)\
                    .then_inc(vec_done, 1)
            tl = [ml["prob"][0][:, j * T:(j + 1) * T] for j in range(2)]
            ra, rb = (ml["prob"][1][:, j * T:(j + 1) * T] for j in range(2))

            def kvq_splits(t):
                for j in range(kvq_slabs(t - 1), kvq_slabs(t)):
                    split_lo(SLAB_AT["mla_kvq"] + j + RING)

            def rotate(name, steps, turn, src, a, b):
                own(name, steps[0], turn)
                nc.vector.tensor_tensor(a[:, :], ml["cos"][:, :], src[:, :], ALU.mult).then_inc(vec_done, 1)
                for j in range(2):
                    own(name, steps[1 + j], turn)
                    to, of = slice(64 * j, 64 * j + 64), slice(64 - 64 * j, 128 - 64 * j)
                    nc.vector.tensor_tensor(b[to, :], ml["sin"][to, :], src[of, :], ALU.mult).then_inc(vec_done, 1)
                own(name, steps[3], turn)
                nc.vector.tensor_tensor(a[:, :], a[:, :], b[:, :], ALU.add).then_inc(vec_done, 1)

            for t in range(2):
                own("mla_kvq", f"l{t}")
                dve.wait_ge(*kvq_done(t))
                nc.vector.tensor_tensor(tl[t], rstd[:, :], bank[KVQ_BANK[t]][:, :], ALU.mult).then_inc(vec_done, 1)
                kvq_splits(t)
            dve.wait_ge(tables_loaded, 32)
            dve.wait_ge(*kvq_done(2))
            rotate("mla_kvq", ["kra", "krb0", "krb1", "krs"], 0, bank[2], ra, rb)
            own("mla_kvq", "krn")
            nc.vector.tensor_tensor(ra, ra, rstd[:, :], ALU.mult).then_inc(vec_done, 1)
            kvq_splits(2)
            for h in range(2):
                own("mla_kvq", f"kr_lo{h}")
                dve.wait_ge(act_done, A.after("mla_kvq", f"kr_hi{h}"))
                nc.vector.scalar_tensor_tensor(ml["kr_lo"][h][:, :], ra, col("rope_pick", h),
                                               ml["kr_hi"][h][:, :].bitcast(F), ALU.mult, ALU.subtract)\
                    .then_inc(vec_done, 1)
            own("mla_kvq", "rstd_l")
            dve.wait_ge(act_done, A.after("mla_kvq", "root_l"))
            nc.vector.reciprocal(sq_sum[:, :], root[:, :]).then_inc(vec_done, 1)
            for j in range(KL):
                own("mla_kvq", f"ln{j}")
                nc.vector.scalar_tensor_tensor(tl[j], tl[j], col("kv_norm", j), sq_sum[:, :], ALU.mult, ALU.mult)\
                    .then_inc(vec_done, 1)
            for j in range(KL):
                own("mla_kvq", f"lo_l{j}")
                dve.wait_ge(act_done, A.after("mla_kvq", f"hi_l{j}"))
                nc.vector.tensor_tensor(ml["l_lo"][:, j, :], tl[j], ml["l_hi"][:, j, :].bitcast(F), ALU.subtract)\
                    .then_inc(vec_done, 1)
            for j in range(KQ):
                own("mla_kvq", f"q{j}")
                dve.wait_ge(*kvq_done(3 + j))
                if j >= 2:
                    dve.wait_ge(act_done, A.after("mla_kvq", f"q_sq{j - 2}"))
                nc.vector.tensor_tensor(tl[j % 2], rstd[:, :], bank[KVQ_BANK[3 + j]][:, :], ALU.mult)\
                    .then_inc(vec_done, 1)
                kvq_splits(3 + j)
                own("mla_kvq", f"q_lo{j}")
                dve.wait_ge(act_done, A.after("mla_kvq", f"q_hi{j}"))
                nc.vector.scalar_tensor_tensor(ml["ql_lo"][:, j, :], tl[j % 2], col("q_norm", j),
                                               ml["ql_hi"][:, j, :].bitcast(F), ALU.mult, ALU.subtract)\
                    .then_inc(vec_done, 1)
            own("mla_kvq", "rstd_q")
            dve.wait_ge(act_done, A.after("mla_kvq", "root_q"))
            nc.vector.reciprocal(rstd[:, :], root[:, :]).then_inc(vec_done, 1)
            scale = (NOPE + ROPE) ** -0.5
            for step, table in (("cos_q", ml["cos"]), ("sin_q", ml["sin"])):
                own("mla_kvq", step)
                nc.vector.scalar_tensor_tensor(table[:, :], table[:, :], scale, rstd[:, :], ALU.mult, ALU.mult)\
                    .then_inc(vec_done, 1)

            def mla_step(name, turn, s0, per, n_out):
                for h, raw_q in ((0, ml["q_raw"]), (1, ml["rot"])):
                    own(name, f"n{h}", turn)
                    dve.wait_ge(slab_used, s0 + h + 1 + turn * per)
                    nc.vector.scalar_tensor_tensor(raw_q[:, :], bank[h][:, :], scale, rstd[:, :], ALU.mult, ALU.mult)\
                        .then_inc(vec_done, 1)
                    split_lo(s0 + h + RING, turn, per)
                    own(name, f"n{h}lo", turn)
                    dve.wait_ge(act_done, A.after(name, f"n{h}hi", turn))
                    nc.vector.tensor_tensor(ml["qn_lo"][h][:, :], raw_q[:, :], ml["qn_hi"][h][:, :].bitcast(F),
                                            ALU.subtract).then_inc(vec_done, 1)
                dve.wait_ge(slab_used, s0 + 3 + turn * per)
                rotate(name, ["ra", "rb0", "rb1", "rs"], turn, bank[0], ml["q_raw"], ml["rot"])
                split_lo(s0 + 2 + RING, turn, per)
                own(name, "rlo", turn)
                dve.wait_ge(act_done, A.after(name, "rhi", turn))
                nc.vector.tensor_tensor(ml["qr_lo"][:, :], ml["q_raw"][:, :], ml["qr_hi"][:, :].bitcast(F),
                                        ALU.subtract).then_inc(vec_done, 1)
                for h in range(2):
                    own(name, f"k{h}lo", turn)
                    dve.wait_ge(act_done, A.after(name, f"k{h}hi", turn))
                    nc.vector.tensor_tensor(ml["k_lo"][h][:, :], bank[1 - h][:, :], ml["k_hi"][h][:, :].bitcast(F),
                                            ALU.subtract).then_inc(vec_done, 1)
                for h in range(2):
                    if n_out is not None:
                        mla_norm(name, turn, n_out, h)
                    head_max(ml, name, h, "", turn)
                split_lo(s0 + 3 + RING, turn, per)

            def mla_norm(name, turn, n, h):
                own(name, f"rc{h}", turn)
                dve.wait_ge(pe_done, M.after(name, f"sum{h}", turn))
                nc.vector.reciprocal(ml["rec"][:, :], bank[0][:, :]).then_inc(vec_done, 1)
                own(name, f"on{h}", turn)
                nc.vector.tensor_tensor(ml["o"][:, :], ml["rec"][:, :], bank[1][:, :], ALU.mult).then_inc(vec_done, 1)
                own(name, f"olo{h}", turn)
                dve.wait_ge(act_done, A.after(name, f"ohi{h}", turn))
                nc.vector.tensor_tensor(ml["o_lo"][:, bass.ds(n + h, 1), :], ml["o"][:, :],
                                        ml["o_hi"][:, bass.ds(n + h, 1), :].bitcast(F), ALU.subtract)\
                    .then_inc(vec_done, 1)

            for half in "ab":
                s = SLAB_AT["mla_" + half]
                mla_step(f"mla_{half}_first", 0, s, 0, None)
                with dve.Fori(0, 3) as i:
                    mla_step(f"mla_{half}_loop", i, s + 4, 4, 2 * i)
                for h in range(2):
                    mla_norm(f"mla_{half}_last", 0, 6, h)
                if half == "a":
                    out_layer("mla_out_a", None, False)
            out_layer("mla_out_b", "ffn_norm1")
            stats("ffn1")
            glu_in("ffn1_in", "conv1")
            out_layer("ffn1_out", None, False)

            stats("x2")
            for n in range(KD):
                own("x2", f"x{n}")
                nc.vector.scalar_tensor_tensor(x[:, n, :], x[:, n, :], col("final_norm", n), rstd[:, :], ALU.mult, ALU.mult)\
                    .then_inc(vec_done, 1)
                norm_lo("x2", n, n, "mix_norm0")
            stats("nsa", True)
            s = SLAB_AT["nsa_misc"]
            for n, kv in enumerate("kv"):
                for g in range(2):
                    for h in range(2):
                        own("nsa_misc", f"b{kv}{g}{h}")
                        dve.wait_ge(slab_used, s + n + 1)
                        dve.wait_ge(pool_done, G.after("nsa_misc", "pad5"))
                        nc.vector.tensor_tensor(ns["bk"][h * DH:(h + 1) * DH, g, 0:T - h],
                                                rstd[g * DH:(g + 1) * DH, h:T], bank[n][g * DH:(g + 1) * DH, h:T],
                                                ALU.mult).then_inc(vec_done, 1)
                split_lo(s + n + RING)
                for g in range(2):
                    for half in range(2):
                        own("nsa_misc", f"bl{kv}{g}{half}")
                        if n:
                            dve.wait_ge(act_done, A.after("nsa_misc", "hik"))
                        src = ns["bk"][:, g, half * STRIDE:half * STRIDE + T].rearrange("p (n j o) -> p j n o", j=8, o=2)
                        js = slice(half * 8, half * 8 + 8)
                        pos = col("cmp_pos_" + kv, half * 8, 8).rearrange("p (j o) -> p j o", o=1)
                        nc.vector.tensor_tensor(ns["blk"][:, js, g, :], src[:, :, :, 0],
                                                pos.broadcast_to([P, 8, NCMPCOL]), ALU.add).then_inc(vec_done, 1)
                if n == 0:
                    own("nsa_misc", "lok")
                    dve.wait_ge(act_done, A.after("nsa_misc", "hik"))
                    nc.vector.tensor_tensor(ns["b_lo"][0][:, :, :, :], ns["blk"][:, :, :, :],
                                            ns["b_hi"][0][:, :, :, :].bitcast(F), ALU.subtract).then_inc(vec_done, 1)
            own("nsa_misc", "lov")
            dve.wait_ge(act_done, A.after("nsa_misc", "hiv"))
            nc.vector.tensor_tensor(ns["b_lo"][1][:, :, :, :], ns["blk"][:, :, :, :],
                                    ns["b_hi"][1][:, :, :, :].bitcast(F), ALU.subtract).then_inc(vec_done, 1)
            for g in range(4):
                run = ns["run"]
                own("nsa_misc", f"u{g}")
                dve.wait_ge(slab_used, s + 3 + g)
                nc.vector.tensor_tensor(run[0][:, STRIDE:], rstd[:, :], bank[2 + g][:, :], ALU.mult).then_inc(vec_done, 1)
                split_lo(s + 2 + g + RING)
                src = run[0]
                for n in range(g + 1):
                    own("nsa_misc", f"sum{n}_{g}")
                    dst = run[1 + n % 2]
                    if g and n < 2:
                        dve.wait_ge(act_done, A.after("nsa_misc", f"d_hi{g - 1}"))
                    nc.vector.tensor_tensor(dst[:, STRIDE:], src[:, STRIDE:], src[:, STRIDE - 2 ** n:STRIDE - 2 ** n + T],
                                            ALU.add).then_inc(vec_done, 1)
                    src = dst
                dst = run[1 + (g + 1) % 2]
                own("nsa_misc", f"d{g}")
                nc.vector.scalar_tensor_tensor(dst[:, STRIDE:], src[:, STRIDE:], 2.0 ** -(g + 1), run[0][:, STRIDE:], ALU.mult,
                                               ALU.subtract).then_inc(vec_done, 1)
                own("nsa_misc", f"early{g}")
                nc.vector.tensor_tensor(src[:, STRIDE:2 * STRIDE], src[:, STRIDE:2 * STRIDE],
                                        col("pool_inv", g * STRIDE, STRIDE), ALU.mult).then_inc(vec_done, 1)
                own("nsa_misc", f"first{g}")
                nc.vector.tensor_tensor(dst[:, STRIDE:2 * STRIDE], src[:, STRIDE:2 * STRIDE], run[0][:, STRIDE:2 * STRIDE],
                                        ALU.subtract).then_inc(vec_done, 1)
                own("nsa_misc", f"d_lo{g}")
                dve.wait_ge(act_done, A.after("nsa_misc", f"d_hi{g}"))
                nc.vector.tensor_tensor(ns["o_lo"][:, 4 + g, :], dst[:, STRIDE:], ns["o_hi"][:, 4 + g, :].bitcast(F),
                                        ALU.subtract).then_inc(vec_done, 1)
            own("nsa_misc", "gz")
            dve.wait_ge(pe_done, M.after("nsa_misc", "gate"))
            dve.wait_ge(pool_done, G.after("nsa_misc", "gates0"))
            nc.vector.tensor_tensor(ns["gates"][0:NGATE, :], rstd[0:NGATE, :], bank[6][0:NGATE, :], ALU.mult)\
                .then_inc(vec_done, 1)
            for c in range(6, 10):
                split_lo(s + c + RING)
            for h in range(2):
                own("nsa_misc", f"kcl{h}")
                dve.wait_ge(act_done, A.after("nsa_misc", f"kc{h}"))
                hs = slice(h * DH, (h + 1) * DH)
                nc.vector.tensor_tensor(ns["kc_lo"][hs, :, h, :], bank[1][hs, 0:64].rearrange("p (g n) -> p g n", g=2),
                                        ns["kc_hi"][hs, :, h, :].bitcast(F), ALU.subtract).then_inc(vec_done, 1)
            split_lo(s + 10 + RING)
            split_lo(s + 11 + RING)
            for g in range(4):
                own("nsa_misc", f"p_lo{g}")
                dve.wait_ge(act_done, A.after("nsa_misc", f"p_hi{g}"))
                nc.vector.scalar_tensor_tensor(ns["o_lo"][:, 4 + g, :], bank[2 + g][:, :], col("pool_scale", g),
                                               ns["o_hi"][:, 4 + g, :].bitcast(F), ALU.mult, ALU.subtract)\
                    .then_inc(vec_done, 1)
            s = SLAB_AT["nsa_attn"]
            for g in range(2):
                for j in range(2):
                    split_lo(s + 4 * g + j + RING)
                    own("nsa_proj", f"q{j}{g}")
                    dve.wait_ge(slab_used, s + 4 * g + j + 1)
                    nc.vector.scalar_tensor_tensor(ns["q_raw"][:, 2 * g + j, :], bank[4 * g + j][:, :], DH ** -0.5, rstd[:, :],
                                                   ALU.mult, ALU.mult).then_inc(vec_done, 1)
                split_lo(s + 4 * g + 2 + RING)
                for b in range(2):
                    for h in range(2):
                        own("nsa_proj", f"k{b}{h}{g}")
                        dve.wait_ge(slab_used, s + 4 * g + 3)
                        nc.vector.tensor_tensor(ns["k_raw"][h * DH:(h + 1) * DH, g, b, :], rstd[b * DH:(b + 1) * DH, :],
                                                bank[4 * g + 2][b * DH:(b + 1) * DH, :], ALU.mult).then_inc(vec_done, 1)
                split_lo(s + 4 * g + 3 + RING)

            def nsa_group(i):
                name = "nsa_attn"
                for n in range(6):
                    for h in range(2):
                        own(name, f"gs{n}{h}", i)
                        dve.wait_ge(slab_used, SLAB_AT["nsa_out"])
                        nc.vector.tensor_scalar(ns["gsel"][:, n * P + h * DH:n * P + (h + 1) * DH], ones[:, 0:DH],
                                                mats[:, 0, bass.ds(12 * i + (6 * (n // 3) + n % 3 + 3 * h), 1)], None,
                                                ALU.mult).then_inc(vec_done, 1)
                own(name, "glo", i)
                dve.wait_ge(act_done, A.after(name, "ghi", i))
                nc.vector.tensor_tensor(ns["diag"][1][:, :, :].rearrange("p t n -> p (t n)"), ns["gates"][:, :],
                                        ns["diag"][0][:, :, :].rearrange("p t n -> p (t n)").bitcast(F), ALU.subtract)\
                    .then_inc(vec_done, 1)
                for j in range(2):
                    own(name, f"q{j}lo", i)
                    dve.wait_ge(act_done, A.after(name, f"q{j}hi", i))
                    nc.vector.tensor_tensor(ns["q_lo"][j][:, :], ns["q_raw"][:, bass.ds(2 * i + j, 1), :],
                                            ns["q_hi"][j][:, :].bitcast(F), ALU.subtract).then_inc(vec_done, 1)
                c = ns["cmp"][:, :]
                c3 = c.rearrange("p (r n) -> p r n", n=NCMPCOL)
                m = ns["cmp_m"][:, :]
                spread = m.rearrange("p (r o) -> p r o", o=1).broadcast_to([P, 16, NCMPCOL])
                own(name, "cs", i)
                dve.wait_ge(pe_done, M.after(name, "cs", i))
                dve.wait_ge(tables_loaded, 64)
                nc.vector.tensor_tensor(c, ns["tab"][:, bass.ds(i, 1), :], bank[0][:, :], ALU.add).then_inc(vec_done, 1)
                own(name, "cm", i)
                nc.vector.tensor_reduce(m, c3, AX, ALU.max, negate=True).then_inc(vec_done, 1)
                own(name, "cmin", i)
                nc.vector.tensor_scalar(m, m, 1e29, None, ALU.min).then_inc(vec_done, 1)
                own(name, "csub", i)
                nc.vector.tensor_tensor(c3, c3, spread, ALU.add).then_inc(vec_done, 1)
                own(name, "csum", i)
                dve.wait_ge(act_done, A.after(name, "cexp", i))
                nc.vector.tensor_reduce(m, c3, AX, ALU.add).then_inc(vec_done, 1)
                own(name, "cmax", i)
                nc.vector.tensor_scalar(m, m, 1e-30, None, ALU.max).then_inc(vec_done, 1)
                own(name, "crec", i)
                nc.vector.reciprocal(m, m).then_inc(vec_done, 1)
                own(name, "cp", i)
                nc.vector.tensor_tensor(c3, c3, spread, ALU.mult).then_inc(vec_done, 1)
                for b in range(2):
                    for h in range(2):
                        own(name, f"klo{b}{h}", i)
                        dve.wait_ge(act_done, A.after(name, f"khi{b}{h}", i))
                        hs = slice(h * DH, (h + 1) * DH)
                        nc.vector.tensor_tensor(ns["k_lo"][b][h][hs, :], ns["k_raw"][hs, bass.ds(i, 1), b, :],
                                                ns["k_hi"][b][h][hs, :].bitcast(F), ALU.subtract).then_inc(vec_done, 1)
                for j in range(2):
                    own(name, f"acc{j}", i)
                    dve.wait_ge(pe_done, M.after(name, f"cpv{j}", i))
                    nc.vector.tensor_tensor(ns["g"][:, 3 * j, :], ns["g"][:, 3 * j, :], bank[j][:, :], ALU.mult)\
                        .then_inc(vec_done, 1)

                def norm(u):
                    for h in range(2):
                        hs, sums = slice(h * DH, (h + 1) * DH), slice((1 - h) * DH, (2 - h) * DH)
                        own(name, f"rc{h}.{u}", i)
                        dve.wait_ge(pe_done, M.after(name, f"pv{h}.{u}", i))
                        nc.vector.reciprocal(ns["rec"][hs, :], bank[h][sums, :]).then_inc(vec_done, 1)
                        own(name, f"on{h}.{u}", i)
                        if u > 1:
                            dve.wait_ge(pool_done, G.after(name, f"gm.{u - 2}", i))
                        nc.vector.tensor_tensor(ns["o"][hs, :], ns["rec"][hs, :], bank[h][hs, :], ALU.mult)\
                            .then_inc(vec_done, 1)

                def out_lo(j):
                    own(name, f"olo{j}", i)
                    dve.wait_ge(act_done, A.after(name, f"ohi{j}", i))
                    nc.vector.tensor_tensor(ns["o_lo"][:, bass.ds(2 * i + j, 1), :], ns["g"][:, 3 * j, :],
                                            ns["o_hi"][:, bass.ds(2 * i + j, 1), :].bitcast(F), ALU.subtract)\
                        .then_inc(vec_done, 1)

                for u in range(4):
                    if u % 2 == 0:
                        for h in range(2):
                            own(name, f"sel{h}.{u}", i)
                            nc.vector.tensor_scalar(ns["sel"][h][:, :], ones[:, :],
                                                    mats[:, 0, bass.ds(4 * i + (u + h), 1)], None, ALU.mult)\
                                .then_inc(vec_done, 1)
                    for h in range(2):
                        head_max(ns, name, h, f".{u}", i)
                    if u:
                        norm(u)
                    if u == 3:
                        out_lo(0)
                norm(4)
                out_lo(1)

            with dve.Fori(0, 2) as i:
                nsa_group(i)
            out_layer("nsa_out", "ffn2_norm0")
            stats("sw0")
            glu_in("sw0_in", None)
            out_layer("sw0_out", "mix_norm1")

            stats("pw1")
            dve.wait_ge(pool_done, G.end("pw1.zero"))
            s = SLAB_AT["pw1"]
            with dve.Fori(0, KD // 2) as i:
                for c in range(2):
                    for n, step, dst in ((0, "ua", cf["a"]), (1, "ug", cf["gate"])):
                        own("pw1", f"{step}{c}", i)
                        dve.wait_ge(slab_used, s + 2 * c + n + 1 + i * 4)
                        nc.vector.tensor_tensor(dst[:, :], rstd[:, :], bank[2 * c + n][:, :], ALU.mult).then_inc(vec_done, 1)
                    split_lo(s + 2 * c + RING, i, 4)
                    own("pw1", f"z{c}", i)
                    dve.wait_ge(act_done, A.after("pw1", f"sg{c}", i))
                    nc.vector.scalar_tensor_tensor(cf["z"][c][:, TAPS - 1:], cf["a"][:, :], col("b_pw1", 2 * i + c),
                                                   cf["gate"][:, :], ALU.add, ALU.mult).then_inc(vec_done, 1)
                    split_lo(s + 2 * c + 1 + RING, i, 4)
                    for k in range(1, TAPS - PE_TAPS):
                        own("pw1", f"t{k}_{c}", i)
                        if k == 1:
                            dve.wait_ge(act_done, A.after("pw1", f"t{c}", i))
                        nc.vector.scalar_tensor_tensor(cf["acc"][c][:, :], cf["z"][c][:, k:k + T], cf["w"][c][:, k:k + 1],
                                                       cf["acc"][c][:, :], ALU.mult, ALU.add).then_inc(vec_done, 1)
                    own("pw1", f"y{c}", i)
                    dve.wait_ge(pe_done, M.after("pw1", f"y{c}", i))
                    nc.vector.tensor_tensor(cf["y"][:, bass.ds(2 * i + c, 1), :], cf["acc"][c][:, :], bank[4 + c][:, :],
                                            ALU.add).then_inc(vec_done, 1)
            for n in range(KD):
                own("ln", f"xc{n}")
                dve.wait_ge(act_done, A.after("ln", "mean"))
                nc.vector.tensor_tensor(cf["y"][:, n, :], cf["y"][:, n, :], root[:, :], ALU.subtract).then_inc(vec_done, 1)
            own("ln", "rstd")
            dve.wait_ge(act_done, A.after("ln", "root"))
            nc.vector.reciprocal(rstd[:, :], root[:, :]).then_inc(vec_done, 1)
            for n in range(KD):
                own("ln", f"yn{n}")
                nc.vector.tensor_tensor(cf["y"][:, n, :], cf["y"][:, n, :], rstd[:, :], ALU.mult).then_inc(vec_done, 1)
            for n in range(KD):
                own("ln", f"lo{n}")
                dve.wait_ge(act_done, A.after("ln", f"hi{n}"))
                nc.vector.tensor_tensor(cf["o_lo"][:, n, :], cf["y"][:, n, :], cf["o_hi"][:, n, :].bitcast(F), ALU.subtract)\
                    .then_inc(vec_done, 1)
            out_layer("pw2", "ffn2_norm1", bias="b_pw2")
            stats("sw1")
            glu_in("sw1_in", None)
            out_layer("sw1_out", None, False)
            stats("final")
            for n in range(KD):
                own("final", f"y{n}")
                nc.vector.scalar_tensor_tensor(x[:, n, :], x[:, n, :], col("final2", n), rstd[:, :], ALU.mult, ALU.mult)\
                    .then_inc(vec_done, 1)

        @block.tensor
        def _(pe):
            def mm(out, lhs, rhs, start, stop):
                return nc.tensor.matmul(out, lhs, rhs, start=start, stop=stop)

            def mm3(out, a, b, start, stop):
                mm(out, a[0], b[0], start, False)
                mm(out, a[0], b[1], False, False)
                return mm(out, a[1], b[0], False, stop)

            def wtile(slot, at, n=P):
                return w_hi[slot][:, at:at + n], w_lo[slot][:, at:at + n]

            def chunk(pair, n):
                return pair[0][:, n, :], pair[1][:, n, :]

            def tile_of(name, out, s0, moving, parts=(KD,), turn=0, per=0, needs=None):
                k = 0
                total = sum(parts)
                for j, n in enumerate(parts):
                    pe.wait_ge(lo_ready, s0 + j + 1 + turn * per)
                    for c in range(n):
                        if needs and needs(k):
                            pe.wait_ge(*needs(k))
                        last = mm3(out, wtile((s0 + j) % RING, c * P), chunk(moving, k), k == 0, k == total - 1)
                        k += 1
                    last.then_inc(slab_used, 1)

            def stats(name, summed, cols_too=False):
                pe.wait_ge(pool_done, G.end(summed))
                mm(bank[7][:, :], ones[:, :], sq_sum[:, :], True, True).then_inc(pe_done, 1)
                if cols_too:
                    for t in range(TT):
                        last = mm(bank[6][:, t:t + 1], sq_sum[:, t * P:(t + 1) * P], ones[:, 0:1], True, True)
                    last.then_inc(pe_done, 1)

            h = (h_hi, h_lo)
            pe.wait_ge(pool_done, G.end("init"))
            stats("fox", "x_in", True)
            pe.wait_ge(vec_done, V.end("x_in"))
            s = SLAB_AT["fox_v"]

            def fox_v_half(half):
                for c in range(4):
                    pe.wait_ge(lo_ready, s + 4 * half + c + 1)
                    for k in (2 * c, 2 * c + 1):
                        for t in range(TT):
                            tok = slice(t * P, (t + 1) * P)
                            last = mm3(bank[t][:, :], (h_hi[:, k, tok], h_lo[:, k, tok]),
                                       wtile((s + c) % RING, (k % 2) * T, T), k == 0, k == KD - 1)
                    last.then_inc(slab_used, 1)

            fox_v_half(0)
            for k in range(KD):
                at = SIDE["w_f"] + k * FOX_H
                last = mm3(bank[4][0:FOX_H, :], (side_hi[:, at:at + FOX_H], side_lo[:, at:at + FOX_H]), chunk(h, k),
                           k == 0, k == KD - 1)
            last.then_inc(pe_done, 1)
            pe.wait_ge(act_done, A.after("fox_v", f"v0t{TT - 1}"))
            fox_v_half(1)
            pe.wait_ge(vec_done, V.after("fox_v", "scan"))
            for t in range(TT):
                last = mm(bank[5][:, t * FOX_H:(t + 1) * FOX_H], fx["negc"][0:FOX_H, t * P:(t + 1) * P],
                          ident[0:FOX_H, 0:FOX_H], True, True)
            last.then_inc(pe_done, 1)

            def fox_proj(s0, turn, per):
                tile_of("fox", bank[0][:, :], s0, h, turn=turn, per=per)
                tile_of("fox", bank[1][:, :], s0 + 1, h, turn=turn, per=per)

            def max_scores(b, h, qs, ks, table=None, mask=0):
                for n, bk, at in MAX_TILES:
                    w = (n + 1) * P
                    out = bank[SLOT[h][bk]][:, at:at + w]
                    for j, (q, k) in enumerate(zip(qs, ks)):
                        mm(out, q[:, n * P:(n + 1) * P], k[:, 0:w], j == 0, False)
                    if table is not None:
                        mm(out, b["sel"][h][:, :], table[:, 0:w], False, False)
                    last = mm(bank[SLOT[h][bk]][:, at + n * P:at + w], ident_r[:, :], mask_r[mask][:, :], False, True)
                    if n != 2:
                        last.then_inc(pe_done, 1)

            def scores(b, h, pairs, mask=0):
                for n, bk, at in SCORE_TILES:
                    w = (TT - n) * P
                    out = bank[SLOT[h][bk]][:, at:at + w]
                    keys, queries = slice(n * P, (n + 1) * P), slice(n * P, T)
                    for j, (k, q) in enumerate(pairs):
                        mm3(out, (k[0][:, keys], k[1][:, keys]), (q[0][:, queries], q[1][:, queries]), j == 0, False)
                    mm(out, ones_r[:, :], b["diag"][h][:, n:TT, :], False, False)
                    last = mm(bank[SLOT[h][bk]][:, at:at + P], mask_r[mask][:, :], ident_r[:, :], False, True)
                    if n != 1:
                        last.then_inc(pe_done, 1)

            def values(out, v, prob):
                for n in range(TT):
                    last = mm(out[:, n * P:T], v(n), prob[:, PROB_AT[n]:PROB_AT[n] + (TT - n) * P], n == 0, n == TT - 1)
                return last

            def fox_pv(h):
                last = values(bank[h][:, :], lambda n: fx["vp"][:, n, h, :], fx["prob"][h])
                last.then_inc(pe_done, 1)

            def fox_max(name, sfx, turn, h):
                pe.wait_ge(vec_done, V.after(name, f"sel{h}{sfx}", turn))
                max_scores(fx, h, [fx["q_hi"]], [fx["k_hi"][h]], fx["negc_r"])

            def fox_scores(name, sfx, turn, h):
                pe.wait_ge(vec_done, V.after(name, f"dg{h}{sfx}", turn))
                scores(fx, h, [((fx["k_hi"][h], fx["k_lo"][h]), (fx["q_hi"], fx["q_lo"]))])

            s = SLAB_AT["fox_qk"]
            pe.wait_ge(act_done, A.after("fox_v", f"v1t{TT - 1}"))
            fox_proj(s, 0, 0)
            pe.wait_ge(pool_done, G.after("fox_v", "zk1h"))
            pe.wait_ge(act_done, A.after("fox_first", "khi1"))
            for h_ in range(2):
                fox_max("fox_first", "", 0, h_)
            for h_ in range(2):
                fox_scores("fox_first", "", 0, h_)

            def fox_step(name, sfx, turn, s0, per):
                pe.wait_ge(vec_done, V.after(name, "qt" + sfx, turn) - 2)
                fox_proj(s0, turn, per)
                pe.wait_ge(act_done, A.after(name, "qhi" + sfx, turn) - 5)
                pe.wait_ge(pool_done, G.after(name, "vp0" + sfx, turn) - 1)
                pe.wait_ge(vec_done, V.after(name, "qt" + sfx, turn))
                fox_pv(0)
                pe.wait_ge(act_done, A.after(name, "khi1" + sfx, turn))
                fox_max(name, sfx, turn, 0)
                fox_max(name, sfx, turn, 1)
                pe.wait_ge(vec_done, V.after(name, "kt" + sfx, turn))
                fox_pv(1)
                fox_scores(name, sfx, turn, 0)
                fox_scores(name, sfx, turn, 1)

            with pe.Fori(0, 3) as i:
                for c in range(2):
                    fox_step("fox_loop", f".{c}", i, s + 2 + 2 * c, 4)
            fox_step("fox_peel", ".0", 0, s + 14, 0)
            pe.wait_ge(act_done, A.after("fox_peel", "exp1t2.0"))
            pe.wait_ge(pool_done, G.end("fox_peel"))
            pe.wait_ge(vec_done, V.end("fox_peel"))
            for h_ in range(2):
                fox_pv(h_)

            def out_layer(name, moving, needs):
                parts = OUT[name]
                s0 = SLAB_AT[name]
                for n in range(KD):
                    if n >= 2:
                        pe.wait_ge(vec_done, V.after(name, f"x{(n - 2) % 4}", (n - 2) // 4))
                    tile_of(name, bank[4 + n % 2][:, :], s0 + n * len(parts), moving, parts,
                            needs=needs if n == 0 else None)

            def glu_in(name, moving, source):
                with pe.Fori(0, KH // 2) as i:
                    for c in range(2):
                        for n, step in ((0, "ug"), (1, "uv")):
                            pe.wait_ge(vec_done, V.after(name, f"{step}{c}", i) - len(V.steps[name]))
                            tile_of(name, bank[2 * c + n][:, :], SLAB_AT[name] + 2 * c + n, moving, (KD,), i, 4,
                                    source if c == 0 and n == 0 else None)

            def normed(name):
                return lambda k: (vec_done, V.after(name, f"lo{k % 4}", k // 4))

            def glu(name):
                return lambda k: (vec_done, V.after(name, f"lo{k % 2}", k // 2)) if k in (0, 19, 20, 21) else None

            out_layer("fox_out", fox_o, lambda k: (vec_done, V.end("fox_last")) if k == KD - 1 else None)
            stats("ffn0", "fox_out")
            glu_in("ffn0_in", h, normed("fox_out"))
            out_layer("ffn0_out", (act_hi, act_lo), glu("ffn0_in"))

            stats("mla", "ffn0_out")
            hq = (ml["o_hi"], ml["o_lo"])
            for i in range(9 * KD):
                t, k = divmod(i, KD)
                s, at = divmod(i, 6)
                s += SLAB_AT["mla_kvq"]
                if at == 0:
                    pe.wait_ge(lo_ready, s + 1)
                if t == 0:
                    pe.wait_ge(*normed("ffn0_out")(k))
                if t == 3:
                    pe.wait_ge(vec_done, V.after("mla_kvq", f"h_lo{k}"))
                if k == 0 and t >= 7:
                    pe.wait_ge(vec_done, V.after("mla_kvq", f"l{t - 7}"))
                last = mm3(bank[KVQ_BANK[t]][:, :], wtile(s % RING, at * P), chunk(h if t < 3 else hq, k), k == 0,
                           k == KD - 1)
                if at == 5:
                    last.then_inc(slab_used, 1)
                elif k == KD - 1:
                    last.then_inc(pe_done, 1)
                if t == 2 and k == KD - 1:
                    for j in range(KL):
                        pe.wait_ge(act_done, A.after("mla_kvq", f"sq_l{j}"))
                        last = mm(bank[7][:, :], ones[:, :], sq[j][:, :], j == 0, j == KL - 1)
                    last.then_inc(pe_done, 1)

            pe.wait_ge(act_done, A.after("mla_kvq", "root_l"))
            for j in range(KQ):
                pe.wait_ge(act_done, A.after("mla_kvq", f"q_sq{j}"))
                mm(bank[7][:, :], ones[:, :], sq[j % 2][:, :], j == 0, j == KQ - 1).then_inc(pe_done, 1)

            ql, lat = (ml["ql_hi"], ml["ql_lo"]), (ml["l_hi"], ml["l_lo"])

            def mla_step(name, turn, s0, per, prev):
                if prev:
                    pe.wait_ge(act_done, A.after(name, "n0hi", turn) - 9)
                tile_of(name, bank[0][:, :], s0, ql, (KQ,), turn, per)
                tile_of(name, bank[1][:, :], s0 + 1, ql, (KQ,), turn, per)
                pe.wait_ge(vec_done, V.after(name, "n0", turn))
                tile_of(name, bank[0][:, :], s0 + 2, ql, (KQ,), turn, per)
                pe.wait_ge(lo_ready, s0 + 4 + turn * per)
                kv = (s0 + 3) % RING
                for hd, step in ((0, "n1"), (1, "rb1")):
                    pe.wait_ge(vec_done, V.after(name, step, turn))
                    for k in range(KL):
                        last = mm3(bank[1 - hd][:, :], wtile(kv, (KL * hd + k) * P), chunk(lat, k), k == 0, k == KL - 1)
                    last.then_inc(pe_done, 1)
                if prev:
                    pe.wait_ge(vec_done, V.after(name, "k1lo", turn))
                    pe.wait_ge(pool_done, G.after(name, "s0a", turn) - 1)
                    mla_pv(0)
                pe.wait_ge(act_done, A.after(name, "k1hi", turn))
                for hd in range(2):
                    max_scores(ml, hd, [ml["qn_hi"][hd], ml["qr_hi"]], [ml["k_hi"][hd], ml["kr_hi"][hd]], None, 1)
                if prev:
                    pe.wait_ge(vec_done, V.after(name, "on0", turn))
                    mla_pv(1)
                    pe.wait_ge(vec_done, V.after(name, "on1", turn))
                else:
                    pe.wait_ge(vec_done, V.after(name, "k1lo", turn))
                for t in range(TT):
                    tok = slice(t * P, (t + 1) * P)
                    for k in range(KL):
                        last = mm3(bank[t // 2][:, (t % 2) * 2 * P:(t % 2 + 1) * 2 * P], (lat[0][:, k, tok], lat[1][:, k, tok]),
                                   wtile(kv, (2 * KL + 2 * k) * P, 2 * P), k == 0, k == KL - 1)
                last.then_inc(slab_used, 1)
                for hd in range(2):
                    pe.wait_ge(vec_done, V.after(name, f"dg{hd}", turn))
                    scores(ml, hd, [((ml["k_hi"][hd], ml["k_lo"][hd]), (ml["qn_hi"][hd], ml["qn_lo"][hd])),
                                    ((ml["kr_hi"][hd], ml["kr_lo"][hd]), (ml["qr_hi"], ml["qr_lo"]))], 1)

            def mla_pv(hd):
                values(bank[1][:, :], lambda n: ml["v"][:, n, hd, :], ml["prob"][hd]).then_inc(pe_done, 1)
                mm(bank[0][:, :], ones[:, :], ml["psum"][hd][:, :], True, True).then_inc(pe_done, 1)

            for half in "ab":
                s = SLAB_AT["mla_" + half]
                name = f"mla_{half}_"
                if half == "a":
                    pe.wait_ge(vec_done, V.end("mla_kvq"))
                mla_step(name + "first", 0, s, 0, False)
                with pe.Fori(0, 3) as i:
                    mla_step(name + "loop", i, s + 4, 4, True)
                pe.wait_ge(pool_done, G.end(name + "loop"))
                mla_pv(0)
                pe.wait_ge(vec_done, V.after(name + "last", "on0"))
                mla_pv(1)
                out_layer("mla_out_" + half, hq, lambda k: (vec_done, V.end(name + "last")) if k == 0 else None)
            stats("ffn1", "mla_out_b")
            glu_in("ffn1_in", h, normed("mla_out_b"))
            out_layer("ffn1_out", (act_hi, act_lo), glu("ffn1_in"))

            stats("x2", "ffn1_out")
            stats("nsa", "x2", True)
            s = SLAB_AT["nsa_misc"]
            for n in range(6):
                tile_of("nsa", bank[n][:, :], s + n, h,
                        needs=(lambda k: (vec_done, V.after("x2", f"lo{k}"))) if n == 0 else None)
            pe.wait_ge(act_done, A.end("nsa.stat"))
            for k in range(KD):
                at = SIDE["w_gate"] + k * NGATE
                last = mm3(bank[6][0:NGATE, :], (side_hi[:, at:at + NGATE], side_lo[:, at:at + NGATE]), chunk(h, k),
                           k == 0, k == KD - 1)
            last.then_inc(pe_done, 1)
            for n, kv in enumerate("kv"):
                pe.wait_ge(vec_done, V.after("nsa_misc", "lo" + kv))
                b = [ns[z][n][:, :, :, :].rearrange("p j g n -> p j (g n)") for z in ("b_hi", "b_lo")]
                tile_of("nsa", bank[7 - 7 * n][:, 0:64], s + 6 + 2 * n, b, (KD, KD))
            pe.wait_ge(tables_loaded, 64)
            for n in range(2):
                pe.wait_ge(act_done, A.after("nsa_misc", "gelu_" + "kv"[n]))
                if n == 0:
                    mm(bank[1][:, 0:64], ns["w2"][:, 0:P], ns["gh"][0][:, :, :].rearrange("p g n -> p (g n)"), True, True)\
                        .then_inc(pe_done, 1)
                else:
                    for g in range(2):
                        last = mm(bank[6][0:NCMPCOL, g * DH:(g + 1) * DH], ns["gh"][1][:, g, :],
                                  ns["w2"][:, P:P + DH], True, True)
                    last.then_inc(pe_done, 1)
            ob = (ns["o_hi"], ns["o_lo"])
            for n in range(4):
                if n % 2 == 0:
                    pe.wait_ge(lo_ready, s + 11 + n // 2)
                pe.wait_ge(vec_done, V.after("nsa_misc", f"d_lo{n}"))
                last = mm3(bank[2 + n][:, :], wtile((s + 10 + n // 2) % RING, (n % 2) * P), chunk(ob, 4 + n), True, True)
                if n % 2:
                    last.then_inc(slab_used, 1)
            s = SLAB_AT["nsa_attn"]
            pe.wait_ge(act_done, A.end("nsa_misc"))
            pe.wait_ge(vec_done, V.end("nsa_misc"))
            for g in range(2):
                for n in range(3):
                    tile_of("nsa", bank[4 * g + n][:, :], s + 4 * g + n, h)
                pe.wait_ge(lo_ready, s + 4 * g + 4)
                for t in range(TT):
                    tok = slice(t * P, (t + 1) * P)
                    for k in range(KD):
                        last = mm3(bank[4 * g + 3][:, tok], (h_hi[:, k, tok], h_lo[:, k, tok]),
                                   wtile((s + 4 * g + 3) % RING, k * P), k == 0, k == KD - 1)
                last.then_inc(slab_used, 1)

            def nsa_group(i):
                name = "nsa_attn"
                pe.wait_ge(vec_done, V.after(name, "glo", i))
                pe.wait_ge(act_done, A.after(name, "ghi", i))
                for n in range(6):
                    for z in range(2):
                        last = mm(bank[2 + n][:, :], ns["gsel"][:, n * P:(n + 1) * P],
                                  ns["diag"][z][:, :, :].rearrange("p t n -> p (t n)"), z == 0, z == 1)
                last.then_inc(pe_done, 1)
                pe.wait_ge(vec_done, V.after(name, "q1lo", i))
                for j in range(2):
                    for t in range(TT):
                        tok = slice(t * P, (t + 1) * P)
                        k = [ns[z][:, bass.ds(i, 1), :, :].rearrange("p o h n -> p (o h n)") for z in ("kc_hi", "kc_lo")]
                        at = (j * TT + t) * 2 * NCMPCOL
                        last = mm3(bank[0][:, at:at + 2 * NCMPCOL], (ns["q_hi"][j][:, tok], ns["q_lo"][j][:, tok]), k,
                                   True, True)
                last.then_inc(pe_done, 1)
                pe.wait_ge(vec_done, V.after(name, "cp", i))
                pe.wait_ge(act_done, A.after(name, "g5", i))
                for n in range(4):
                    j, h_ = n // 2, n % 2
                    for t in range(TT):
                        at = ((j * TT + t) * 2 + h_) * NCMPCOL
                        last = mm(bank[2 + n][0:NCMPCOL, t * P:(t + 1) * P], ns["cmp"][:, at:at + NCMPCOL], ident, True, True)
                last.then_inc(pe_done, 1)
                pe.wait_ge(act_done, A.after(name, "pt3", i))
                for j in range(2):
                    for h_ in range(2):
                        last = mm(bank[j][:, :], ns["vcg"][:, h_, :],
                                  ns["prob"][j][0:NCMPCOL, h_ * T:(h_ + 1) * T], h_ == 0, h_ == 1)
                    last.then_inc(pe_done, 1)

                def pv(u, h_):
                    values(bank[h_][:, :], lambda n: ns["v"][:, n, u % 2, h_, :], ns["prob"][h_])\
                        .then_inc(pe_done, 1)

                for u in range(5):
                    j, b = u // 2, u % 2
                    if u:
                        pe.wait_ge(act_done, A.after(name, f"exp1t2.{u - 1}", i))
                        pe.wait_ge(vec_done, V.after(name, f"on1.{u - 1}" if u > 1 else "acc1", i))
                        if u == 1:
                            pe.wait_ge(pool_done, G.after(name, "vz1", i))
                        pv(u - 1, 0)
                    if u < 4:
                        pe.wait_ge(vec_done, V.after(name, f"sel1.{u - u % 2}", i))
                        for h_ in range(2):
                            max_scores(ns, h_, [ns["q_hi"][j]], [ns["k_hi"][b][h_]], ns["table"])
                    if u:
                        pv(u - 1, 1)
                    if u < 4:
                        for h_ in range(2):
                            pe.wait_ge(vec_done, V.after(name, f"dg{h_}.{u}", i))
                            scores(ns, h_, [((ns["k_hi"][b][h_], ns["k_lo"][b][h_]), (ns["q_hi"][j], ns["q_lo"][j]))])

            pe.wait_ge(act_done, A.end("nsa_attn.zero"))
            with pe.Fori(0, 2) as i:
                nsa_group(i)
            out_layer("nsa_out", ob, lambda k: (vec_done, V.end("nsa_attn")) if k == 0 else None)
            stats("sw0", "nsa_out")
            glu_in("sw0_in", h, normed("nsa_out"))
            out_layer("sw0_out", (act_hi, act_lo), glu("sw0_in"))

            stats("pw1", "sw0_out")
            s = SLAB_AT["pw1"]

            def pw1_tiles(c, turn, first=False):
                for n in range(2):
                    if not first:
                        pe.wait_ge(vec_done, V.after("pw1", ("ua", "ug")[n] + str(c), turn) - len(V.steps["pw1"]))
                    tile_of("pw1", bank[2 * c + n][:, :], s + 2 * c + n, h, (KD,), turn, 4,
                            normed("sw0_out") if first and n == 0 else None)

            def pw1_taps(c, turn):
                pe.wait_ge(vec_done, V.after("pw1", f"z{c}", turn))
                pe.wait_ge(act_done, A.after("pw1", f"diag{PE_TAPS - 1}_{c}", turn))
                for k in range(PE_TAPS):
                    t = TAPS - PE_TAPS + k
                    last = mm(bank[4 + c][:, :], cf["diag"][c][:, k, :], cf["z"][c][:, t:t + T], k == 0, k == PE_TAPS - 1)
                last.then_inc(pe_done, 1)

            pw1_tiles(0, 0, True)
            with pe.Fori(0, KD // 2 - 1) as i:
                pw1_tiles(1, i)
                pw1_taps(0, i)
                pw1_tiles(0, i + 1)
                pw1_taps(1, i)
            pw1_tiles(1, KD // 2 - 1)
            pw1_taps(0, KD // 2 - 1)
            pw1_taps(1, KD // 2 - 1)
            pe.wait_ge(pool_done, G.end("pw1"))
            mm(bank[7][:, :], ones[:, :], sq_sum[:, :], True, True).then_inc(pe_done, 1)
            for n in range(KD):
                pe.wait_ge(act_done, A.after("ln", f"sq{n}"))
                mm(bank[7][:, :], ones[:, :], sq[n % 2][:, :], n == 0, n == KD - 1).then_inc(pe_done, 1)
            out_layer("pw2", (cf["o_hi"], cf["o_lo"]), lambda k: (vec_done, V.after("ln", f"lo{k}")))
            stats("sw1", "pw2")
            glu_in("sw1_in", h, normed("pw2"))
            out_layer("sw1_out", (act_hi, act_lo), glu("sw1_in"))
            stats("final", "sw1_out")


OUT = {
    "fox_out": (KD,), "ffn0_out": HID_SPLIT, "mla_out_a": (KD,),
    "mla_out_b": (KD,), "ffn1_out": HID_SPLIT, "nsa_out": (KD,),
    "sw0_out": HID_SPLIT, "pw2": (KD,), "sw1_out": HID_SPLIT,
}


def tiles_in_order(w):
    k, n = w.shape
    return [w[a:a + P, b:b + P] for b in range(0, n, P) for a in range(0, k, P)]


def pack(tiles, per_slab):
    out, at = [], 0
    for n in per_slab:
        slab = np.zeros((P, SLAB), np.float32)
        part = np.concatenate([np.ascontiguousarray(x) for x in tiles[at:at + n]], axis=1)
        slab[:, :part.shape[1]] = part
        out.append(slab)
        at += n
    assert at == len(tiles)
    return out


def interleave(a, b, n=1):
    return [s for i in range(0, len(a), n) for s in a[i:i + n] + b[i:i + n]]


def weight_stream(w):
    ws = {}
    fin = w["w_fox_in"][0]
    v = fin[:, 2048:3072]
    ws["fox_v"] = pack([v[k * P:(k + 1) * P, h * T:(h + 1) * T] for h in range(2) for k in range(KD)], [2] * 8)
    q, k = pack(tiles_in_order(fin[:, 0:1024]), [8] * 8), pack(tiles_in_order(fin[:, 1024:2048]), [8] * 8)
    ws["fox_qk"] = interleave(q, k)
    ws["fox_out"] = pack(tiles_in_order(w["w_fox_out"][0]), [8] * 8)
    ckv, half = w["w_dkv"], ROPE // 2
    x1, x2 = ckv[:, LAT:LAT + half], ckv[:, LAT + half:]
    ws["mla_kvq"] = pack(tiles_in_order(ckv[:, :LAT]) + tiles_in_order(np.concatenate([x1, x1, x2, x2], axis=1))
                         + tiles_in_order(w["w_dq"][0]), [6] * 12)
    uq = w["w_uq"][0].reshape(QLAT, MLA_H, NOPE + ROPE)
    pairs = []
    for p in range(0, MLA_H, 2):
        for h in (p, p + 1):
            pairs += pack(tiles_in_order(uq[:, h, :NOPE]), [KQ])
        rope = [uq[:, h, NOPE + o:NOPE + o + half] for o in (0, half) for h in (p, p + 1)]
        pairs += pack(tiles_in_order(np.concatenate(rope, axis=1)), [KQ])
        v = w["w_uv"][:, p * P:(p + 2) * P]
        pairs += pack(tiles_in_order(w["w_uk"][:, p * P:(p + 2) * P]) + [v[:P], v[P:]], [3 * KL])
    ws["mla_a"], ws["mla_b"] = pairs[:16], pairs[16:]
    o = w["w_mla_out"][0]
    ws["mla_out_a"] = pack(tiles_in_order(o[:D]), [8] * 8)
    ws["mla_out_b"] = pack(tiles_in_order(o[D:]), [8] * 8)
    a = w["nsa_w_in_2"][0]

    def piece(at, n):
        return tiles_in_order(a[:, at:at + n])

    ws["nsa_misc"] = pack(piece(512, 2 * P) + piece(1304, T) + [t for z in "kv" for t in tiles_in_order(w[f"cmp_{z}_w1_2"][0])],
                          [8] * 10) + pack([w["pool_w_2"][0, g] for g in range(4)], [2, 2])
    ws["pw1"] = interleave(pack(tiles_in_order(w["conv_w_pw1_2"][0][:, :D]), [8] * 8),
                           pack(tiles_in_order(w["conv_w_pw1_2"][0][:, D:]), [8] * 8))
    ws["pw2"] = pack(tiles_in_order(w["conv_w_pw2_2"][0]), [8] * 8)
    ws["nsa_attn"] = []
    for g in range(2):
        def both(at):
            return np.concatenate([a[:, at + g * DH:at + (g + 1) * DH], a[:, at + 2 * P + g * DH:at + 2 * P + (g + 1) * DH]], axis=1)
        ws["nsa_attn"] += pack(piece(2 * g * P, 2 * P) + tiles_in_order(both(768)) + tiles_in_order(both(896)), [8] * 4)
    ws["nsa_out"] = pack(tiles_in_order(w["mix_w_out_2"][0]), [8] * 8)
    for n in range(2):
        a = w["w_ffn_in"][n]
        ws[f"ffn{n}_in"] = interleave(pack(tiles_in_order(a[:, :HID]), [8] * KH), pack(tiles_in_order(a[:, HID:]), [8] * KH))
        ws[f"ffn{n}_out"] = pack(tiles_in_order(w["w_ffn_out"][n]), list(HID_SPLIT) * 8)
        a, b = w["ffn_w_gate_2"][n], w["ffn_w_up_2"][n]
        ws[f"sw{n}_in"] = interleave(pack(tiles_in_order(a), [8] * KH), pack(tiles_in_order(b), [8] * KH))
        ws[f"sw{n}_out"] = pack(tiles_in_order(w["ffn_w_down_2"][n]), list(HID_SPLIT) * 8)
    return ws


def by_chunk(a):
    return np.ascontiguousarray(a.reshape(-1, P).T)


def conv_cols(w, b):
    return np.stack([by_chunk(w[0]), by_chunk(w[1]), by_chunk(w[2]), by_chunk(b)], axis=2).reshape(P, -1)


def constants(w):
    cols = np.zeros((P, NCOLS), np.float32)

    def put(name, a):
        cols[:a.shape[0], COLS[name]:COLS[name] + a.shape[1]] = a

    for name, a in [
        ("fox_norm", w["fox_norm"][0]), ("kv_in_norm", w["kv_in_norm"]), ("kv_norm", w["kv_norm"]),
        ("mla_norm", w["mla_norm"][0]), ("q_norm", w["q_norm"][0]), ("ffn_norm0", w["ffn_norm"][0]),
        ("ffn_norm1", w["ffn_norm"][1]), ("final_norm", w["final_norm"]), ("mix_norm0", w["mix_norm_2"][0]),
        ("mix_norm1", w["mix_norm_2"][1]), ("ffn2_norm0", w["ffn_norm_2"][0]), ("ffn2_norm1", w["ffn_norm_2"][1]),
        ("final2", w["final_norm_2"]), ("pool_scale", w["pool_scale_2"][0]), ("b_pw1", w["conv_b_pw1_2"][0]),
        ("b_dw", w["conv_b_dw_2"][0]), ("ln_g", w["conv_ln_g_2"][0]), ("ln_b", w["conv_ln_b_2"][0]),
        ("b_pw2", w["conv_b_pw2_2"][0]),
    ]:
        put(name, by_chunk(a))
    put("b_fox", w["b_fox_f"][0][:, None])
    for n in range(2):
        put(f"conv{n}", conv_cols(w["ffn_conv_w"][n], w["ffn_conv_b"][n]))
    put("w_dw", w["conv_w_dw_2"][0].reshape(TAPS, KD, P).transpose(2, 1, 0).reshape(P, -1))
    put("cmp_pos_k", by_chunk(w["cmp_pos_k_2"][0].reshape(-1)))
    put("cmp_pos_v", by_chunk(w["cmp_pos_v_2"][0].reshape(-1)))
    f = np.arange(P)
    put("rope_pick", np.stack([(f // 32) % 2 == 0, (f // 32) % 2 == 1], axis=1).astype(np.float32))
    slope = 2.0 ** -np.arange(1, NSA_H + 1, dtype=np.float32)
    pos = np.arange(T).reshape(TT, P).T
    a = (pos[:, :, None] * slope).reshape(P, TT, 2, NSA_H // 2).transpose(0, 2, 1, 3)
    put("alibi", a.reshape(P, -1).astype(np.float32))
    tok = np.arange(STRIDE)
    inv = np.concatenate([1.0 / np.minimum(tok + 1, 2 ** (g + 1)) for g in range(4)]).astype(np.float32)
    put("pool_inv", np.tile(inv, (P, 1)))
    put("eps", np.full((P, 1), 1e-6, np.float32))
    put("eps_ln", np.full((P, 1), 1e-5, np.float32))

    mats = np.zeros((P, 3, P), np.float32)
    q, k = np.arange(P)[:, None], np.arange(P)[None, :]
    mats[:, 0] = np.eye(P)
    mats[:, 1] = np.where(k > q, NEG, 0)
    mats[:, 2] = np.where(k >= (q // SEL + 1) * SEL, NEG, 0)
    end = np.arange(NCMPCOL) * STRIDE + CMP - 1
    tok = np.arange(T).reshape(TT, P).T
    hidden = (end[None, None, :] > tok[:, :, None]) | (np.arange(NCMPCOL) >= NCMP)
    tab = np.where(hidden[:, None, :, None, :], NEG, slope.reshape(1, NSA_H // 2, 1, 2, 1) * end).astype(np.float32)
    tab = np.ascontiguousarray(tab.reshape(P, -1))

    pos = np.arange(T, dtype=np.float32)
    inv = (10000.0 ** (-np.arange(0, ROPE, 2, dtype=np.float32) / ROPE)).astype(np.float32)
    ang = inv[:, None] * pos[None, :]
    cos, sin = np.cos(ang).astype(np.float32), np.sin(ang).astype(np.float32)
    rows = np.zeros((P, 3, T), np.float32)
    rows[:, 0, :T] = np.concatenate([cos] * 4)
    rows[:, 1, :T] = np.concatenate([-sin, -sin, sin, sin])
    rows[:NSA_H, 2, :] = slope[:, None] * np.arange(T)[None, :]
    return cols, mats, rows, tab


def side_weights(w):
    side = np.zeros((P, NSIDE), np.float32)

    def put(name, a):
        side[:, SIDE[name]:SIDE[name] + a.shape[1]] = a

    f = w["w_fox_in"][0][:, 3072:]
    put("w_f", f.reshape(KD, P, FOX_H).transpose(1, 0, 2).reshape(P, -1))
    g = w["nsa_w_in_2"][0][:, 1280:1304]
    put("w_gate", g.reshape(KD, P, 24).transpose(1, 0, 2).reshape(P, -1))
    side[:, SIDE["w2"]:SIDE["w2"] + P + DH] = np.concatenate([w["cmp_k_w2_2"][0]] * 2 + [w["cmp_v_w2_2"][0]], axis=1)
    return side


def kernel(**inputs):
    import concourse.bacc as bacc
    from concourse.bass_utils import run_bass_kernel_spmd

    w = {k: np.asarray(v) for k, v in inputs.items()}
    arrays = layout(w)
    nc = bacc.Bacc("TRN2", target_bir_lowering=False, num_devices=1)
    aps = [nc.dram_tensor(n, a.shape, F, kind="ExternalInput").ap() for n, a in arrays.items()]
    out = nc.dram_tensor("out_t", (P, KD, T), F, kind="ExternalOutput").ap()
    build(nc, *aps, out)
    r = run_bass_kernel_spmd(nc, [arrays], core_ids=[0])
    y = r.results[0]["out_t"]
    return np.ascontiguousarray(y.transpose(2, 1, 0).reshape(1, T, D))


def layout(w):
    ws = weight_stream(w)
    stream = np.zeros((NSLABS, P, SLAB), np.float32)
    for name, slabs in ws.items():
        assert len(slabs) == dict(SLABS)[name], (name, len(slabs))
        for n, slab in enumerate(slabs):
            stream[SLAB_AT[name] + n] = slab
    cols, mats, rows, tab = constants(w)
    xt = np.ascontiguousarray(w["x"][0].reshape(T, KD, P).transpose(2, 1, 0))
    return {"stream_dram": stream, "x_dram": xt, "cols_dram": cols, "mats_dram": mats,
            "side_dram": side_weights(w), "rows_dram": rows, "tab_dram": tab}
```

```python
from contextlib import ExitStack

import numpy as np

import concourse.bass as bass
from concourse import mybir

F = mybir.dt.float32
R = mybir.dt.float32r
ALU = mybir.AluOpType
ACT = mybir.ActivationFunctionType
AX = mybir.AxisListType.X

P = 128
T = 512
TT = T // P
D = 1024
KD = D // P
SLAB = KD * P
RAW = 2
RING = 4
HID = 2816
KH = HID // P
FOX_H, DH = 16, 64
FOX_PAIRS = FOX_H // 2
MLA_H, NOPE, ROPE, LAT, QLAT = 16, 128, 64, 256, 768
KL, KQ = LAT // P, QLAT // P
NSA_H = 8
CMP, STRIDE, SEL = 32, 16, 64
NCMP = T // STRIDE - 1
TAPS = 31
PE_TAPS = 14
EPS = 1e-6
NEG = -1e30

SLABS = [
    ("fox_v", 8), ("fox_qk", 16), ("fox_out", 8), ("ffn0_in", 44), ("ffn0_out", 24),
    ("mla_kvq", 12), ("mla_a", 16), ("mla_out_a", 8), ("mla_b", 16), ("mla_out_b", 8),
    ("ffn1_in", 44), ("ffn1_out", 24),
    ("nsa_in", 6), ("nsa_proj", 8), ("nsa_cmp", 6), ("nsa_out", 8), ("sw0_in", 44), ("sw0_out", 24),
    ("pw1", 16), ("pw2", 8), ("sw1_in", 44), ("sw1_out", 24),
]
SLAB_AT = {}
NSLABS = 0
for _name, _n in SLABS:
    SLAB_AT[_name] = NSLABS
    NSLABS += _n

HID_SPLIT = (8, 7, 7)

COLS = {}
NCOLS = 0
for _name, _n in [
    ("fox_norm", KD), ("kv_in_norm", KD), ("kv_norm", KL), ("mla_norm", KD), ("q_norm", KQ),
    ("ffn_norm0", KD), ("ffn_norm1", KD), ("final_norm", KD), ("b_fox", 1), ("rope_pick", 2),
    ("mix_norm0", KD), ("mix_norm1", KD), ("ffn2_norm0", KD), ("ffn2_norm1", KD), ("final2", KD),
    ("pool_scale", 4), ("b_pw1", 2 * KD), ("b_dw", KD), ("ln_g", KD), ("ln_b", KD), ("b_pw2", KD),
    ("w_dw", TAPS * KD), ("conv0", 4 * 2 * KH), ("conv1", 4 * 2 * KH), ("alibi", TT * NSA_H),
    ("pool_inv", 4 * STRIDE), ("eps", 1), ("eps_ln", 1), ("cmp_pos_k", 16), ("cmp_pos_v", 16),
]:
    COLS[_name] = NCOLS
    NCOLS += _n

SIDE = {"w_f": 0, "w_gate": 128, "w2": 320}
NSIDE = 512
NGATE = 3 * NSA_H
NCMPCOL = 32
NCMPTAB = NSA_H * TT * NCMPCOL


class Plan:

    def __init__(self):
        self.base, self.steps, self.reps, self.total = {}, {}, {}, 0

    def stage(self, name, steps, reps=1):
        assert name not in self.base and len(set(steps)) == len(steps), name
        self.base[name], self.steps[name], self.reps[name] = self.total, list(steps), reps
        self.total += len(steps) * reps

    def after(self, name, step, turn=0):
        return turn * len(self.steps[name]) + (self.base[name] + self.steps[name].index(step) + 1)

    def before(self, name):
        return self.base[name]

    def end(self, name):
        return self.base[name] + len(self.steps[name]) * self.reps[name]


SLOT = ((2, 3, 4), (5, 6, 7))
MAX_TILES = [(2, 1, 0), (0, 1, 384), (3, 0, 0), (1, 2, 0)]
SCORE_TILES = [(1, 1, 0), (3, 1, 384), (0, 0, 0), (2, 2, 0)]
PROB_AT = [0, 512, 896, 1152]
NPROB = 1280
MAX_STEPS = ["mx1", "mx0", "mx2"]


def attn_pe(h):
    return [f"max{h}b1", f"max{h}b0", f"max{h}b2"]


def score_pe(h):
    return [f"sc{h}b1", f"sc{h}b0", f"sc{h}b2"]


def max_vec(h):
    return [f"mx{h}t{n}" for n, _, _ in MAX_TILES] + [f"dg{h}"]


def exp_act(h):
    return [f"exp{h}t{n}" for n, _, _ in SCORE_TILES]


def make_plans():
    act, vec, pool, pe = Plan(), Plan(), Plan(), Plan()

    def norm_stats(name, cols=False):
        pe.stage(name + ".stat", ["sum"] + (["cols"] if cols else []))
        act.stage(name + ".stat", ["root"] + (["root_cols"] if cols else []))
        vec.stage(name + ".stat", ["rstd"] + (["rstd_cols"] if cols else []))

    def units(name, reps, n, full=True, second=False):
        if second:
            act.stage(name, [f"{s}{c}" for c in range(n) for s in ("hi", "sq", "sg")], reps)
            vec.stage(name, [f"{s}{c}" for c in range(n) for s in ("x", "lo")], reps)
            pool.stage(name, [f"{s}{c}" for c in range(n) for s in ("acc", "acg")], reps)
            return
        act.stage(name, [f"{s}{c}" for c in range(n) for s in (["hi", "sq"] if full else ["sq"])], reps)
        vec.stage(name, [f"{s}{c}" for c in range(n) for s in (["x", "lo"] if full else ["x"])], reps)
        pool.stage(name, [f"acc{c}" for c in range(n)], reps)

    def out_layer(name, full=True):
        pool.stage(name + ".zero", ["zero"])
        pe.stage(name, [], 2)
        units(name, 2, 4, full)

    def glu_in(name, conv):
        pe.stage(name, [], KH // 2)
        a = ["tapg", "tapv", "silu", "hi"] if conv else ["silu", "hi"]
        v = ["ug", "uv", "c1g", "c1v", "c2g", "c2v", "mul", "lo"] if conv else ["ug", "uv", "mul", "lo"]
        act.stage(name, [f"{s}{c}" for c in range(2) for s in a], KH // 2)
        vec.stage(name, [f"{s}{c}" for c in range(2) for s in v], KH // 2)

    pool.stage("init", ["ones", "ones_r", "zero_negc"])
    pool.stage("x_in.zero", ["zero"])
    act.stage("x_in", [f"{s}{c}" for c in range(KD) for s in ("hi", "sq")])
    vec.stage("x_in", [f"lo{c}" for c in range(KD)])
    act.stage("init", ["ident", "mask0", "mask1", "side"])
    vec.stage("init", ["side", "gains"])
    pool.stage("x_in", [f"acc{c}" for c in range(KD)])

    norm_stats("fox", cols=True)
    pe.stage("fox_v", ["f", "negc_cols"])
    act.stage("fox_v", [f"v{h}t{t}" for h in range(2) for t in range(TT)] + ["e", "ln"])
    vec.stage("fox_v", ["z0", "z", "na", "logf", "scan", "negc_r"])
    pool.stage("fox_v", ["vones", "ones_row", "zk0l", "zk1l", "zk0h", "zk1h"])
    v_proj = ["qt", "qlo", "sel0", "sel1", "kt", "klo0", "klo1"]
    a_proj = ["qhi", "khi0", "khi1"]
    v_max = max_vec(0) + max_vec(1)
    v_norm = ["rc", "on0", "on1", "olo"]
    pe_max = attn_pe(0) + attn_pe(1)
    pe_sc = score_pe(0) + score_pe(1)
    pe_body = ["pv0"] + pe_max + ["pv1"] + pe_sc
    pe.stage("fox_first", pe_max + pe_sc)
    act.stage("fox_first", a_proj + exp_act(0) + exp_act(1))
    vec.stage("fox_first", v_proj)
    vec.stage("fox_cols", ["negc_cols"])
    vec.stage("fox_first_max", v_max)
    pool.stage("fox_first", ["vp0", "vp1"])

    def twice(steps):
        return [f"{s}.{c}" for c in range(2) for s in steps]

    for name, reps, two in (("fox_loop", 3, twice), ("fox_peel", 1, lambda s: [f"{x}.0" for x in s])):
        pe.stage(name, two(pe_body), reps)
        act.stage(name, two(a_proj + ["s0", "s1"] + exp_act(0) + exp_act(1) + ["ohi"]), reps)
        vec.stage(name, two(v_proj + v_max + v_norm), reps)
        pool.stage(name, two(["vp0", "vp1"]), reps)
    pe.stage("fox_last", ["pv0", "pv1"])
    act.stage("fox_last", ["s0", "s1", "ohi"])
    vec.stage("fox_last", v_norm)
    out_layer("fox_out")

    norm_stats("ffn0")
    pool.stage("pad0", ["pad0", "pad1"])
    glu_in("ffn0_in", True)
    out_layer("ffn0_out")

    pe.stage("mla_t0", ["t0"])
    norm_stats("mla")
    pe.stage("mla_kvq", ["t1", "lat_sum", "t3", "t4", "q_sum0", "q_sum1", "t6", "q_sum2", "t7", "q_sum3", "q_sum4", "q_sum5"])
    act.stage("mla_kvq", [f"h_hi{n}" for n in range(KD)] + ["sq_l0", "sq_l1", "kr_hi0", "kr_hi1", "root_l", "hi_l0", "hi_l1"]
              + [f"{s}{j}" for j in range(KQ) for s in ("q_hi", "q_sq")] + ["root_q"])
    vec.stage("mla_kvq", [f"h_lo{n}" for n in range(KD)] + ["l0", "l1", "kra", "krb0", "krb1", "krs", "krn", "kr_lo0", "kr_lo1",
              "rstd_l", "ln0", "ln1", "lo_l0", "lo_l1"] + [f"{s}{j}" for j in range(KQ) for s in ("q", "q_lo")]
              + ["rstd_q", "cos_q", "sin_q"])
    m_pe = attn_pe(0) + attn_pe(1)
    m_v = ["n0", "n0lo", "n1", "n1lo", "ra", "rb0", "rb1", "rs", "rlo", "k0lo", "k1lo"]
    m_a = ["n0hi", "n1hi", "rhi", "k0hi", "k1hi"]
    m_sum = [f"s{h}{c}" for h in range(2) for c in "abcd"]
    for half in "ab":
        n = "mla_" + half
        pe.stage(n + "_first", ["k0", "k1"] + m_pe + pe_sc)
        act.stage(n + "_first", m_a + exp_act(0) + exp_act(1) + ["v0", "v1"])
        vec.stage(n + "_first", m_v + max_vec(0) + max_vec(1))
        pool.stage(n + "_first", m_sum)
        pe.stage(n + "_loop", ["k0", "k1", "pv0", "sum0"] + m_pe + ["pv1", "sum1"] + pe_sc, 3)
        act.stage(n + "_loop", m_a + ["ohi0"] + exp_act(0) + exp_act(1) + ["ohi1", "v0", "v1"], 3)
        vec.stage(n + "_loop", m_v + ["rc0", "on0"] + max_vec(0) + ["olo0"] + max_vec(1) + ["rc1", "on1", "olo1"], 3)
        pool.stage(n + "_loop", m_sum, 3)
        pe.stage(n + "_last", ["pv0", "sum0", "pv1", "sum1"])
        act.stage(n + "_last", ["ohi0", "ohi1"])
        vec.stage(n + "_last", ["rc0", "on0", "olo0", "rc1", "on1", "olo1"])
        if half == "a":
            vec.stage("mla_out_a", [f"x{c}" for c in range(4)], 2)
        else:
            out_layer("mla_out_b")

    norm_stats("ffn1")
    pool.stage("pad1", ["pad0", "pad1"])
    glu_in("ffn1_in", True)
    pool.stage("ffn1_out.zero", ["zero", "zero_g"])
    pe.stage("ffn1_out", [], 2)
    units("ffn1_out", 2, 4, second=True)

    pe.stage("x2", ["sum", "sum_g"])
    act.stage("x2", ["root", "root2"])
    vec.stage("x2", ["r1", "r1sq", "ms", "r2", "rstd"] + [f"x{n}" for n in range(KD)])

    pool.stage("nsa_in", ["pad0", "pad1", "pad2", "pad3", "pad4", "pad5", "pad6", "gates0"])
    pe.stage("nsa_in", ["gate", "cols"])
    act.stage("nsa_in", ["hik", "hiv"] + [f"d_hi{g}" for g in range(4)] + ["sig"])
    vec.stage("nsa_in", [f"bk{g}{h}" for g in range(2) for h in range(2)]
              + [f"blk{g}{h}" for g in range(2) for h in range(2)] + ["lok"]
              + [f"bv{g}{h}" for g in range(2) for h in range(2)]
              + [f"blv{g}{h}" for g in range(2) for h in range(2)] + ["lov"]
              + [f"{z}{g}" for g in range(4) for z in ["u"] + [f"sum{n}_" for n in range(g + 1)] + ["d", "early", "first", "d_lo"]]
              + ["gz", "cols"])
    act.stage("nsa_cmp.table", ["table"])
    act.stage("nsa_proj", [f"v{t}" for t in range(TT)])
    pe.stage("nsa_cmp", ["kcmp", "vcmp"])
    act.stage("nsa_cmp", ["gelu_k", "gelu_v"] + [f"p_hi{g}" for g in range(4)] + ["kc0", "kc1", "vc0", "vc1"])
    vec.stage("nsa_proj", [f"q{n}" for n in range(4)] + [f"k{g}{b}{h}" for g in range(2) for b in range(2) for h in range(2)])
    vec.stage("nsa_cmp", [f"p_lo{g}" for g in range(4)] + ["kcl0", "kcl1"])
    pool.stage("nsa_attn.zero", [f"k{n}" for n in range(8)] + ["vones"])
    def unit(steps, u):
        return [f"{z}.{u}" for z in steps]

    act.stage("nsa_gates", ["ghi"])
    vec.stage("nsa_gates", ["glo"])
    pe.stage("nsa_attn", ["g", "cs"] + unit(pe_max + pe_sc, 0) + ["tr", "cpv0", "cpv1"]
             + [z for u in range(1, 4) for z in unit(["pv0"] + pe_max + ["pv1"] + pe_sc, u)] + ["pv0.4", "pv1.4"], 2)
    a = ["bias", "vcg", "q0hi", "q1hi", "khi00", "khi01"] + [f"g{n}" for n in range(6)] + ["khi10", "khi11", "cexp"]
    for u in range(4):
        a += unit((["s0", "s1"] if u else []) + exp_act(0) + exp_act(1), u)
        if u == 0:
            a += ["pt0", "pt1"]
        if u == 2:
            a += ["ohi0"]
    act.stage("nsa_attn", a + ["s0.4", "s1.4", "ohi1"], 2)
    v = ["gs0", "gs1", "q0lo", "q1lo", "klo00", "klo01", "sel0.0", "sel1.0", "cs", "cm", "cmin", "csub", "klo10", "klo11",
         "csum", "cmax", "crec", "cp"]
    for u in range(4):
        v += unit((["sel0", "sel1"] if u == 2 else []) + max_vec(0) + max_vec(1), u)
        if u == 0:
            v += ["acc0", "acc1"]
        if u:
            v += unit(["rc", "on0", "on1"], u)
        if u == 3:
            v += ["olo0"]
    vec.stage("nsa_attn", v + unit(["rc", "on0", "on1"], 4) + ["olo1"], 2)
    pool.stage("nsa_attn", ["vz0", "vz1"] + [f"{z}.{u}" for u in range(4) for z in ("gm", "ga")], 2)
    out_layer("nsa_out")
    norm_stats("sw0")
    glu_in("sw0_in", False)
    out_layer("sw0_out")

    norm_stats("pw1")
    pool.stage("pw1.zero", ["zero"] + [f"zpad{z}{c}" for c in range(2) for z in range(3)])
    pe.stage("pw1", ["y0", "y1"], KD // 2)
    act.stage("pw1", [f"{s}{c}" for c in range(2) for s in ["w", "wh", "sg", "zh", "t"]], KD // 2)
    vec.stage("pw1", [f"{s}{c}" for c in range(2) for s in ["ua", "ug", "wl", "z", "zl"]
                      + [f"t{k}_" for k in range(1, TAPS - PE_TAPS)] + ["y"]], KD // 2)
    pool.stage("pw1", [f"{s}{c}" for c in range(2) for s in ("dh", "dl", "acc")], KD // 2)
    pe.stage("ln", ["mean"] + [f"v{n}" for n in range(KD)])
    act.stage("ln", ["mean"] + [f"sq{n}" for n in range(KD)] + ["root"] + [f"{s}{n}" for n in range(KD) for s in ("s", "hi")])
    vec.stage("ln", [f"xc{n}" for n in range(KD)] + ["rstd", "yn0"] + [z for n in range(1, KD) for z in (f"yn{n}", f"lo{n - 1}")] + [f"lo{KD - 1}"])
    out_layer("pw2")
    norm_stats("sw1")
    glu_in("sw1_in", False)
    out_layer("sw1_out", False)
    norm_stats("final")
    vec.stage("final", [f"y{n}" for n in range(KD)])
    return act, vec, pool, pe


def build(nc, stream, xt_dram, cols_dram, mats_dram, side_dram, rows_dram, tab_dram, out_dram):
    ctx = ExitStack()
    with ctx:
        def sb(name, shape, dt=F, scope=ctx):
            return scope.enter_context(nc.sbuf_tensor(name, shape, dt))

        def sem(name):
            return ctx.enter_context(nc.semaphore(name))

        A, V, G, M = make_plans()

        x = sb("x", [P, KD, T])
        raw = [sb(f"raw{n}", [P, SLAB]) for n in range(RAW)]
        w_hi = [sb(f"w_hi{n}", [P, SLAB], R) for n in range(RING)]
        w_lo = [sb(f"w_lo{n}", [P, SLAB], R) for n in range(RING)]
        rstd = sb("rstd", [P, T])
        root = sb("root", [P, T])
        rstd_col = sb("rstd_col", [P, TT])
        root_col = sb("root_col", [P, TT])
        sq = [sb(f"sq{n}", [P, T]) for n in range(2)]
        sq_sum = sb("sq_sum", [P, T])
        cols = sb("cols", [P, NCOLS])
        mats = sb("mats", [P, 3, P])
        gains = sb("gains", [P, KD])
        ident = mats[:, 0, :]
        ident_r = sb("ident_r", [P, P], R)
        mask_r = [sb(f"mask_r{n}", [P, P], R) for n in range(2)]
        ones = sb("ones", [P, P])
        ones_r = sb("ones_r", [P, P], R)
        side_raw = root
        side_hi = sb("side_hi", [P, NSIDE], R)
        side_lo = sb("side_lo", [P, NSIDE], R)
        h_scope = ctx.enter_context(ExitStack())
        h_hi = sb("h_hi", [P, KD, T], R, h_scope)
        h_lo = sb("h_lo", [P, KD, T], R, h_scope)

        with ExitStack() as fox:
            o_hi = sb("fox_o_hi", [P, KD, T], R, fox)
            o_lo = sb("fox_o_lo", [P, KD, T], R, fox)
            fx = dict(
                v=sb("fox_v", [P, TT, D], F, fox),
                q_raw=sb("fox_q_raw", [P, T], F, fox), k_raw=sb("fox_k_raw", [P, T], F, fox),
                q_hi=sb("fox_q_hi", [P, T], R, fox), q_lo=sb("fox_q_lo", [P, T], R, fox),
                k_hi=[sb(f"fox_k_hi{h}", [P, T], R, fox) for h in range(2)],
                k_lo=[sb(f"fox_k_lo{h}", [P, T], R, fox) for h in range(2)],
                vp=sb("fox_vp", [P, TT, 2, P], F, fox),
                prob=[sb(f"fox_prob{h}", [P, NPROB], F, fox) for h in range(2)],
                diag=[sb(f"fox_diag{h}", [P, TT, P], R, fox) for h in range(2)],
                sel=[sb(f"fox_sel{h}", [P, P], R, fox) for h in range(2)],
                negm=[sb(f"fox_negm{h}", [P, TT], F, fox) for h in range(2)],
                rec=sb("fox_rec", [P, T], F, fox), o=sb("fox_o", [P, T], F, fox),
                negc=sb("fox_negc", [P, T], F, fox), negc_r=sb("fox_negc_r", [P, T], R, fox),
                negc_col=sb("fox_negc_col", [P, TT, FOX_H], F, fox),
            )
            fx.update(z=fx["rec"], ones_row=fx["o"], na=fx["prob"][0])
            fox_o = (o_hi, o_lo)
        with ExitStack() as ffn:
            act_hi = sb("glu_hi", [P, KH, T], R, ffn)
            act_lo = sb("glu_lo", [P, KH, T], R, ffn)
            u = [sb(f"glu_u{n}", [P, T + 2], F, ffn) for n in range(2)]
            tap = [sb(f"glu_tap{n}", [P, T], F, ffn) for n in range(2)]

        h_scope.close()
        with ExitStack() as mla:
            ml = dict(
                qn_hi=[sb(f"mla_qn_hi{h}", [P, T], R, mla) for h in range(2)],
                qn_lo=[sb(f"mla_qn_lo{h}", [P, T], R, mla) for h in range(2)],
                qr_hi=sb("mla_qr_hi", [P, T], R, mla), qr_lo=sb("mla_qr_lo", [P, T], R, mla),
                v=sb("mla_v", [P, TT, 2, P], F, mla),
                q_raw=sb("mla_q_raw", [P, T], F, mla), rot=sb("mla_rot", [P, T], F, mla),
                rec=sb("mla_rec", [P, T], F, mla), o=sb("mla_o", [P, T], F, mla),
                psum=[sb(f"mla_psum{h}", [P, T], F, mla) for h in range(2)],
                k_hi=[sb(f"mla_k_hi{h}", [P, T], R, mla) for h in range(2)],
            )
            ml["o_hi"] = sb("mla_o_hi", [P, KD, T], R, mla)
            ml["o_lo"] = sb("mla_o_lo", [P, KD, T], R, mla)
            ml.update(
                ql_hi=sb("mla_ql_hi", [P, KQ, T], R, mla), ql_lo=sb("mla_ql_lo", [P, KQ, T], R, mla),
                l_hi=sb("mla_l_hi", [P, KL, T], R, mla), l_lo=sb("mla_l_lo", [P, KL, T], R, mla),
                kr_hi=[sb(f"mla_kr_hi{h}", [P, T], R, mla) for h in range(2)],
                kr_lo=[sb(f"mla_kr_lo{h}", [P, T], R, mla) for h in range(2)],
                k_lo=[sb(f"mla_k_lo{h}", [P, T], R, mla) for h in range(2)],
                cos=sb("mla_cos", [P, T], F, mla), sin=sb("mla_sin", [P, T], F, mla),
                prob=[sb(f"mla_prob{h}", [P, NPROB], F, mla) for h in range(2)],
                diag=[sb(f"mla_diag{h}", [P, TT, P], R, mla) for h in range(2)],
                negm=[sb(f"mla_negm{h}", [P, TT], F, mla) for h in range(2)],
            )

        with ExitStack() as nsa:
            sb("nsa_under", [P, 2 * KD * T], F, nsa)
            ns = dict(
                o_hi=sb("nsa_o_hi", [P, KD, T], R, nsa), o_lo=sb("nsa_o_lo", [P, KD, T], R, nsa),
                q_raw=sb("nsa_q_raw", [P, NSA_H // 2, T], F, nsa),
                k_raw=sb("nsa_k_raw", [P, 2, 2, T], F, nsa),
                v_raw=sb("nsa_v_raw", [P, TT, 2, P], F, nsa),
                kc_hi=sb("nsa_kc_hi", [P, 2, 2, NCMPCOL], R, nsa),
                kc_lo=sb("nsa_kc_lo", [P, 2, 2, NCMPCOL], R, nsa),
                vc=sb("nsa_vc", [2 * NCMPCOL, 2, P], F, nsa),
                w2=sb("nsa_w2", [P, P + DH], F, nsa),
                tab=sb("nsa_tab", [P, 2, 2 * 2 * TT * NCMPCOL], F, nsa),
                table=sb("nsa_table", [P, T], R, nsa),
                gates=sq_sum, cmp=root, rec=sq[0], o=sq[1],
            )
            misc = nsa.enter_context(ExitStack())
            ns.update(
                bk=sb("nsa_bk", [P, 2, T + STRIDE], F, misc), blk=sb("nsa_blk", [P, 16, 2, NCMPCOL], F, misc),
                b_hi=[sb(f"nsa_b_hi{n}", [P, 16, 2, NCMPCOL], R, misc) for n in range(2)],
                b_lo=[sb(f"nsa_b_lo{n}", [P, 16, 2, NCMPCOL], R, misc) for n in range(2)],
                run=[sb(f"nsa_run{n}", [P, STRIDE + T], F, misc) for n in range(3)],
                gh=[sb(f"nsa_gh{n}", [P, 2, NCMPCOL], F, misc) for n in range(2)],
            )
            misc.close()
            ns.update(
                prob=[sb(f"nsa_prob{h}", [P, NPROB], F, nsa) for h in range(2)],
                sel=[sb(f"nsa_sel{h}", [P, P], R, nsa) for h in range(2)],
                negm=[sb(f"nsa_negm{h}", [P, TT], F, nsa) for h in range(2)],
                bias=sb("nsa_bias", [P, TT * NSA_H // 2], F, nsa),
                cmp_m=sb("nsa_cmp_m", [P, 16], F, nsa),
                q_lo=[sb(f"nsa_q_lo{j}", [P, T], R, nsa) for j in range(2)],
                gsel=sb("nsa_gsel", [P, 6 * P], R, nsa),
                g_hi=sb("nsa_g_hi", [P, T], R, nsa), g_lo=sb("nsa_g_lo", [P, T], R, nsa),
                pt=sb("nsa_pt", [2 * NCMPCOL, T], F, nsa),
                g=sb("nsa_g", [P, 6, T], F, nsa), vcg=sb("nsa_vcg", [2 * NCMPCOL, P], F, nsa),
            )
        with ExitStack() as nsa2:
            ns.update(
                k_hi=[[sb(f"nsa_k_hi{b}{h}", [P, T], R, nsa2) for h in range(2)] for b in range(2)],
                k_lo=[[sb(f"nsa_k_lo{b}{h}", [P, T], R, nsa2) for h in range(2)] for b in range(2)],
                v=sb("nsa_v", [P, TT, 2, 2, P], F, nsa2),
                diag=[sb(f"nsa_diag{h}", [P, TT, P], R, nsa2) for h in range(2)],
                q_hi=[sb(f"nsa_q_hi{j}", [P, T], R, nsa2) for j in range(2)],
            )

        with ExitStack() as conf:
            sb("conf_under", [P, 2 * KD * T], F, conf)
            cf = dict(
                o_hi=sb("conf_o_hi", [P, KD, T], R, conf), o_lo=sb("conf_o_lo", [P, KD, T], R, conf),
                y=sb("conf_y", [P, KD, T], F, conf),
                a=sb("conf_a", [P, T], F, conf), gate=sb("conf_gate", [P, T], F, conf),
                z=[sb(f"conf_z{c}", [P, TAPS - 1 + T], F, conf) for c in range(2)],
                acc=[sb(f"conf_acc{c}", [P, T], F, conf) for c in range(2)],
                w=[sb(f"conf_w{c}", [P, TAPS], F, conf) for c in range(2)],
                w_hi=[sb(f"conf_w_hi{c}", [P, TAPS + 1], R, conf) for c in range(2)],
                w_lo=[sb(f"conf_w_lo{c}", [P, TAPS + 1], F, conf) for c in range(2)],
                z_hi=[sb(f"conf_z_hi{c}", [P, TAPS - 1 + T], R, conf) for c in range(2)],
                z_lo=[sb(f"conf_z_lo{c}", [P, TAPS - 1 + T], R, conf) for c in range(2)],
                diag=[[sb(f"conf_diag{z}{c}", [P, PE_TAPS, P], R, conf) for z in "hl"] for c in range(2)],
            )

        turned = [ns["cmp"][0:2 * NCMPCOL, :], ns["pt"][:, :]]

        bank = [ctx.enter_context(nc.psum_tensor(f"bank{n}", [P, T], F)) for n in range(8)]

        const_loaded = sem("const_loaded")
        gain_loaded = sem("gain_loaded")
        x_loaded = [sem(f"x_loaded{n}") for n in range(KD)]
        raw_loaded = [sem(f"raw_loaded{n}") for n in range(RAW)]
        hi_ready = sem("hi_ready")
        lo_ready = sem("lo_ready")
        slab_used = sem("slab_used")
        act_done = sem("act_done")
        vec_done = sem("vec_done")
        pool_done = sem("pool_done")
        pe_done = sem("pe_done")
        out_stored = sem("out_stored")
        tables_loaded = sem("tables_loaded")

        def kvq_slabs(t):
            return KD * (t + 1) // 6

        def kvq_done(t):
            if KD * (t + 1) % 6 == 0:
                return slab_used, SLAB_AT["mla_kvq"] + kvq_slabs(t)
            return pe_done, M.after("mla_kvq" if t else "mla_t0", f"t{t}")

        POOL_BANK = (0, 4, 5, 6)
        KVQ_BANK = (0, 1, 2, 3, 4, 5, 6, 0, 1)

        def col(name, n=0, count=1):
            if name == "gains":
                return gains[:, bass.ds(n, count)]
            return cols[:, bass.ds(COLS[name] + n, count)]

        block = ctx.enter_context(nc.Block())

        @block.sync
        def _(sp):
            sp.dma_start(cols[:, 0:KD], cols_dram[:, 0:KD]).then_inc(gain_loaded, 16)
            for n in range(KD):
                sp.dma_start(x[:, n, :], xt_dram[:, n, :]).then_inc(x_loaded[n], 16)
                if n < RAW:
                    sp.dma_start(raw[n][:, :], stream[n, :, :]).then_inc(raw_loaded[n], 16)
            sp.dma_start(mats[:, :, :], mats_dram).then_inc(const_loaded, 16)
            sp.dma_start(side_raw[:, :], side_dram).then_inc(const_loaded, 16)
            sp.dma_start(cols[:, KD:], cols_dram[:, KD:]).then_inc(const_loaded, 16)
            last = NSLABS
            with sp.Fori(1, last // RAW) as i:
                for n in range(RAW):
                    sp.wait_ge(lo_ready, RAW * i + (n - RAW + 1))
                    sp.dma_start(raw[n][:, :], stream[bass.ds(RAW * i + n, 1), :, :].rearrange("a p n -> (a p) n"))\
                        .then_inc(raw_loaded[n], 16)
            for n in range(0, KD, 2):
                sp.wait_ge(vec_done, V.after("final", f"y{n + 1}"))
                sp.dma_start(out_dram[:, n:n + 2, :], x[:, n:n + 2, :]).then_inc(out_stored, 16)
            sp.wait_ge(out_stored, 16 * KD // 2)

        @block.gpsimd
        def _(pool):
            order = [0]

            def own(plan_stage, step, turn=0):
                n = G.after(plan_stage, step, turn) - 1
                if isinstance(n, int) and n == 0:
                    return
                pool.wait_ge(pool_done, n)

            def zero_sum(name, read):
                own(name + ".zero", "zero")
                if read:
                    pool.wait_ge(pe_done, M.end(read + ".stat"))
                nc.gpsimd.memset(sq_sum[:, :], 0.0).then_inc(pool_done, 1)

            def sum_squares(name, n, turn=0):
                for c in range(n):
                    own(name, f"acc{c}", turn)
                    pool.wait_ge(act_done, A.after(name, f"sq{c}", turn))
                    nc.gpsimd.tensor_tensor(sq_sum[:, :], sq_sum[:, :], sq[c % 2][:, :], ALU.add)\
                        .then_inc(pool_done, 1)

            def out_layer(name, read):
                zero_sum(name, read)
                with pool.Fori(0, 2) as i:
                    sum_squares(name, 4, i)

            own("init", "ones")
            nc.gpsimd.memset(ones[:, :], 1.0).then_inc(pool_done, 1)
            own("init", "ones_r")
            nc.gpsimd.memset(ones_r[:, :].bitcast(F), 1.0).then_inc(pool_done, 1)
            own("init", "zero_negc")
            nc.gpsimd.memset(fx["negc_r"][:, :].bitcast(F), 0.0).then_inc(pool_done, 1)
            zero_sum("x_in", None)
            sum_squares("x_in", KD)

            own("fox_v", "vones")
            nc.gpsimd.memset(fx["vp"][:, :, :, :], 1.0).then_inc(pool_done, 1)
            own("fox_v", "ones_row")
            nc.gpsimd.memset(fx["ones_row"][:, :], 1.0).then_inc(pool_done, 1)
            for name, buf, lo in (("zk0l", fx["k_lo"][0], 64), ("zk1l", fx["k_lo"][1], 0),
                                  ("zk0h", fx["k_hi"][0], 64), ("zk1h", fx["k_hi"][1], 0)):
                own("fox_v", name)
                nc.gpsimd.memset(buf[lo:lo + 64, :].bitcast(F), 0.0).then_inc(pool_done, 1)

            def fox_values(name, sfx, turn, pair):
                for h in range(2):
                    own(name, f"vp{h}{sfx}", turn)
                    src = fx["v"][:, :, bass.ds(pair * P + h * DH, DH)]
                    nc.gpsimd.tensor_copy(fx["vp"][:, :, h, h * DH:(h + 1) * DH], src).then_inc(pool_done, 1)

            pool.wait_ge(act_done, A.after("fox_v", f"v1t{TT - 1}"))
            fox_values("fox_first", "", 0, 0)
            with pool.Fori(0, 3) as i:
                for c in range(2):
                    pool.wait_ge(pe_done, M.after("fox_loop", f"pv1.{c}", i))
                    fox_values("fox_loop", f".{c}", i, 2 * i + (c + 1))
            pool.wait_ge(pe_done, M.after("fox_peel", "pv1.0"))
            fox_values("fox_peel", ".0", 0, FOX_PAIRS - 1)
            out_layer("fox_out", "fox")
            for n in range(2):
                own("pad0", f"pad{n}")
                nc.gpsimd.memset(u[n][:, 0:2], 0.0).then_inc(pool_done, 1)
            out_layer("ffn0_out", "ffn0")

            def prob_sums(name, turn):
                for h in range(2):
                    p, total = ml["prob"][h], ml["psum"][h]
                    own(name, f"s{h}a", turn)
                    pool.wait_ge(act_done, A.after(name, f"exp{h}t2", turn))
                    nc.gpsimd.tensor_tensor(total[:, 0:P], p[:, 0:P], ones[:, :], ALU.mult).then_inc(pool_done, 1)
                    own(name, f"s{h}b", turn)
                    nc.gpsimd.tensor_tensor(total[:, P:T], p[:, P:T], p[:, PROB_AT[1]:PROB_AT[1] + T - P], ALU.add)\
                        .then_inc(pool_done, 1)
                    for n, c in ((2, "c"), (3, "d")):
                        own(name, f"s{h}{c}", turn)
                        nc.gpsimd.tensor_tensor(total[:, n * P:T], total[:, n * P:T],
                                                p[:, PROB_AT[n]:PROB_AT[n] + T - n * P], ALU.add).then_inc(pool_done, 1)

            for half in "ab":
                prob_sums(f"mla_{half}_first", 0)
                with pool.Fori(0, 3) as i:
                    prob_sums(f"mla_{half}_loop", i)
            out_layer("mla_out_b", "mla")
            for n in range(2):
                own("pad1", f"pad{n}")
                pool.wait_ge(slab_used, SLAB_AT["ffn1_in"])
                nc.gpsimd.memset(u[n][:, 0:2], 0.0).then_inc(pool_done, 1)
            zero_sum("ffn1_out", "ffn1")
            own("ffn1_out.zero", "zero_g")
            pool.wait_ge(vec_done, V.end("ffn1_in"))
            nc.gpsimd.memset(u[0][:, 0:T], 0.0).then_inc(pool_done, 1)
            with pool.Fori(0, 2) as i:
                for c in range(4):
                    for step, need, total, buf in (("acc", "sq", sq_sum[:, :], sq), ("acg", "sg", u[0][:, 0:T], tap)):
                        own("ffn1_out", f"{step}{c}", i)
                        pool.wait_ge(act_done, A.after("ffn1_out", f"{need}{c}", i))
                        nc.gpsimd.tensor_tensor(total, total, buf[c % 2][:, :], ALU.add).then_inc(pool_done, 1)
            for n, dst in enumerate([ns["bk"][:, :, T:T + STRIDE]] + [r[:, 0:STRIDE] for r in ns["run"]]
                                    + [ns[z][:, :, :, :].bitcast(F) for z in ("kc_hi", "kc_lo")]
                                    + [ns["vc"][:, :, :]]):
                own("nsa_in", f"pad{n}")
                pool.wait_ge(pe_done, M.end("x2"))
                nc.gpsimd.memset(dst, 0.0).then_inc(pool_done, 1)
            own("nsa_in", "gates0")
            pool.wait_ge(vec_done, V.end("x2"))
            nc.gpsimd.memset(ns["gates"][:, :], 0.0).then_inc(pool_done, 1)
            for n in range(8):
                b, h, kind = n // 4, n // 2 % 2, ("k_hi", "k_lo")[n % 2]
                own("nsa_attn.zero", f"k{n}")
                pool.wait_ge(slab_used, SLAB_AT["nsa_cmp"])
                nc.gpsimd.memset(ns[kind][b][h][(1 - h) * DH:(2 - h) * DH, :].bitcast(F), 0.0).then_inc(pool_done, 1)
            own("nsa_attn.zero", "vones")
            nc.gpsimd.memset(ns["v"][:, :, :, :, :], 1.0).then_inc(pool_done, 1)
            with pool.Fori(0, 2) as i:
                pool.wait_ge(pe_done, M.after("nsa_attn", "g", i) - 1)
                for b in range(2):
                    own("nsa_attn", f"vz{b}", i)
                    pool.wait_ge(act_done, A.end("nsa_proj"))
                    nc.gpsimd.tensor_copy(
                        ns["v"][:, :, b, :, :].rearrange("p t h (a d) -> p t (h a) d", a=2)[:, :, 0:4:3, :],
                        ns["v_raw"][:, :, bass.ds(i, 1), b * DH:(b + 1) * DH].broadcast_to([P, TT, 2, DH]))\
                        .then_inc(pool_done, 1)
                for n in range(4):
                    j, b = n // 2, n % 2
                    g = ns["g"][:, 3 * j + 1 + b, :]
                    own("nsa_attn", f"gm.{n}", i)
                    pool.wait_ge(vec_done, V.after("nsa_attn", f"on1.{n + 1}", i))
                    nc.gpsimd.tensor_tensor(g, g, ns["o"][:, :], ALU.mult).then_inc(pool_done, 1)
                    own("nsa_attn", f"ga.{n}", i)
                    nc.gpsimd.tensor_tensor(ns["g"][:, 3 * j, :], ns["g"][:, 3 * j, :], g, ALU.add).then_inc(pool_done, 1)
            out_layer("nsa_out", None)
            out_layer("sw0_out", "sw0")
            zero_sum("pw1", "pw1")
            for c in range(2):
                for n, z in enumerate([cf["z"][c][:, 0:TAPS - 1]] + [cf[z][c][:, 0:TAPS - 1].bitcast(F) for z in ("z_hi", "z_lo")]):
                    own("pw1.zero", f"zpad{n}{c}")
                    pool.wait_ge(slab_used, SLAB_AT["pw1"])
                    nc.gpsimd.memset(z, 0.0).then_inc(pool_done, 1)
            with pool.Fori(0, KD // 2) as i:
                for c in range(2):
                    for z, name, need in ((0, "dh", (act_done, A.after("pw1", f"wh{c}", i))),
                                          (1, "dl", (vec_done, V.after("pw1", f"wl{c}", i)))):
                        own("pw1", f"{name}{c}", i)
                        pool.wait_ge(*need)
                        w = (cf["w_hi"][c][:, 0:TAPS].bitcast(F), cf["w_lo"][c][:, 0:TAPS])[z][:, TAPS - PE_TAPS:]
                        nc.gpsimd.tensor_tensor(cf["diag"][c][z][:, :, :], mats[:, 0:1, :].broadcast_to([P, PE_TAPS, P]),
                                                w.rearrange("p (k o) -> p k o", o=1).broadcast_to([P, PE_TAPS, P]),
                                                ALU.mult).then_inc(pool_done, 1)
                    own("pw1", f"acc{c}", i)
                    pool.wait_ge(vec_done, V.after("pw1", f"y{c}", i))
                    nc.gpsimd.tensor_tensor(sq_sum[:, :], sq_sum[:, :], cf["y"][:, bass.ds(2 * i + c, 1), :], ALU.add)\
                        .then_inc(pool_done, 1)
            own("pw2.zero", "zero")
            pool.wait_ge(pe_done, M.after("ln", "mean"))
            nc.gpsimd.memset(sq_sum[:, :], 0.0).then_inc(pool_done, 1)
            with pool.Fori(0, 2) as i:
                sum_squares("pw2", 4, i)
            out_layer("sw1_out", "sw1")

        @block.scalar
        def _(act):
            def own(plan_stage, step, turn=0):
                n = A.after(plan_stage, step, turn) - 1
                if isinstance(n, int) and n == 0:
                    return
                act.wait_ge(act_done, n)

            def split_hi(s0, turn=0, per=0):
                if isinstance(turn, int) and s0 + per * turn >= NSLABS:
                    return
                act.wait_ge(raw_loaded[s0 % RAW], 16 * (s0 // RAW + 1) + turn * (16 * per // RAW))
                if s0 >= RING:
                    act.wait_ge(slab_used, s0 - RING + 1 + turn * per)
                nc.scalar.activation(w_hi[s0 % RING][:, :], raw[s0 % RAW][:, :], ACT.Copy).then_inc(hi_ready, 1)

            def norm_unit(name, c, n, gain, turn=0, full=True, need=None):
                own(name, f"hi{c}" if full else f"sq{c}", turn)
                if need:
                    act.wait_ge(*need)
                if name != "x_in" or c >= 2:
                    act.wait_ge(pool_done, G.after(name, f"acc{c}", turn) - 2)
                if full:
                    nc.scalar.activation(h_hi[:, bass.ds(n, 1), :], x[:, bass.ds(n, 1), :], ACT.Copy,
                                         scale=col(gain, n)).then_inc(act_done, 1)
                nc.scalar.activation(sq[c % 2][:, :], x[:, bass.ds(n, 1), :], ACT.Square).then_inc(act_done, 1)

            def stats(name, width, cols_too=False):
                own(name + ".stat", "root")
                act.wait_ge(pe_done, M.after(name + ".stat", "sum"))
                nc.scalar.activation(root[:, :], bank[7][:, :], ACT.Sqrt, bias=col("eps"),
                                     scale=1.0 / width).then_inc(act_done, 1)
                if cols_too:
                    own(name + ".stat", "root_cols")
                    act.wait_ge(pe_done, M.after(name + ".stat", "cols"))
                    nc.scalar.activation(root_col[:, :], bank[6][:, 0:TT], ACT.Sqrt, bias=col("eps"),
                                         scale=1.0 / width).then_inc(act_done, 1)

            def out_layer(name, gain, full=True):
                def half(i):
                    s = SLAB_AT[name]
                    for c in range(4):
                        for _k in OUT[name]:
                            split_hi(s + RING, i, 4 * len(OUT[name]))
                            s += 1
                        norm_unit(name, c, 4 * i + c, gain, i, full, (vec_done, V.after(name, f"x{c}", i)))

                if name == "sw1_out":
                    half(0)
                    half(1)
                else:
                    with act.Fori(0, 2) as i:
                        half(i)

            act.wait_ge(gain_loaded, 16)
            for n in range(KD):
                act.wait_ge(x_loaded[n], 16)
                norm_unit("x_in", n, n, "fox_norm")
                if n % 2 == 0:
                    split_hi(n // 2)
            act.wait_ge(const_loaded, 48)
            for step, dst, src in (("ident", ident_r[:, :], ident), ("mask0", mask_r[0][:, :], mats[:, 1, :]),
                                   ("mask1", mask_r[1][:, :], mats[:, 2, :]),
                                   ("side", side_hi[:, :], side_raw[:, :])):
                own("init", step)
                nc.scalar.activation(dst, src, ACT.Copy).then_inc(act_done, 1)
            act.wait_ge(vec_done, V.after("init", "side"))
            stats("fox", D, True)

            act.wait_ge(vec_done, V.after("fox.stat", "rstd_cols"))
            s = SLAB_AT["fox_v"]

            def fox_v_half(half):
                for c in range(4):
                    split_hi(s + 4 * half + c + RING)
                for t in range(TT):
                    own("fox_v", f"v{half}t{t}")
                    act.wait_ge(slab_used, s + 4 * half + 4)
                    nc.scalar.activation(fx["v"][:, t, half * T:(half + 1) * T], bank[4 * half + t][:, :], ACT.Copy,
                                         scale=rstd_col[:, t:t + 1]).then_inc(act_done, 1)

            fox_v_half(0)
            fox_v_half(1)
            own("fox_v", "e")
            act.wait_ge(vec_done, V.after("fox_v", "na"))
            nc.scalar.activation(fx["q_raw"][0:FOX_H, :], fx["na"][0:FOX_H, 0:T], ACT.Exp).then_inc(act_done, 1)
            own("fox_v", "ln")
            nc.scalar.activation(fx["k_raw"][0:FOX_H, :], fx["q_raw"][0:FOX_H, :], ACT.Ln, bias=1.0)\
                .then_inc(act_done, 1)

            def fox_proj(name, sfx, turn, s0, per):
                split_hi(s0 + RING, turn, per)
                own(name, "qhi" + sfx, turn)
                act.wait_ge(vec_done, V.after(name, "qt" + sfx, turn))
                nc.scalar.activation(fx["q_hi"][:, :], fx["q_raw"][:, :], ACT.Copy).then_inc(act_done, 1)
                for h in range(2):
                    own(name, f"khi{h}{sfx}", turn)
                    act.wait_ge(vec_done, V.after(name, "kt" + sfx, turn))
                    nc.scalar.activation(fx["k_hi"][h][h * DH:(h + 1) * DH, :], fx["k_raw"][h * DH:(h + 1) * DH, :],
                                         ACT.Copy).then_inc(act_done, 1)
                split_hi(s0 + 1 + RING, turn, per)

            def fox_exps(name, sfx, turn, pair):
                for h in range(2):
                    for n, b, at in SCORE_TILES:
                        own(name, f"exp{h}t{n}{sfx}", turn)
                        act.wait_ge(pe_done, M.after(name, f"sc{h}b{b}{sfx}", turn))
                        w = (TT - n) * P
                        nc.scalar.activation(fx["prob"][h][:, PROB_AT[n]:PROB_AT[n] + w],
                                             bank[SLOT[h][b]][:, at:at + w], ACT.Exp,
                                             bias=fx["negc_col"][:, n, bass.ds(2 * pair + h, 1)]).then_inc(act_done, 1)

            def head_sums(b, name, sfx, turn, free):
                for h in range(2):
                    own(name, f"s{h}{sfx}", turn)
                    act.wait_ge(vec_done, free)
                    act.wait_ge(pe_done, M.after(name, f"pv{h}{sfx}", turn))
                    nc.scalar.activation(b["rec"][h * DH:(h + 1) * DH, :], bank[h][(1 - h) * DH:(2 - h) * DH, :],
                                         ACT.Copy).then_inc(act_done, 1)

            def fox_sums(name, sfx, turn, proj=True):
                head_sums(fx, name, sfx, turn, V.after(name, "qt" + sfx, turn) - 1 if proj else V.before(name))

            def fox_out_hi(name, sfx, turn, pair):
                own(name, "ohi" + sfx, turn)
                act.wait_ge(vec_done, V.after(name, "on1" + sfx, turn))
                nc.scalar.activation(fox_o[0][:, bass.ds(pair, 1), :], fx["o"][:, :], ACT.Copy).then_inc(act_done, 1)

            s = SLAB_AT["fox_qk"]
            fox_proj("fox_first", "", 0, s, 0)
            act.wait_ge(vec_done, V.after("fox_cols", "negc_cols"))
            fox_exps("fox_first", "", 0, 0)
            with act.Fori(0, 3) as i:
                for c in range(2):
                    fox_proj("fox_loop", f".{c}", i, s + 2 + 2 * c, 4)
                    fox_sums("fox_loop", f".{c}", i)
                    fox_exps("fox_loop", f".{c}", i, 2 * i + (c + 1))
                    fox_out_hi("fox_loop", f".{c}", i, 2 * i + c)
            fox_proj("fox_peel", ".0", 0, s + 14, 0)
            fox_sums("fox_peel", ".0", 0)
            fox_exps("fox_peel", ".0", 0, FOX_PAIRS - 1)
            fox_out_hi("fox_peel", ".0", 0, FOX_PAIRS - 2)
            fox_sums("fox_last", "", 0, False)
            fox_out_hi("fox_last", "", 0, FOX_PAIRS - 1)
            out_layer("fox_out", "ffn_norm0")

            def glu_in(name, conv):
                with act.Fori(0, KH // 2) as i:
                    for c in range(2):
                        s = SLAB_AT[name] + 2 * c
                        split_hi(s + RING, i, 4)
                        if conv:
                            for n, step, need in ((0, "tapg", "ug"), (1, "tapv", "uv")):
                                own(name, f"{step}{c}", i)
                                act.wait_ge(vec_done, V.after(name, f"{need}{c}", i))
                                at = (2 * i + (c + KH * n)) * 4
                                nc.scalar.activation(tap[n][:, :], u[n][:, 2:T + 2], ACT.Identity,
                                                     bias=col(conv, at + 3), scale=col(conv, at + 2))\
                                    .then_inc(act_done, 1)
                        split_hi(s + 1 + RING, i, 4)
                        own(name, f"silu{c}", i)
                        act.wait_ge(vec_done, V.after(name, ("c2g" if conv else "ug") + str(c), i))
                        nc.scalar.activation(tap[0][:, :], tap[0][:, :], ACT.Silu).then_inc(act_done, 1)
                        own(name, f"hi{c}", i)
                        act.wait_ge(vec_done, V.after(name, f"mul{c}", i))
                        nc.scalar.activation(act_hi[:, bass.ds(2 * i + c, 1), :], tap[0][:, :], ACT.Copy)\
                            .then_inc(act_done, 1)

            stats("ffn0", D)
            glu_in("ffn0_in", "conv0")
            out_layer("ffn0_out", "kv_in_norm")

            act.wait_ge(slab_used, SLAB_AT["mla_kvq"])
            act.dma_start(ml["cos"][:, :], rows_dram[:, 0, 0:T]).then_inc(tables_loaded, 16)
            act.dma_start(ml["sin"][:, :], rows_dram[:, 1, 0:T]).then_inc(tables_loaded, 16)
            stats("mla", D)
            for n in range(KD):
                own("mla_kvq", f"h_hi{n}")
                nc.scalar.activation(ml["o_hi"][:, n, :], x[:, n, :], ACT.Copy, scale=col("mla_norm", n))\
                    .then_inc(act_done, 1)
            tl = [ml["prob"][0][:, j * T:(j + 1) * T] for j in range(2)]

            def kvq_splits(split, t):
                for j in range(kvq_slabs(t - 1), kvq_slabs(t)):
                    split(SLAB_AT["mla_kvq"] + j + RING)

            for t in range(2):
                kvq_splits(split_hi, t)
                own("mla_kvq", f"sq_l{t}")
                act.wait_ge(vec_done, V.after("mla_kvq", f"l{t}"))
                nc.scalar.activation(sq[t][:, :], tl[t], ACT.Square).then_inc(act_done, 1)
            kvq_splits(split_hi, 2)
            for h in range(2):
                own("mla_kvq", f"kr_hi{h}")
                act.wait_ge(vec_done, V.after("mla_kvq", "krn"))
                nc.scalar.activation(ml["kr_hi"][h][:, :], ml["prob"][1][:, 0:T], ACT.Copy, scale=col("rope_pick", h))\
                    .then_inc(act_done, 1)
            own("mla_kvq", "root_l")
            act.wait_ge(pe_done, M.after("mla_kvq", "lat_sum"))
            nc.scalar.activation(root[:, :], bank[7][:, :], ACT.Sqrt, bias=col("eps"), scale=1.0 / LAT)\
                .then_inc(act_done, 1)
            for j in range(KL):
                own("mla_kvq", f"hi_l{j}")
                act.wait_ge(vec_done, V.after("mla_kvq", f"ln{j}"))
                nc.scalar.activation(ml["l_hi"][:, j, :], tl[j], ACT.Copy).then_inc(act_done, 1)
            for j in range(KQ):
                kvq_splits(split_hi, 3 + j)
                own("mla_kvq", f"q_hi{j}")
                act.wait_ge(vec_done, V.after("mla_kvq", f"q{j}"))
                nc.scalar.activation(ml["ql_hi"][:, j, :], tl[j % 2], ACT.Copy, scale=col("q_norm", j))\
                    .then_inc(act_done, 1)
                own("mla_kvq", f"q_sq{j}")
                if j >= 2:
                    act.wait_ge(pe_done, M.after("mla_kvq", f"q_sum{j - 2}"))
                nc.scalar.activation(sq[j % 2][:, :], tl[j % 2], ACT.Square).then_inc(act_done, 1)
            own("mla_kvq", "root_q")
            act.wait_ge(pe_done, M.after("mla_kvq", f"q_sum{KQ - 1}"))
            nc.scalar.activation(root[:, :], bank[7][:, :], ACT.Sqrt, bias=col("eps"), scale=1.0 / QLAT)\
                .then_inc(act_done, 1)

            def mla_step(name, turn, s0, per, n_out):
                for step, need, dst, src in (("n0hi", "n0", ml["qn_hi"][0], ml["q_raw"]),
                                             ("n1hi", "n1", ml["qn_hi"][1], ml["rot"]),
                                             ("rhi", "rs", ml["qr_hi"], ml["q_raw"])):
                    own(name, step, turn)
                    act.wait_ge(vec_done, V.after(name, need, turn))
                    nc.scalar.activation(dst[:, :], src[:, :], ACT.Copy).then_inc(act_done, 1)
                    split_hi(s0 + ("n0hi", "n1hi", "rhi").index(step) + RING, turn, per)
                for h in range(2):
                    own(name, f"k{h}hi", turn)
                    act.wait_ge(pe_done, M.after(name, f"k{h}", turn))
                    nc.scalar.activation(ml["k_hi"][h][:, :], bank[5 + h][:, :], ACT.Copy).then_inc(act_done, 1)
                if n_out is not None:
                    mla_out_hi(name, turn, n_out, 0)
                for h in range(2):
                    for n, b, at in SCORE_TILES:
                        own(name, f"exp{h}t{n}", turn)
                        act.wait_ge(pe_done, M.after(name, f"sc{h}b{b}", turn))
                        w = (TT - n) * P
                        nc.scalar.activation(ml["prob"][h][:, PROB_AT[n]:PROB_AT[n] + w],
                                             bank[SLOT[h][b]][:, at:at + w], ACT.Exp).then_inc(act_done, 1)
                if n_out is not None:
                    mla_out_hi(name, turn, n_out, 1)
                for j in range(2):
                    own(name, f"v{j}", turn)
                    act.wait_ge(slab_used, s0 + 4 + turn * per)
                    nc.scalar.activation(ml["v"][:, 2 * j:2 * j + 2, :, :].rearrange("p t h d -> p (t h d)"),
                                         bank[j][:, :], ACT.Copy).then_inc(act_done, 1)
                split_hi(s0 + 3 + RING, turn, per)

            def mla_out_hi(name, turn, n, h):
                own(name, f"ohi{h}", turn)
                act.wait_ge(vec_done, V.after(name, f"on{h}", turn))
                nc.scalar.activation(ml["o_hi"][:, bass.ds(n + h, 1), :], ml["o"][:, :], ACT.Copy).then_inc(act_done, 1)

            for half in "ab":
                s = SLAB_AT["mla_" + half]
                mla_step(f"mla_{half}_first", 0, s, 0, None)
                with act.Fori(0, 3) as i:
                    mla_step(f"mla_{half}_loop", i, s + 4, 4, 2 * i)
                for h in range(2):
                    mla_out_hi(f"mla_{half}_last", 0, 6, h)
                if half == "a":
                    for n in range(KD):
                        split_hi(SLAB_AT["mla_out_a"] + n + RING)
            out_layer("mla_out_b", "ffn_norm1")
            stats("ffn1", D)
            glu_in("ffn1_in", "conv1")
            with act.Fori(0, 2) as i:
                s = SLAB_AT["ffn1_out"]
                for c in range(4):
                    for _k in OUT["ffn1_out"]:
                        split_hi(s + RING, i, 4 * len(OUT["ffn1_out"]))
                        s += 1
                    own("ffn1_out", f"hi{c}", i)
                    act.wait_ge(vec_done, V.after("ffn1_out", f"x{c}", i))
                    act.wait_ge(pool_done, G.after("ffn1_out", f"acc{c}", i) - 3)
                    n = 4 * i + c
                    nc.scalar.activation(h_hi[:, bass.ds(n, 1), :], x[:, bass.ds(n, 1), :], ACT.Copy,
                                         scale=col("gains", n)).then_inc(act_done, 1)
                    nc.scalar.activation(sq[c % 2][:, :], x[:, bass.ds(n, 1), :], ACT.Square).then_inc(act_done, 1)
                    nc.scalar.activation(tap[c % 2][:, :], x[:, bass.ds(n, 1), :], ACT.Square,
                                         scale=col("final_norm", n)).then_inc(act_done, 1)

            act.wait_ge(slab_used, SLAB_AT["nsa_in"])
            act.dma_start(ns["w2"][:, :], side_dram[:, SIDE["w2"]:SIDE["w2"] + P + DH]).then_inc(tables_loaded, 16)
            act.dma_start(ns["tab"][:, :, :].rearrange("p g n -> p (g n)"), tab_dram).then_inc(tables_loaded, 16)
            own("x2", "root")
            act.wait_ge(pe_done, M.after("x2", "sum"))
            nc.scalar.activation(root[:, :], bank[7][:, :], ACT.Sqrt, bias=col("eps"), scale=1.0 / D).then_inc(act_done, 1)
            own("x2", "root2")
            act.wait_ge(vec_done, V.after("x2", "ms"))
            nc.scalar.activation(root[:, :], root[:, :], ACT.Sqrt, bias=col("eps"), scale=1.0 / D).then_inc(act_done, 1)
            s = SLAB_AT["nsa_in"]
            for n, kv in enumerate("kv"):
                split_hi(s + n + RING)
                own("nsa_in", "hi" + kv)
                act.wait_ge(vec_done, V.after("nsa_in", f"bl{kv}11"))
                nc.scalar.activation(ns["b_hi"][n][:, :, :, :], ns["blk"][:, :, :, :], ACT.Copy).then_inc(act_done, 1)
            for g in range(4):
                split_hi(s + 2 + g + RING)
                own("nsa_in", f"d_hi{g}")
                act.wait_ge(vec_done, V.after("nsa_in", f"first{g}"))
                nc.scalar.activation(ns["o_hi"][:, 4 + g, :], ns["run"][1 + (g + 1) % 2][:, STRIDE:], ACT.Copy)\
                    .then_inc(act_done, 1)
            own("nsa_in", "sig")
            act.wait_ge(vec_done, V.after("nsa_in", "gz"))
            nc.scalar.activation(ns["gates"][0:NGATE, :], ns["gates"][0:NGATE, :], ACT.Sigmoid).then_inc(act_done, 1)
            act.dma_start(ns["o"][:, :], rows_dram[:, 2, :]).then_inc(tables_loaded, 16)
            own("nsa_cmp.table", "table")
            act.wait_ge(tables_loaded, 80)
            nc.scalar.activation(ns["table"][:, :], ns["o"][:, :], ACT.Copy).then_inc(act_done, 1)
            s = SLAB_AT["nsa_proj"]
            for c in range(8):
                split_hi(s + c + RING)
            for t in range(TT):
                own("nsa_proj", f"v{t}")
                act.wait_ge(slab_used, s + 8)
                act.wait_ge(vec_done, V.after("nsa_in", "cols"))
                nc.scalar.activation(ns["v_raw"][:, t, :, :].rearrange("p g n -> p (g n)"),
                                     bank[5 + t // 2][:, (t % 2) * 2 * P:(t % 2 + 1) * 2 * P], ACT.Copy,
                                     scale=rstd_col[:, t:t + 1]).then_inc(act_done, 1)
            s = SLAB_AT["nsa_cmp"]
            for n, kv in enumerate("kv"):
                split_hi(s + 2 * n + RING)
                split_hi(s + 1 + 2 * n + RING)
                own("nsa_cmp", "gelu_" + kv)
                act.wait_ge(slab_used, s + 2 * n + 2)
                nc.scalar.activation(ns["gh"][n][:, :, :].rearrange("p g n -> p (g n)"), bank[(7, 1)[n]][:, 0:64],
                                     ACT.Gelu_apprx_tanh).then_inc(act_done, 1)
            split_hi(s + 4 + RING)
            split_hi(s + 5 + RING)
            for g in range(4):
                own("nsa_cmp", f"p_hi{g}")
                act.wait_ge(slab_used, s + 5 + g // 2)
                nc.scalar.activation(ns["o_hi"][:, 4 + g, :], bank[POOL_BANK[g]][:, :], ACT.Copy,
                                     scale=col("pool_scale", g)).then_inc(act_done, 1)
            for h in range(2):
                own("nsa_cmp", f"kc{h}")
                act.wait_ge(pe_done, M.after("nsa_cmp", "kcmp"))
                hs = slice(h * DH, (h + 1) * DH)
                nc.scalar.activation(ns["kc_hi"][hs, :, h, :], bank[2][hs, 0:64].rearrange("p (g n) -> p g n", g=2),
                                     ACT.Copy).then_inc(act_done, 1)
            for h in range(2):
                own("nsa_cmp", f"vc{h}")
                act.wait_ge(pe_done, M.after("nsa_cmp", "vcmp"))
                nc.scalar.activation(ns["vc"][h * NCMPCOL:(h + 1) * NCMPCOL, :, h * DH:(h + 1) * DH],
                                     bank[3][0:NCMPCOL, 0:P].rearrange("p (g d) -> p g d", g=2), ACT.Copy)\
                    .then_inc(act_done, 1)
            own("nsa_gates", "ghi")
            act.wait_ge(pe_done, M.end("nsa_cmp"))
            nc.scalar.activation(ns["g_hi"][:, :], ns["gates"][:, :], ACT.Copy).then_inc(act_done, 1)

            def nsa_group(i):
                name = "nsa_attn"

                def step(what, dst, src, *waits, **kw):
                    own(name, what, i)
                    for w in waits:
                        act.wait_ge(*w)
                    nc.scalar.activation(dst, src, ACT.Copy, **kw).then_inc(act_done, 1)

                act.wait_ge(vec_done, V.after(name, "gs0", i) - 1)
                step("bias", ns["bias"][:, :], col("alibi", 16 * i, 16))
                step("vcg", ns["vcg"][:, :], ns["vc"][:, bass.ds(i, 1), :])
                for j in range(2):
                    step(f"q{j}hi", ns["q_hi"][j][:, :], ns["q_raw"][:, bass.ds(2 * i + j, 1), :])

                def keys(b):
                    for h in range(2):
                        hs = slice(h * DH, (h + 1) * DH)
                        step(f"khi{b}{h}", ns["k_hi"][b][h][hs, :], ns["k_raw"][hs, bass.ds(i, 1), b, :])

                keys(0)
                for n in range(6):
                    step(f"g{n}", ns["g"][:, n, :], bank[2 + n][:, :], (pe_done, M.after(name, "g", i)))
                keys(1)
                own(name, "cexp", i)
                act.wait_ge(vec_done, V.after(name, "csub", i))
                nc.scalar.activation(ns["cmp"][:, :], ns["cmp"][:, :], ACT.Exp).then_inc(act_done, 1)

                def out_hi(j):
                    step(f"ohi{j}", ns["o_hi"][:, bass.ds(2 * i + j, 1), :], ns["g"][:, 3 * j, :],
                         (pool_done, G.after(name, f"ga.{2 * j + 1}", i)))

                def sums(u):
                    head_sums(ns, name, f".{u}", i, V.after(name, f"on1.{u - 1}" if u > 1 else "acc1", i))

                for u in range(4):
                    if u:
                        sums(u)
                    for h in range(2):
                        for n, b, at in SCORE_TILES:
                            own(name, f"exp{h}t{n}.{u}", i)
                            act.wait_ge(pe_done, M.after(name, f"sc{h}b{b}.{u}", i))
                            w = (TT - n) * P
                            nc.scalar.activation(ns["prob"][h][:, PROB_AT[n]:PROB_AT[n] + w],
                                                 bank[SLOT[h][b]][:, at:at + w], ACT.Exp,
                                                 bias=ns["bias"][:, 4 * n + 2 * (u // 2) + h:4 * n + 2 * (u // 2) + h + 1]).then_inc(act_done, 1)
                    if u == 0:
                        for j in range(2):
                            step(f"pt{j}", turned[j], bank[j][0:2 * NCMPCOL, :], (pe_done, M.after(name, "tr", i)))
                    if u == 2:
                        out_hi(0)
                sums(4)
                out_hi(1)

            with act.Fori(0, 2) as i:
                nsa_group(i)
            out_layer("nsa_out", "ffn2_norm0")
            stats("sw0", D)
            glu_in("sw0_in", None)
            out_layer("sw0_out", "mix_norm1")

            stats("pw1", D)
            s = SLAB_AT["pw1"]
            with act.Fori(0, KD // 2) as i:
                for c in range(2):
                    split_hi(s + 2 * c + RING, i, 4)
                    own("pw1", f"w{c}", i)
                    act.wait_ge(vec_done, V.after("pw1", f"ua{c}", i) - 1 - len(V.steps["pw1"]) // 2)
                    nc.scalar.activation(cf["w"][c][:, :], col("w_dw", 2 * TAPS * i + TAPS * c, TAPS), ACT.Copy)\
                        .then_inc(act_done, 1)
                    own("pw1", f"wh{c}", i)
                    nc.scalar.activation(cf["w_hi"][c][:, 0:TAPS], cf["w"][c][:, :], ACT.Copy).then_inc(act_done, 1)
                    own("pw1", f"sg{c}", i)
                    act.wait_ge(vec_done, V.after("pw1", f"ug{c}", i))
                    nc.scalar.activation(cf["gate"][:, :], cf["gate"][:, :], ACT.Sigmoid,
                                         bias=col("b_pw1", 2 * i + (KD + c))).then_inc(act_done, 1)
                    split_hi(s + 2 * c + 1 + RING, i, 4)
                    own("pw1", f"zh{c}", i)
                    act.wait_ge(vec_done, V.after("pw1", f"z{c}", i))
                    nc.scalar.activation(cf["z_hi"][c][:, TAPS - 1:], cf["z"][c][:, TAPS - 1:], ACT.Copy).then_inc(act_done, 1)
                    own("pw1", f"t{c}", i)
                    nc.scalar.activation(cf["acc"][c][:, :], cf["z"][c][:, 0:T], ACT.Identity,
                                         bias=col("b_dw", 2 * i + c), scale=cf["w"][c][:, 0:1]).then_inc(act_done, 1)
            own("ln", "mean")
            act.wait_ge(pe_done, M.after("ln", "mean"))
            nc.scalar.activation(root[:, :], bank[7][:, :], ACT.Copy, scale=1.0 / D).then_inc(act_done, 1)
            for n in range(KD):
                own("ln", f"sq{n}")
                act.wait_ge(vec_done, V.after("ln", f"xc{n}"))
                if n >= 2:
                    act.wait_ge(pe_done, M.after("ln", f"v{n - 2}"))
                nc.scalar.activation(sq[n % 2][:, :], cf["y"][:, n, :], ACT.Square).then_inc(act_done, 1)
            own("ln", "root")
            act.wait_ge(pe_done, M.after("ln", f"v{KD - 1}"))
            nc.scalar.activation(root[:, :], bank[7][:, :], ACT.Sqrt, bias=col("eps_ln"), scale=1.0 / D)\
                .then_inc(act_done, 1)
            for n in range(KD):
                own("ln", f"s{n}")
                act.wait_ge(vec_done, V.after("ln", f"yn{n}"))
                nc.scalar.activation(cf["y"][:, n, :], cf["y"][:, n, :], ACT.Silu, bias=col("ln_b", n),
                                     scale=col("ln_g", n)).then_inc(act_done, 1)
                own("ln", f"hi{n}")
                nc.scalar.activation(cf["o_hi"][:, n, :], cf["y"][:, n, :], ACT.Copy).then_inc(act_done, 1)
            out_layer("pw2", "ffn2_norm1")
            stats("sw1", D)
            glu_in("sw1_in", None)
            out_layer("sw1_out", None, False)
            stats("final", D)

        @block.vector
        def _(dve):
            def own(plan_stage, step, turn=0):
                n = V.after(plan_stage, step, turn) - 1
                if isinstance(n, int) and n == 0:
                    return
                dve.wait_ge(vec_done, n)

            def split_lo(s0, turn=0, per=0):
                if isinstance(turn, int) and s0 + per * turn >= NSLABS:
                    return
                dve.wait_ge(hi_ready, s0 + 1 + turn * per)
                nc.vector.tensor_tensor(w_lo[s0 % RING][:, :], raw[s0 % RAW][:, :],
                                        w_hi[s0 % RING][:, :].bitcast(F), ALU.subtract).then_inc(lo_ready, 1)

            def norm_lo(name, c, n, gain, turn=0):
                own(name, f"lo{c}", turn)
                dve.wait_ge(act_done, A.after(name, f"hi{c}", turn))
                nc.vector.scalar_tensor_tensor(h_lo[:, bass.ds(n, 1), :], x[:, bass.ds(n, 1), :], col(gain, n),
                                               h_hi[:, bass.ds(n, 1), :].bitcast(F), ALU.mult, ALU.subtract)\
                    .then_inc(vec_done, 1)

            def stats(name, cols_too=False):
                own(name + ".stat", "rstd")
                dve.wait_ge(act_done, A.after(name + ".stat", "root"))
                nc.vector.reciprocal(rstd[:, :], root[:, :]).then_inc(vec_done, 1)
                if cols_too:
                    own(name + ".stat", "rstd_cols")
                    dve.wait_ge(act_done, A.after(name + ".stat", "root_cols"))
                    nc.vector.reciprocal(rstd_col[:, :], root_col[:, :]).then_inc(vec_done, 1)

            def out_layer(name, gain, full=True, bias=None):
                parts = OUT[name]

                def half(i):
                    s = SLAB_AT[name]
                    for c in range(4):
                        for _k in parts:
                            split_lo(s + RING, i, 4 * len(parts))
                            s += 1
                        own(name, f"x{c}", i)
                        dve.wait_ge(slab_used, s + i * (4 * len(parts)))
                        n = 4 * i + c
                        if bias:
                            nc.vector.scalar_tensor_tensor(x[:, bass.ds(n, 1), :], bank[4 + c % 2][:, :], col(bias, n),
                                                           x[:, bass.ds(n, 1), :], ALU.add, ALU.add).then_inc(vec_done, 1)
                        else:
                            nc.vector.tensor_tensor(x[:, bass.ds(n, 1), :], x[:, bass.ds(n, 1), :],
                                                    bank[4 + c % 2][:, :], ALU.add).then_inc(vec_done, 1)
                        if full:
                            norm_lo(name, c, n, gain, i)

                if name == "sw1_out":
                    half(0)
                    half(1)
                else:
                    with dve.Fori(0, 2) as i:
                        half(i)

            for n in range(KD):
                norm_lo("x_in", n, n, "fox_norm")
                if n % 2 == 0:
                    split_lo(n // 2)
            own("init", "side")
            dve.wait_ge(act_done, A.after("init", "side"))
            nc.vector.tensor_tensor(side_lo[:, :], side_raw[:, :], side_hi[:, :].bitcast(F), ALU.subtract)\
                .then_inc(vec_done, 1)
            own("init", "gains")
            nc.vector.tensor_tensor(gains[:, :], col("final_norm", 0, KD), col("mix_norm0", 0, KD), ALU.mult)\
                .then_inc(vec_done, 1)
            stats("fox", True)

            s = SLAB_AT["fox_v"]
            for c in range(8):
                split_lo(s + c + RING)
            hs = slice(0, FOX_H)
            own("fox_v", "z0")
            dve.wait_ge(pe_done, M.after("fox_v", "f"))
            nc.vector.tensor_tensor(fx["z"][hs, :], rstd[hs, :], bank[0][hs, :], ALU.mult).then_inc(vec_done, 1)
            own("fox_v", "z")
            nc.vector.tensor_scalar(fx["z"][hs, :], fx["z"][hs, :], cols[hs, COLS["b_fox"]:COLS["b_fox"] + 1], None,
                                    ALU.add).then_inc(vec_done, 1)
            own("fox_v", "na")
            nc.vector.scalar_tensor_tensor(fx["na"][hs, 0:T], fx["z"][hs, :], -1.0, fx["z"][hs, :], ALU.mult, ALU.min)\
                .then_inc(vec_done, 1)
            own("fox_v", "logf")
            dve.wait_ge(act_done, A.after("fox_v", "ln"))
            nc.vector.scalar_tensor_tensor(fx["na"][hs, 0:T], fx["z"][hs, :], 0.0, fx["k_raw"][hs, :], ALU.min,
                                           ALU.subtract).then_inc(vec_done, 1)
            own("fox_v", "scan")
            dve.wait_ge(pool_done, G.after("fox_v", "ones_row"))
            nc.vector.tensor_tensor_scan(fx["negc"][hs, :], fx["ones_row"][hs, :], fx["na"][hs, 0:T], 0.0, ALU.mult,
                                         ALU.subtract).then_inc(vec_done, 1)
            own("fox_v", "negc_r")
            nc.vector.tensor_copy(fx["negc_r"][hs, :], fx["negc"][hs, :]).then_inc(vec_done, 1)

            def fox_proj(name, sfx, turn, s0, per, pair):
                split_lo(s0 + RING, turn, per)
                own(name, "qt" + sfx, turn)
                dve.wait_ge(slab_used, s0 + 1 + turn * per)
                nc.vector.scalar_tensor_tensor(fx["q_raw"][:, :], bank[2][:, :], DH ** -0.5, rstd[:, :], ALU.mult,
                                               ALU.mult).then_inc(vec_done, 1)
                own(name, "qlo" + sfx, turn)
                dve.wait_ge(act_done, A.after(name, "qhi" + sfx, turn))
                nc.vector.tensor_tensor(fx["q_lo"][:, :], fx["q_raw"][:, :], fx["q_hi"][:, :].bitcast(F),
                                        ALU.subtract).then_inc(vec_done, 1)
                for h in range(2):
                    own(name, f"sel{h}{sfx}", turn)
                    nc.vector.tensor_scalar(fx["sel"][h][:, :], ones[:, :], mats[:, 0, bass.ds(2 * pair + h, 1)], None,
                                            ALU.mult).then_inc(vec_done, 1)
                own(name, "kt" + sfx, turn)
                dve.wait_ge(slab_used, s0 + 2 + turn * per)
                nc.vector.tensor_tensor(fx["k_raw"][:, :], rstd[:, :], bank[3][:, :], ALU.mult).then_inc(vec_done, 1)
                for h in range(2):
                    own(name, f"klo{h}{sfx}", turn)
                    dve.wait_ge(act_done, A.after(name, f"khi{h}{sfx}", turn))
                    hs = slice(h * DH, (h + 1) * DH)
                    nc.vector.tensor_tensor(fx["k_lo"][h][hs, :], fx["k_raw"][hs, :], fx["k_hi"][h][hs, :].bitcast(F),
                                            ALU.subtract).then_inc(vec_done, 1)
                split_lo(s0 + 1 + RING, turn, per)

            def head_max(b, name, h, sfx, turn, pe_name=None):
                for n, bk, at in MAX_TILES:
                    own(name, f"mx{h}t{n}{sfx}", turn)
                    dve.wait_ge(pe_done, M.after(pe_name or name, f"max{h}b{bk}{sfx}", turn))
                    nc.vector.tensor_reduce(b["negm"][h][:, n:n + 1], bank[SLOT[h][bk]][:, at:at + (n + 1) * P], AX,
                                            ALU.max, negate=True).then_inc(vec_done, 1)
                own(name, f"dg{h}{sfx}", turn)
                nc.vector.tensor_tensor(
                    b["diag"][h][:, :, :], mats[:, 0:1, :].broadcast_to([P, TT, P]),
                    b["negm"][h][:, :].rearrange("p (t o) -> p t o", o=1).broadcast_to([P, TT, P]),
                    ALU.mult).then_inc(vec_done, 1)

            def fox_max(name, sfx, turn):
                for h in range(2):
                    head_max(fx, name, h, sfx, turn, name.replace("_max", ""))

            def fox_norm(name, sfx, turn, pair):
                own(name, "rc" + sfx, turn)
                dve.wait_ge(act_done, A.after(name, "s1" + sfx, turn))
                nc.vector.reciprocal(fx["rec"][:, :], fx["rec"][:, :]).then_inc(vec_done, 1)
                for h in range(2):
                    hs = slice(h * DH, (h + 1) * DH)
                    own(name, f"on{h}{sfx}", turn)
                    nc.vector.tensor_tensor(fx["o"][hs, :], fx["rec"][hs, :], bank[h][hs, :], ALU.mult)\
                        .then_inc(vec_done, 1)
                own(name, "olo" + sfx, turn)
                dve.wait_ge(act_done, A.after(name, "ohi" + sfx, turn))
                nc.vector.tensor_tensor(fox_o[1][:, bass.ds(pair, 1), :], fx["o"][:, :],
                                        fox_o[0][:, bass.ds(pair, 1), :].bitcast(F), ALU.subtract).then_inc(vec_done, 1)

            s = SLAB_AT["fox_qk"]
            fox_proj("fox_first", "", 0, s, 0, 0)
            own("fox_cols", "negc_cols")
            dve.wait_ge(pe_done, M.after("fox_v", "negc_cols"))
            nc.vector.tensor_copy(fx["negc_col"][:, :, :].rearrange("p t h -> p (t h)"), bank[1][:, 0:TT * FOX_H])\
                .then_inc(vec_done, 1)
            fox_max("fox_first_max", "", 0)
            with dve.Fori(0, 3) as i:
                for c in range(2):
                    fox_proj("fox_loop", f".{c}", i, s + 2 + 2 * c, 4, 2 * i + (c + 1))
                    fox_max("fox_loop", f".{c}", i)
                    fox_norm("fox_loop", f".{c}", i, 2 * i + c)
            fox_proj("fox_peel", ".0", 0, s + 14, 0, FOX_PAIRS - 1)
            fox_max("fox_peel", ".0", 0)
            fox_norm("fox_peel", ".0", 0, FOX_PAIRS - 2)
            fox_norm("fox_last", "", 0, FOX_PAIRS - 1)
            out_layer("fox_out", "ffn_norm0")

            def glu_in(name, conv):
                if conv:
                    dve.wait_ge(pool_done, G.end("pad" + name[3]))
                with dve.Fori(0, KH // 2) as i:
                    for c in range(2):
                        s = SLAB_AT[name] + 2 * c
                        for n, step in ((0, "ug"), (1, "uv")):
                            own(name, f"{step}{c}", i)
                            dve.wait_ge(slab_used, s + 1 + n + i * 4)
                            dst = u[n][:, 2:T + 2] if conv else tap[n][:, :]
                            nc.vector.tensor_tensor(dst, rstd[:, :], bank[2 * c + n][:, :], ALU.mult)\
                                .then_inc(vec_done, 1)
                        split_lo(s + RING, i, 4)
                        if conv:
                            for k in (1, 2):
                                for n, g in ((0, "g"), (1, "v")):
                                    own(name, f"c{k}{g}{c}", i)
                                    dve.wait_ge(act_done, A.after(name, f"tap{g}{c}", i))
                                    at = (2 * i + (c + KH * n)) * 4
                                    nc.vector.scalar_tensor_tensor(tap[n][:, :], u[n][:, 2 - k:T + 2 - k],
                                                                   col(conv, at + 2 - k), tap[n][:, :], ALU.mult,
                                                                   ALU.add).then_inc(vec_done, 1)
                        split_lo(s + 1 + RING, i, 4)
                        own(name, f"mul{c}", i)
                        dve.wait_ge(act_done, A.after(name, f"silu{c}", i))
                        nc.vector.tensor_tensor(tap[0][:, :], tap[0][:, :], tap[1][:, :], ALU.mult).then_inc(vec_done, 1)
                        own(name, f"lo{c}", i)
                        dve.wait_ge(act_done, A.after(name, f"hi{c}", i))
                        nc.vector.tensor_tensor(act_lo[:, bass.ds(2 * i + c, 1), :], tap[0][:, :],
                                                act_hi[:, bass.ds(2 * i + c, 1), :].bitcast(F), ALU.subtract)\
                            .then_inc(vec_done, 1)

            stats("ffn0")
            glu_in("ffn0_in", "conv0")
            out_layer("ffn0_out", "kv_in_norm")

            stats("mla")
            for n in range(KD):
                own("mla_kvq", f"h_lo{n}")
                dve.wait_ge(act_done, A.after("mla_kvq", f"h_hi{n}"))
                nc.vector.scalar_tensor_tensor(ml["o_lo"][:, n, :], x[:, n, :], col("mla_norm", n),
                                               ml["o_hi"][:, n, :].bitcast(F), ALU.mult, ALU.subtract)\
                    .then_inc(vec_done, 1)
            tl = [ml["prob"][0][:, j * T:(j + 1) * T] for j in range(2)]
            ra, rb = (ml["prob"][1][:, j * T:(j + 1) * T] for j in range(2))

            def kvq_splits(t):
                for j in range(kvq_slabs(t - 1), kvq_slabs(t)):
                    split_lo(SLAB_AT["mla_kvq"] + j + RING)

            def rotate(name, steps, turn, src, a, b):
                own(name, steps[0], turn)
                nc.vector.tensor_tensor(a[:, :], ml["cos"][:, :], src[:, :], ALU.mult).then_inc(vec_done, 1)
                for j in range(2):
                    own(name, steps[1 + j], turn)
                    to, of = slice(64 * j, 64 * j + 64), slice(64 - 64 * j, 128 - 64 * j)
                    nc.vector.tensor_tensor(b[to, :], ml["sin"][to, :], src[of, :], ALU.mult).then_inc(vec_done, 1)
                own(name, steps[3], turn)
                nc.vector.tensor_tensor(a[:, :], a[:, :], b[:, :], ALU.add).then_inc(vec_done, 1)

            for t in range(2):
                own("mla_kvq", f"l{t}")
                dve.wait_ge(*kvq_done(t))
                nc.vector.tensor_tensor(tl[t], rstd[:, :], bank[KVQ_BANK[t]][:, :], ALU.mult).then_inc(vec_done, 1)
                kvq_splits(t)
            dve.wait_ge(tables_loaded, 32)
            dve.wait_ge(*kvq_done(2))
            rotate("mla_kvq", ["kra", "krb0", "krb1", "krs"], 0, bank[2], ra, rb)
            own("mla_kvq", "krn")
            nc.vector.tensor_tensor(ra, ra, rstd[:, :], ALU.mult).then_inc(vec_done, 1)
            kvq_splits(2)
            for h in range(2):
                own("mla_kvq", f"kr_lo{h}")
                dve.wait_ge(act_done, A.after("mla_kvq", f"kr_hi{h}"))
                nc.vector.scalar_tensor_tensor(ml["kr_lo"][h][:, :], ra, col("rope_pick", h),
                                               ml["kr_hi"][h][:, :].bitcast(F), ALU.mult, ALU.subtract)\
                    .then_inc(vec_done, 1)
            own("mla_kvq", "rstd_l")
            dve.wait_ge(act_done, A.after("mla_kvq", "root_l"))
            nc.vector.reciprocal(sq_sum[:, :], root[:, :]).then_inc(vec_done, 1)
            for j in range(KL):
                own("mla_kvq", f"ln{j}")
                nc.vector.scalar_tensor_tensor(tl[j], tl[j], col("kv_norm", j), sq_sum[:, :], ALU.mult, ALU.mult)\
                    .then_inc(vec_done, 1)
            for j in range(KL):
                own("mla_kvq", f"lo_l{j}")
                dve.wait_ge(act_done, A.after("mla_kvq", f"hi_l{j}"))
                nc.vector.tensor_tensor(ml["l_lo"][:, j, :], tl[j], ml["l_hi"][:, j, :].bitcast(F), ALU.subtract)\
                    .then_inc(vec_done, 1)
            for j in range(KQ):
                own("mla_kvq", f"q{j}")
                dve.wait_ge(*kvq_done(3 + j))
                if j >= 2:
                    dve.wait_ge(act_done, A.after("mla_kvq", f"q_sq{j - 2}"))
                nc.vector.tensor_tensor(tl[j % 2], rstd[:, :], bank[KVQ_BANK[3 + j]][:, :], ALU.mult)\
                    .then_inc(vec_done, 1)
                kvq_splits(3 + j)
                own("mla_kvq", f"q_lo{j}")
                dve.wait_ge(act_done, A.after("mla_kvq", f"q_hi{j}"))
                nc.vector.scalar_tensor_tensor(ml["ql_lo"][:, j, :], tl[j % 2], col("q_norm", j),
                                               ml["ql_hi"][:, j, :].bitcast(F), ALU.mult, ALU.subtract)\
                    .then_inc(vec_done, 1)
            own("mla_kvq", "rstd_q")
            dve.wait_ge(act_done, A.after("mla_kvq", "root_q"))
            nc.vector.reciprocal(rstd[:, :], root[:, :]).then_inc(vec_done, 1)
            scale = (NOPE + ROPE) ** -0.5
            for step, table in (("cos_q", ml["cos"]), ("sin_q", ml["sin"])):
                own("mla_kvq", step)
                nc.vector.scalar_tensor_tensor(table[:, :], table[:, :], scale, rstd[:, :], ALU.mult, ALU.mult)\
                    .then_inc(vec_done, 1)

            def mla_step(name, turn, s0, per, n_out):
                for h, raw_q in ((0, ml["q_raw"]), (1, ml["rot"])):
                    own(name, f"n{h}", turn)
                    dve.wait_ge(slab_used, s0 + h + 1 + turn * per)
                    nc.vector.scalar_tensor_tensor(raw_q[:, :], bank[2 + h][:, :], scale, rstd[:, :], ALU.mult, ALU.mult)\
                        .then_inc(vec_done, 1)
                    own(name, f"n{h}lo", turn)
                    dve.wait_ge(act_done, A.after(name, f"n{h}hi", turn))
                    nc.vector.tensor_tensor(ml["qn_lo"][h][:, :], raw_q[:, :], ml["qn_hi"][h][:, :].bitcast(F),
                                            ALU.subtract).then_inc(vec_done, 1)
                    split_lo(s0 + h + RING, turn, per)
                dve.wait_ge(slab_used, s0 + 3 + turn * per)
                rotate(name, ["ra", "rb0", "rb1", "rs"], turn, bank[4], ml["q_raw"], ml["rot"])
                own(name, "rlo", turn)
                dve.wait_ge(act_done, A.after(name, "rhi", turn))
                nc.vector.tensor_tensor(ml["qr_lo"][:, :], ml["q_raw"][:, :], ml["qr_hi"][:, :].bitcast(F),
                                        ALU.subtract).then_inc(vec_done, 1)
                for h in range(2):
                    own(name, f"k{h}lo", turn)
                    dve.wait_ge(act_done, A.after(name, f"k{h}hi", turn))
                    nc.vector.tensor_tensor(ml["k_lo"][h][:, :], bank[5 + h][:, :], ml["k_hi"][h][:, :].bitcast(F),
                                            ALU.subtract).then_inc(vec_done, 1)
                if n_out is not None:
                    mla_norm(name, turn, 0)
                head_max(ml, name, 0, "", turn)
                if n_out is not None:
                    mla_out_lo(name, turn, n_out, 0)
                head_max(ml, name, 1, "", turn)
                split_lo(s0 + 2 + RING, turn, per)
                if n_out is not None:
                    mla_norm(name, turn, 1)
                    mla_out_lo(name, turn, n_out, 1)
                split_lo(s0 + 3 + RING, turn, per)

            def mla_norm(name, turn, h):
                own(name, f"rc{h}", turn)
                dve.wait_ge(pe_done, M.after(name, f"sum{h}", turn))
                nc.vector.reciprocal(ml["rec"][:, :], bank[0][:, :]).then_inc(vec_done, 1)
                own(name, f"on{h}", turn)
                nc.vector.tensor_tensor(ml["o"][:, :], ml["rec"][:, :], bank[1][:, :], ALU.mult).then_inc(vec_done, 1)

            def mla_out_lo(name, turn, n, h):
                own(name, f"olo{h}", turn)
                dve.wait_ge(act_done, A.after(name, f"ohi{h}", turn))
                nc.vector.tensor_tensor(ml["o_lo"][:, bass.ds(n + h, 1), :], ml["o"][:, :],
                                        ml["o_hi"][:, bass.ds(n + h, 1), :].bitcast(F), ALU.subtract)\
                    .then_inc(vec_done, 1)

            for half in "ab":
                s = SLAB_AT["mla_" + half]
                mla_step(f"mla_{half}_first", 0, s, 0, None)
                with dve.Fori(0, 3) as i:
                    mla_step(f"mla_{half}_loop", i, s + 4, 4, 2 * i)
                for h in range(2):
                    mla_norm(f"mla_{half}_last", 0, h)
                    mla_out_lo(f"mla_{half}_last", 0, 6, h)
                if half == "a":
                    out_layer("mla_out_a", None, False)
            out_layer("mla_out_b", "ffn_norm1")
            stats("ffn1")
            glu_in("ffn1_in", "conv1")
            out_layer("ffn1_out", "gains")

            r1 = sq_sum
            own("x2", "r1")
            dve.wait_ge(act_done, A.after("x2", "root"))
            nc.vector.reciprocal(r1[:, :], root[:, :]).then_inc(vec_done, 1)
            own("x2", "r1sq")
            nc.vector.tensor_tensor(root[:, :], r1[:, :], r1[:, :], ALU.mult).then_inc(vec_done, 1)
            own("x2", "ms")
            dve.wait_ge(pe_done, M.after("x2", "sum_g"))
            nc.vector.tensor_tensor(root[:, :], root[:, :], bank[6][:, :], ALU.mult).then_inc(vec_done, 1)
            own("x2", "r2")
            dve.wait_ge(act_done, A.after("x2", "root2"))
            nc.vector.reciprocal(rstd[:, :], root[:, :]).then_inc(vec_done, 1)
            own("x2", "rstd")
            nc.vector.tensor_tensor(rstd[:, :], rstd[:, :], r1[:, :], ALU.mult).then_inc(vec_done, 1)
            for n in range(KD):
                own("x2", f"x{n}")
                nc.vector.scalar_tensor_tensor(x[:, n, :], x[:, n, :], col("final_norm", n), r1[:, :], ALU.mult, ALU.mult)\
                    .then_inc(vec_done, 1)
            s = SLAB_AT["nsa_in"]
            for n, kv in enumerate("kv"):
                for g in range(2):
                    for h in range(2):
                        own("nsa_in", f"b{kv}{g}{h}")
                        dve.wait_ge(slab_used, s + n + 1)
                        dve.wait_ge(pool_done, G.after("nsa_in", "pad6"))
                        nc.vector.tensor_tensor(ns["bk"][h * DH:(h + 1) * DH, g, 0:T - h],
                                                rstd[g * DH:(g + 1) * DH, h:T], bank[n][g * DH:(g + 1) * DH, h:T],
                                                ALU.mult).then_inc(vec_done, 1)
                split_lo(s + n + RING)
                for g in range(2):
                    for half in range(2):
                        own("nsa_in", f"bl{kv}{g}{half}")
                        if n:
                            dve.wait_ge(act_done, A.after("nsa_in", "hik"))
                        src = ns["bk"][:, g, half * STRIDE:half * STRIDE + T].rearrange("p (n j o) -> p j n o", j=8, o=2)
                        js = slice(half * 8, half * 8 + 8)
                        pos = col("cmp_pos_" + kv, half * 8, 8).rearrange("p (j o) -> p j o", o=1)
                        nc.vector.tensor_tensor(ns["blk"][:, js, g, :], src[:, :, :, 0],
                                                pos.broadcast_to([P, 8, NCMPCOL]), ALU.add).then_inc(vec_done, 1)
                if n == 0:
                    own("nsa_in", "lok")
                    dve.wait_ge(act_done, A.after("nsa_in", "hik"))
                    nc.vector.tensor_tensor(ns["b_lo"][0][:, :, :, :], ns["blk"][:, :, :, :],
                                            ns["b_hi"][0][:, :, :, :].bitcast(F), ALU.subtract).then_inc(vec_done, 1)
            own("nsa_in", "lov")
            dve.wait_ge(act_done, A.after("nsa_in", "hiv"))
            nc.vector.tensor_tensor(ns["b_lo"][1][:, :, :, :], ns["blk"][:, :, :, :],
                                    ns["b_hi"][1][:, :, :, :].bitcast(F), ALU.subtract).then_inc(vec_done, 1)
            for g in range(4):
                run = ns["run"]
                own("nsa_in", f"u{g}")
                dve.wait_ge(slab_used, s + 3 + g)
                nc.vector.tensor_tensor(run[0][:, STRIDE:], rstd[:, :], bank[2 + g][:, :], ALU.mult).then_inc(vec_done, 1)
                split_lo(s + 2 + g + RING)
                src = run[0]
                for n in range(g + 1):
                    own("nsa_in", f"sum{n}_{g}")
                    dst = run[1 + n % 2]
                    if g and n < 2:
                        dve.wait_ge(act_done, A.after("nsa_in", f"d_hi{g - 1}"))
                    nc.vector.tensor_tensor(dst[:, STRIDE:], src[:, STRIDE:], src[:, STRIDE - 2 ** n:STRIDE - 2 ** n + T],
                                            ALU.add).then_inc(vec_done, 1)
                    src = dst
                dst = run[1 + (g + 1) % 2]
                own("nsa_in", f"d{g}")
                nc.vector.scalar_tensor_tensor(dst[:, STRIDE:], src[:, STRIDE:], 2.0 ** -(g + 1), run[0][:, STRIDE:], ALU.mult,
                                               ALU.subtract).then_inc(vec_done, 1)
                own("nsa_in", f"early{g}")
                nc.vector.tensor_tensor(src[:, STRIDE:2 * STRIDE], src[:, STRIDE:2 * STRIDE],
                                        col("pool_inv", g * STRIDE, STRIDE), ALU.mult).then_inc(vec_done, 1)
                own("nsa_in", f"first{g}")
                nc.vector.tensor_tensor(dst[:, STRIDE:2 * STRIDE], src[:, STRIDE:2 * STRIDE], run[0][:, STRIDE:2 * STRIDE],
                                        ALU.subtract).then_inc(vec_done, 1)
                own("nsa_in", f"d_lo{g}")
                dve.wait_ge(act_done, A.after("nsa_in", f"d_hi{g}"))
                nc.vector.tensor_tensor(ns["o_lo"][:, 4 + g, :], dst[:, STRIDE:], ns["o_hi"][:, 4 + g, :].bitcast(F),
                                        ALU.subtract).then_inc(vec_done, 1)
            own("nsa_in", "gz")
            dve.wait_ge(pe_done, M.after("nsa_in", "gate"))
            dve.wait_ge(pool_done, G.after("nsa_in", "gates0"))
            nc.vector.tensor_tensor(ns["gates"][0:NGATE, :], rstd[0:NGATE, :], bank[6][0:NGATE, :], ALU.mult)\
                .then_inc(vec_done, 1)
            own("nsa_in", "cols")
            dve.wait_ge(pe_done, M.after("nsa_in", "cols"))
            nc.vector.tensor_copy(rstd_col[:, :], bank[7][:, 0:TT]).then_inc(vec_done, 1)
            s = SLAB_AT["nsa_proj"]
            for n in range(4):
                split_lo(s + n + RING)
                own("nsa_proj", f"q{n}")
                dve.wait_ge(slab_used, s + n + 1)
                nc.vector.scalar_tensor_tensor(ns["q_raw"][:, n, :], bank[n][:, :], DH ** -0.5, rstd[:, :],
                                               ALU.mult, ALU.mult).then_inc(vec_done, 1)
            for g in range(2):
                split_lo(s + 4 + g + RING)
                for b in range(2):
                    for h in range(2):
                        own("nsa_proj", f"k{g}{b}{h}")
                        dve.wait_ge(slab_used, s + 5 + g)
                        nc.vector.tensor_tensor(ns["k_raw"][h * DH:(h + 1) * DH, g, b, :], rstd[b * DH:(b + 1) * DH, :],
                                                bank[(4, 0)[g]][b * DH:(b + 1) * DH, :], ALU.mult).then_inc(vec_done, 1)
            for c in range(6, 8):
                split_lo(s + c + RING)
            s = SLAB_AT["nsa_cmp"]
            for c in range(6):
                split_lo(s + c + RING)
            for g in range(4):
                own("nsa_cmp", f"p_lo{g}")
                dve.wait_ge(act_done, A.after("nsa_cmp", f"p_hi{g}"))
                nc.vector.scalar_tensor_tensor(ns["o_lo"][:, 4 + g, :], bank[POOL_BANK[g]][:, :], col("pool_scale", g),
                                               ns["o_hi"][:, 4 + g, :].bitcast(F), ALU.mult, ALU.subtract)\
                    .then_inc(vec_done, 1)
            for h in range(2):
                own("nsa_cmp", f"kcl{h}")
                dve.wait_ge(act_done, A.after("nsa_cmp", f"kc{h}"))
                hs = slice(h * DH, (h + 1) * DH)
                nc.vector.tensor_tensor(ns["kc_lo"][hs, :, h, :], bank[2][hs, 0:64].rearrange("p (g n) -> p g n", g=2),
                                        ns["kc_hi"][hs, :, h, :].bitcast(F), ALU.subtract).then_inc(vec_done, 1)

            own("nsa_gates", "glo")
            dve.wait_ge(act_done, A.after("nsa_gates", "ghi"))
            nc.vector.tensor_tensor(ns["g_lo"][:, :], ns["gates"][:, :], ns["g_hi"][:, :].bitcast(F), ALU.subtract)\
                .then_inc(vec_done, 1)

            def nsa_group(i):
                name = "nsa_attn"
                one = ones[:, 0:1].rearrange("p (a b c) -> p a b c", a=1, b=1).broadcast_to([P, 3, 2, DH])
                for j in range(2):
                    own(name, f"gs{j}", i)
                    pick = mats[:, 0, bass.ds(12 * i + 6 * j, 6)].rearrange("p (h b o) -> p b h o", h=2, b=3)
                    nc.vector.tensor_tensor(ns["gsel"][:, 3 * j * P:3 * (j + 1) * P].rearrange("p (b h d) -> p b h d", b=3, h=2),
                                            pick.broadcast_to([P, 3, 2, DH]), one, ALU.mult).then_inc(vec_done, 1)
                for j in range(2):
                    own(name, f"q{j}lo", i)
                    dve.wait_ge(act_done, A.after(name, f"q{j}hi", i))
                    nc.vector.tensor_tensor(ns["q_lo"][j][:, :], ns["q_raw"][:, bass.ds(2 * i + j, 1), :],
                                            ns["q_hi"][j][:, :].bitcast(F), ALU.subtract).then_inc(vec_done, 1)

                def keys(b):
                    for h in range(2):
                        own(name, f"klo{b}{h}", i)
                        dve.wait_ge(act_done, A.after(name, f"khi{b}{h}", i))
                        hs = slice(h * DH, (h + 1) * DH)
                        nc.vector.tensor_tensor(ns["k_lo"][b][h][hs, :], ns["k_raw"][hs, bass.ds(i, 1), b, :],
                                                ns["k_hi"][b][h][hs, :].bitcast(F), ALU.subtract).then_inc(vec_done, 1)

                def selectors(u):
                    for h in range(2):
                        own(name, f"sel{h}.{u}", i)
                        nc.vector.tensor_scalar(ns["sel"][h][:, :], ones[:, :], mats[:, 0, bass.ds(4 * i + (u + h), 1)], None,
                                                ALU.mult).then_inc(vec_done, 1)

                keys(0)
                selectors(0)
                c = ns["cmp"][:, :]
                c3 = c.rearrange("p (r n) -> p r n", n=NCMPCOL)
                m = ns["cmp_m"][:, :]
                spread = m.rearrange("p (r o) -> p r o", o=1).broadcast_to([P, 16, NCMPCOL])
                own(name, "cs", i)
                dve.wait_ge(pe_done, M.after(name, "cs", i))
                dve.wait_ge(tables_loaded, 64)
                nc.vector.tensor_tensor(c, ns["tab"][:, bass.ds(i, 1), :], bank[0][:, :], ALU.add).then_inc(vec_done, 1)
                own(name, "cm", i)
                nc.vector.tensor_reduce(m, c3, AX, ALU.max, negate=True).then_inc(vec_done, 1)
                own(name, "cmin", i)
                nc.vector.tensor_scalar(m, m, 1e29, None, ALU.min).then_inc(vec_done, 1)
                own(name, "csub", i)
                nc.vector.tensor_tensor(c3, c3, spread, ALU.add).then_inc(vec_done, 1)
                keys(1)
                own(name, "csum", i)
                dve.wait_ge(act_done, A.after(name, "cexp", i))
                nc.vector.tensor_reduce(m, c3, AX, ALU.add).then_inc(vec_done, 1)
                own(name, "cmax", i)
                nc.vector.tensor_scalar(m, m, 1e-30, None, ALU.max).then_inc(vec_done, 1)
                own(name, "crec", i)
                nc.vector.reciprocal(m, m).then_inc(vec_done, 1)
                own(name, "cp", i)
                nc.vector.tensor_tensor(c3, c3, spread, ALU.mult).then_inc(vec_done, 1)

                def norm(u):
                    own(name, f"rc.{u}", i)
                    dve.wait_ge(act_done, A.after(name, f"s1.{u}", i))
                    nc.vector.reciprocal(ns["rec"][:, :], ns["rec"][:, :]).then_inc(vec_done, 1)
                    for h in range(2):
                        hs = slice(h * DH, (h + 1) * DH)
                        own(name, f"on{h}.{u}", i)
                        if u > 1:
                            dve.wait_ge(pool_done, G.after(name, f"gm.{u - 2}", i))
                        nc.vector.tensor_tensor(ns["o"][hs, :], ns["rec"][hs, :], bank[h][hs, :], ALU.mult)\
                            .then_inc(vec_done, 1)

                def out_lo(j):
                    own(name, f"olo{j}", i)
                    dve.wait_ge(act_done, A.after(name, f"ohi{j}", i))
                    nc.vector.tensor_tensor(ns["o_lo"][:, bass.ds(2 * i + j, 1), :], ns["g"][:, 3 * j, :],
                                            ns["o_hi"][:, bass.ds(2 * i + j, 1), :].bitcast(F), ALU.subtract)\
                        .then_inc(vec_done, 1)

                for u in range(4):
                    if u == 2:
                        selectors(2)
                    for h in range(2):
                        head_max(ns, name, h, f".{u}", i)
                    if u == 0:
                        for j in range(2):
                            own(name, f"acc{j}", i)
                            dve.wait_ge(pe_done, M.after(name, f"cpv{j}", i))
                            nc.vector.tensor_tensor(ns["g"][:, 3 * j, :], ns["g"][:, 3 * j, :], bank[j][:, :], ALU.mult)\
                                .then_inc(vec_done, 1)
                    if u:
                        norm(u)
                    if u == 3:
                        out_lo(0)
                norm(4)
                out_lo(1)

            with dve.Fori(0, 2) as i:
                nsa_group(i)
            out_layer("nsa_out", "ffn2_norm0")
            stats("sw0")
            glu_in("sw0_in", None)
            out_layer("sw0_out", "mix_norm1")

            stats("pw1")
            dve.wait_ge(pool_done, G.end("pw1.zero"))
            s = SLAB_AT["pw1"]
            with dve.Fori(0, KD // 2) as i:
                for c in range(2):
                    for n, step, dst in ((0, "ua", cf["a"]), (1, "ug", cf["gate"])):
                        own("pw1", f"{step}{c}", i)
                        dve.wait_ge(slab_used, s + 2 * c + n + 1 + i * 4)
                        nc.vector.tensor_tensor(dst[:, :], rstd[:, :], bank[2 * c + n][:, :], ALU.mult).then_inc(vec_done, 1)
                    own("pw1", f"wl{c}", i)
                    dve.wait_ge(act_done, A.after("pw1", f"wh{c}", i))
                    nc.vector.tensor_tensor(cf["w_lo"][c][:, 0:TAPS], cf["w"][c][:, :], cf["w_hi"][c][:, 0:TAPS].bitcast(F),
                                            ALU.subtract).then_inc(vec_done, 1)
                    split_lo(s + 2 * c + RING, i, 4)
                    own("pw1", f"z{c}", i)
                    dve.wait_ge(act_done, A.after("pw1", f"sg{c}", i))
                    nc.vector.scalar_tensor_tensor(cf["z"][c][:, TAPS - 1:], cf["a"][:, :], col("b_pw1", 2 * i + c),
                                                   cf["gate"][:, :], ALU.add, ALU.mult).then_inc(vec_done, 1)
                    split_lo(s + 2 * c + 1 + RING, i, 4)
                    own("pw1", f"zl{c}", i)
                    dve.wait_ge(act_done, A.after("pw1", f"zh{c}", i))
                    nc.vector.tensor_tensor(cf["z_lo"][c][:, TAPS - 1:], cf["z"][c][:, TAPS - 1:],
                                            cf["z_hi"][c][:, TAPS - 1:].bitcast(F), ALU.subtract).then_inc(vec_done, 1)
                    for k in range(1, TAPS - PE_TAPS):
                        own("pw1", f"t{k}_{c}", i)
                        if k == 1:
                            dve.wait_ge(act_done, A.after("pw1", f"t{c}", i))
                        nc.vector.scalar_tensor_tensor(cf["acc"][c][:, :], cf["z"][c][:, k:k + T], cf["w"][c][:, k:k + 1],
                                                       cf["acc"][c][:, :], ALU.mult, ALU.add).then_inc(vec_done, 1)
                    own("pw1", f"y{c}", i)
                    dve.wait_ge(pe_done, M.after("pw1", f"y{c}", i))
                    nc.vector.tensor_tensor(cf["y"][:, bass.ds(2 * i + c, 1), :], cf["acc"][c][:, :], bank[4 + c][:, :],
                                            ALU.add).then_inc(vec_done, 1)
            for n in range(KD):
                own("ln", f"xc{n}")
                dve.wait_ge(act_done, A.after("ln", "mean"))
                nc.vector.tensor_tensor(cf["y"][:, n, :], cf["y"][:, n, :], root[:, :], ALU.subtract).then_inc(vec_done, 1)
            own("ln", "rstd")
            dve.wait_ge(act_done, A.after("ln", "root"))
            nc.vector.reciprocal(rstd[:, :], root[:, :]).then_inc(vec_done, 1)
            for n in range(KD + 1):
                if n < KD:
                    own("ln", f"yn{n}")
                    nc.vector.tensor_tensor(cf["y"][:, n, :], cf["y"][:, n, :], rstd[:, :], ALU.mult).then_inc(vec_done, 1)
                if n:
                    own("ln", f"lo{n - 1}")
                    dve.wait_ge(act_done, A.after("ln", f"hi{n - 1}"))
                    nc.vector.tensor_tensor(cf["o_lo"][:, n - 1, :], cf["y"][:, n - 1, :], cf["o_hi"][:, n - 1, :].bitcast(F),
                                            ALU.subtract).then_inc(vec_done, 1)
            out_layer("pw2", "ffn2_norm1", bias="b_pw2")
            stats("sw1")
            glu_in("sw1_in", None)
            out_layer("sw1_out", None, False)
            stats("final")
            for n in range(KD):
                own("final", f"y{n}")
                nc.vector.scalar_tensor_tensor(x[:, n, :], x[:, n, :], col("final2", n), rstd[:, :], ALU.mult, ALU.mult)\
                    .then_inc(vec_done, 1)

        @block.tensor
        def _(pe):
            def mm(out, lhs, rhs, start, stop):
                return nc.tensor.matmul(out, lhs, rhs, start=start, stop=stop)

            def mm3(out, a, b, start, stop):
                mm(out, a[0], b[0], start, False)
                mm(out, a[0], b[1], False, False)
                return mm(out, a[1], b[0], False, stop)

            def wtile(slot, at, n=P):
                return w_hi[slot][:, at:at + n], w_lo[slot][:, at:at + n]

            def chunk(pair, n):
                return pair[0][:, n, :], pair[1][:, n, :]

            def tile_of(name, out, s0, moving, parts=(KD,), turn=0, per=0, needs=None):
                k = 0
                total = sum(parts)
                for j, n in enumerate(parts):
                    pe.wait_ge(lo_ready, s0 + j + 1 + turn * per)
                    for c in range(n):
                        wait = needs(k) if needs else None
                        if wait:
                            pe.wait_ge(*wait)
                        last = mm3(out, wtile((s0 + j) % RING, c * P), chunk(moving, k), k == 0, k == total - 1)
                        k += 1
                    last.then_inc(slab_used, 1)

            def stats(name, summed, cols_too=False):
                pe.wait_ge(pool_done, G.end(summed))
                mm(bank[7][:, :], ones[:, :], sq_sum[:, :], True, True).then_inc(pe_done, 1)
                if cols_too:
                    for t in range(TT):
                        last = mm(bank[6][:, t:t + 1], sq_sum[:, t * P:(t + 1) * P], ones[:, 0:1], True, True)
                    last.then_inc(pe_done, 1)

            h = (h_hi, h_lo)
            s = SLAB_AT["fox_v"]

            def fox_v_half(half):
                for c in range(4):
                    pe.wait_ge(lo_ready, s + 4 * half + c + 1)
                    for k in (2 * c, 2 * c + 1):
                        if half == 0:
                            pe.wait_ge(vec_done, V.after("x_in", f"lo{k}"))
                        for t in range(TT):
                            tok = slice(t * P, (t + 1) * P)
                            last = mm3(bank[4 * half + t][:, :], (h_hi[:, k, tok], h_lo[:, k, tok]),
                                       wtile((s + c) % RING, (k % 2) * T, T), k == 0, k == KD - 1)
                    last.then_inc(slab_used, 1)

            fox_v_half(0)
            stats("fox", "x_in", True)
            pe.wait_ge(act_done, A.after("fox.stat", "root_cols"))
            fox_v_half(1)
            pe.wait_ge(vec_done, V.after("init", "side"))
            pe.wait_ge(act_done, A.after("fox_v", "v0t0"))
            for k in range(KD):
                at = SIDE["w_f"] + k * FOX_H
                last = mm3(bank[0][0:FOX_H, :], (side_hi[:, at:at + FOX_H], side_lo[:, at:at + FOX_H]), chunk(h, k),
                           k == 0, k == KD - 1)
            last.then_inc(pe_done, 1)

            def fox_proj(s0, turn, per):
                tile_of("fox", bank[2][:, :], s0, h, turn=turn, per=per)
                tile_of("fox", bank[3][:, :], s0 + 1, h, turn=turn, per=per)

            def max_scores(b, h, qs, ks, table=None, mask=0):
                for n, bk, at in MAX_TILES:
                    w = (n + 1) * P
                    out = bank[SLOT[h][bk]][:, at:at + w]
                    for j, (q, k) in enumerate(zip(qs, ks)):
                        mm(out, q[:, n * P:(n + 1) * P], k[:, 0:w], j == 0, False)
                    if table is not None:
                        mm(out, b["sel"][h][:, :], table[:, 0:w], False, False)
                    last = mm(bank[SLOT[h][bk]][:, at + n * P:at + w], ident_r[:, :], mask_r[mask][:, :], False, True)
                    if n != 2:
                        last.then_inc(pe_done, 1)

            def scores(b, h, pairs, mask=0):
                for n, bk, at in SCORE_TILES:
                    w = (TT - n) * P
                    out = bank[SLOT[h][bk]][:, at:at + w]
                    keys, queries = slice(n * P, (n + 1) * P), slice(n * P, T)
                    for j, (k, q) in enumerate(pairs):
                        mm3(out, (k[0][:, keys], k[1][:, keys]), (q[0][:, queries], q[1][:, queries]), j == 0, False)
                    mm(out, ones_r[:, :], b["diag"][h][:, n:TT, :], False, False)
                    last = mm(bank[SLOT[h][bk]][:, at:at + P], mask_r[mask][:, :], ident_r[:, :], False, True)
                    if n != 1:
                        last.then_inc(pe_done, 1)

            def values(out, v, prob):
                for n in range(TT):
                    last = mm(out[:, n * P:T], v(n), prob[:, PROB_AT[n]:PROB_AT[n] + (TT - n) * P], n == 0, n == TT - 1)
                return last

            def fox_pv(h):
                last = values(bank[h][:, :], lambda n: fx["vp"][:, n, h, :], fx["prob"][h])
                last.then_inc(pe_done, 1)

            def fox_max(name, sfx, turn, h):
                pe.wait_ge(vec_done, V.after(name, f"sel{h}{sfx}", turn))
                max_scores(fx, h, [fx["q_hi"]], [fx["k_hi"][h]], fx["negc_r"])

            def fox_scores(name, sfx, turn, h):
                pe.wait_ge(vec_done, V.after("fox_first_max" if name == "fox_first" else name, f"dg{h}{sfx}", turn))
                scores(fx, h, [((fx["k_hi"][h], fx["k_lo"][h]), (fx["q_hi"], fx["q_lo"]))])

            s = SLAB_AT["fox_qk"]
            pe.wait_ge(act_done, A.after("fox_v", f"v1t{TT - 1}"))
            fox_proj(s, 0, 0)
            pe.wait_ge(vec_done, V.after("fox_v", "scan"))
            for t in range(TT):
                last = mm(bank[1][:, t * FOX_H:(t + 1) * FOX_H], fx["negc"][0:FOX_H, t * P:(t + 1) * P],
                          ident[0:FOX_H, 0:FOX_H], True, True)
            last.then_inc(pe_done, 1)
            pe.wait_ge(pool_done, G.after("fox_v", "zk1h"))
            pe.wait_ge(act_done, A.after("fox_first", "khi1"))
            for h_ in range(2):
                fox_max("fox_first", "", 0, h_)
            for h_ in range(2):
                fox_scores("fox_first", "", 0, h_)

            def fox_step(name, sfx, turn, s0, per):
                pe.wait_ge(act_done, A.after(name, "qhi" + sfx, turn) - 1 - 5)
                fox_proj(s0, turn, per)
                pe.wait_ge(pool_done, G.after(name, "vp0" + sfx, turn) - 1)
                pe.wait_ge(act_done, A.after(name, "qhi" + sfx, turn) - 1)
                pe.wait_ge(vec_done, V.after(name, "qt" + sfx, turn) - 2)
                fox_pv(0)
                pe.wait_ge(act_done, A.after(name, "khi1" + sfx, turn))
                fox_max(name, sfx, turn, 0)
                fox_max(name, sfx, turn, 1)
                fox_pv(1)
                fox_scores(name, sfx, turn, 0)
                fox_scores(name, sfx, turn, 1)

            with pe.Fori(0, 3) as i:
                for c in range(2):
                    fox_step("fox_loop", f".{c}", i, s + 2 + 2 * c, 4)
            fox_step("fox_peel", ".0", 0, s + 14, 0)
            def out_layer(name, moving, needs):
                parts = OUT[name]
                s0 = SLAB_AT[name]
                for n in range(KD):
                    if n >= 2:
                        pe.wait_ge(vec_done, V.after(name, f"x{(n - 2) % 4}", (n - 2) // 4))
                    tile_of(name, bank[4 + n % 2][:, :], s0 + n * len(parts), moving, parts,
                            needs=needs if n == 0 else None)

            def glu_in(name, moving, source, stat):
                def turn(i):
                    for c in range(2):
                        for n, step in ((0, "ug"), (1, "uv")):
                            first = isinstance(i, int) and c == 0 and n == 0
                            if not isinstance(i, int):
                                pe.wait_ge(vec_done, V.after(name, f"{step}{c}", i) - len(V.steps[name]))
                            tile_of(name, bank[2 * c + n][:, :], SLAB_AT[name] + 2 * c + n, moving, (KD,), i, 4,
                                    source if first else None)
                            if first:
                                stats(*stat)

                turn(0)
                with pe.Fori(1, KH // 2) as i:
                    turn(i)

            def normed(name):
                return lambda k: (vec_done, V.after(name, f"lo{k % 4}", k // 4))

            def glu(name):
                return lambda k: (vec_done, V.after(name, f"lo{k % 2}", k // 2)) if k in (0, 19, 20, 21) else None

            def fox_last(k):
                if k == 1:
                    pe.wait_ge(act_done, A.after("fox_peel", "exp1t2.0"))
                    pe.wait_ge(pool_done, G.end("fox_peel"))
                    pe.wait_ge(vec_done, V.end("fox_peel"))
                    fox_pv(0)
                    fox_pv(1)
                return {0: (vec_done, V.end("fox_peel")), KD - 1: (vec_done, V.end("fox_last"))}.get(k)

            pe.wait_ge(act_done, A.after("fox_peel", "exp0t2.0"))
            out_layer("fox_out", fox_o, fox_last)
            glu_in("ffn0_in", h, normed("fox_out"), ("ffn0", "fox_out"))
            out_layer("ffn0_out", (act_hi, act_lo), glu("ffn0_in"))

            hq = (ml["o_hi"], ml["o_lo"])

            def q_sum(j):
                if j == 0:
                    pe.wait_ge(act_done, A.after("mla_kvq", "root_l"))
                pe.wait_ge(act_done, A.after("mla_kvq", f"q_sq{j}"))
                mm(bank[7][:, :], ones[:, :], sq[j % 2][:, :], j == 0, j == KQ - 1).then_inc(pe_done, 1)

            for i in range(9 * KD):
                t, k = divmod(i, KD)
                s, at = divmod(i, 6)
                s += SLAB_AT["mla_kvq"]
                if at == 0:
                    pe.wait_ge(lo_ready, s + 1)
                if t == 0:
                    pe.wait_ge(*normed("ffn0_out")(k))
                if t == 3:
                    pe.wait_ge(vec_done, V.after("mla_kvq", f"h_lo{k}"))
                if k == 0 and t >= 7:
                    pe.wait_ge(vec_done, V.after("mla_kvq", f"l{t - 7}"))
                last = mm3(bank[KVQ_BANK[t]][:, :], wtile(s % RING, at * P), chunk(h if t < 3 else hq, k), k == 0,
                           k == KD - 1)
                if at == 5:
                    last.then_inc(slab_used, 1)
                elif k == KD - 1:
                    last.then_inc(pe_done, 1)
                if t == 0 and k == KD - 1:
                    stats("mla", "ffn0_out")
                if t >= 4 and k == KD - 1:
                    q_sum(t - 4)
                if t == 2 and k == KD - 1:
                    for j in range(KL):
                        pe.wait_ge(act_done, A.after("mla_kvq", f"sq_l{j}"))
                        last = mm(bank[7][:, :], ones[:, :], sq[j][:, :], j == 0, j == KL - 1)
                    last.then_inc(pe_done, 1)

            ql, lat = (ml["ql_hi"], ml["ql_lo"]), (ml["l_hi"], ml["l_lo"])

            def mla_step(name, turn, s0, per, prev, first=False):
                if prev:
                    pe.wait_ge(act_done, A.after(name, "n0hi", turn) - 1 - 6)
                for n in range(3):
                    tile_of(name, bank[2 + n][:, :], s0 + n, ql, (KQ,), turn, per,
                            (lambda k: (vec_done, V.after("mla_kvq", f"q_lo{k}"))) if first and n == 0 else None)
                    if first and n == 0:
                        q_sum(KQ - 1)
                if prev:
                    pe.wait_ge(act_done, A.after(name, "n0hi", turn) - 1 - 2)
                pe.wait_ge(lo_ready, s0 + 4 + turn * per)
                kv = (s0 + 3) % RING
                for hd in range(2):
                    for k in range(KL):
                        last = mm3(bank[5 + hd][:, :], wtile(kv, (KL * hd + k) * P), chunk(lat, k), k == 0, k == KL - 1)
                    last.then_inc(pe_done, 1)
                if prev:
                    pe.wait_ge(act_done, A.after(name, "n0hi", turn) - 1)
                    pe.wait_ge(pool_done, G.after(name, "s0a", turn) - 1)
                    mla_pv(0)
                pe.wait_ge(act_done, A.after(name, "k1hi", turn))
                for hd in range(2):
                    if hd == 1:
                        pe.wait_ge(vec_done, V.after(name, "k1lo", turn))
                    max_scores(ml, hd, [ml["qn_hi"][hd], ml["qr_hi"]], [ml["k_hi"][hd], ml["kr_hi"][hd]], None, 1)
                if prev:
                    pe.wait_ge(vec_done, V.after(name, "on0", turn))
                    mla_pv(1)
                for hd in range(2):
                    pe.wait_ge(vec_done, V.after(name, f"dg{hd}", turn))
                    scores(ml, hd, [((ml["k_hi"][hd], ml["k_lo"][hd]), (ml["qn_hi"][hd], ml["qn_lo"][hd])),
                                    ((ml["kr_hi"][hd], ml["kr_lo"][hd]), (ml["qr_hi"], ml["qr_lo"]))], 1)
                if prev:
                    pe.wait_ge(vec_done, V.after(name, "on1", turn))
                for t in range(TT):
                    tok = slice(t * P, (t + 1) * P)
                    for k in range(KL):
                        last = mm3(bank[t // 2][:, (t % 2) * 2 * P:(t % 2 + 1) * 2 * P], (lat[0][:, k, tok], lat[1][:, k, tok]),
                                   wtile(kv, (2 * KL + 2 * k) * P, 2 * P), k == 0, k == KL - 1)
                last.then_inc(slab_used, 1)

            def mla_pv(hd):
                values(bank[1][:, :], lambda n: ml["v"][:, n, hd, :], ml["prob"][hd]).then_inc(pe_done, 1)
                mm(bank[0][:, :], ones[:, :], ml["psum"][hd][:, :], True, True).then_inc(pe_done, 1)

            for half in "ab":
                s = SLAB_AT["mla_" + half]
                name = f"mla_{half}_"
                if half == "b":
                    pe.wait_ge(vec_done, V.end("mla_out_a"))
                mla_step(name + "first", 0, s, 0, False, half == "a")
                with pe.Fori(0, 3) as i:
                    mla_step(name + "loop", i, s + 4, 4, True)

                def last_pair(k):
                    if k == 1:
                        pe.wait_ge(pool_done, G.end(name + "loop"))
                        pe.wait_ge(act_done, A.end(name + "loop"))
                        mla_pv(0)
                    if k == 4:
                        pe.wait_ge(vec_done, V.after(name + "last", "on0"))
                        mla_pv(1)
                    return {0: (vec_done, V.end(name + "loop")), 6: (vec_done, V.after(name + "last", "olo0")),
                            7: (vec_done, V.after(name + "last", "olo1"))}.get(k)

                pe.wait_ge(act_done, A.end(name + "loop") - 3)
                out_layer("mla_out_" + half, hq, last_pair)
            glu_in("ffn1_in", h, normed("mla_out_b"), ("ffn1", "mla_out_b"))
            out_layer("ffn1_out", (act_hi, act_lo), glu("ffn1_in"))

            s = SLAB_AT["nsa_in"]
            for n in range(6):
                tile_of("nsa", bank[n][:, :], s + n, h, needs=normed("ffn1_out") if n == 0 else None)
                if n == 0:
                    pe.wait_ge(pool_done, G.end("ffn1_out"))
                    mm(bank[7][:, :], ones[:, :], sq_sum[:, :], True, True).then_inc(pe_done, 1)
                    mm(bank[6][:, :], ones[:, :], u[0][:, 0:T], True, True).then_inc(pe_done, 1)
            pe.wait_ge(vec_done, V.after("x2", "ms"))
            for k in range(KD):
                at = SIDE["w_gate"] + k * NGATE
                last = mm3(bank[6][0:NGATE, :], (side_hi[:, at:at + NGATE], side_lo[:, at:at + NGATE]), chunk(h, k),
                           k == 0, k == KD - 1)
            last.then_inc(pe_done, 1)
            pe.wait_ge(vec_done, V.after("x2", "rstd"))
            for t in range(TT):
                last = mm(bank[7][:, t:t + 1], rstd[:, t * P:(t + 1) * P], ident[:, 0:1], True, True)
            last.then_inc(pe_done, 1)
            s = SLAB_AT["nsa_proj"]
            for n, (b, free) in enumerate([(0, V.after("nsa_in", "bk11")), (1, V.after("nsa_in", "bv11")),
                                           (2, V.after("nsa_in", "u0")), (3, V.after("nsa_in", "u1")),
                                           (4, V.after("nsa_in", "u2")), (0, V.after("nsa_proj", "q0"))]):
                pe.wait_ge(vec_done, free)
                tile_of("nsa", bank[b][:, :], s + n, h)
            pe.wait_ge(vec_done, V.after("nsa_in", "gz"))
            pe.wait_ge(lo_ready, s + 8)
            for t in range(TT):
                tok = slice(t * P, (t + 1) * P)
                for k in range(KD):
                    last = mm3(bank[5 + t // 2][:, (t % 2) * 2 * P:(t % 2 + 1) * 2 * P], (h_hi[:, k, tok], h_lo[:, k, tok]),
                               wtile((s + 6 + k // 4) % RING, (k % 4) * 2 * P, 2 * P), k == 0, k == KD - 1)
            last.then_inc(slab_used, 2)
            s = SLAB_AT["nsa_cmp"]
            pe.wait_ge(vec_done, V.after("nsa_proj", "q3"))
            for n, kv in enumerate("kv"):
                b = [ns[z][n][:, :, :, :].rearrange("p j g n -> p j (g n)") for z in ("b_hi", "b_lo")]
                tile_of("nsa", bank[(7, 1)[n]][:, 0:64], s + 2 * n, b, (KD, KD))
            ob = (ns["o_hi"], ns["o_lo"])
            pe.wait_ge(vec_done, V.end("nsa_proj"))
            pe.wait_ge(act_done, A.end("nsa_proj"))
            for n in range(4):
                if n % 2 == 0:
                    pe.wait_ge(lo_ready, s + 5 + n // 2)
                last = mm3(bank[POOL_BANK[n]][:, :], wtile((s + 4 + n // 2) % RING, (n % 2) * P), chunk(ob, 4 + n), True, True)
                if n % 2:
                    last.then_inc(slab_used, 1)
            pe.wait_ge(tables_loaded, 64)
            for n in range(2):
                pe.wait_ge(act_done, A.after("nsa_cmp", "gelu_" + "kv"[n]))
                if n == 0:
                    mm(bank[2][:, 0:64], ns["w2"][:, 0:P], ns["gh"][0][:, :, :].rearrange("p g n -> p (g n)"), True, True)\
                        .then_inc(pe_done, 1)
                else:
                    for g in range(2):
                        last = mm(bank[3][0:NCMPCOL, g * DH:(g + 1) * DH], ns["gh"][1][:, g, :],
                                  ns["w2"][:, P:P + DH], True, True)
                    last.then_inc(pe_done, 1)

            def nsa_group(i):
                name = "nsa_attn"
                pe.wait_ge(vec_done, V.after(name, "gs1", i))
                for n in range(6):
                    for z in range(2):
                        last = mm(bank[2 + n][:, :], ns["gsel"][:, n * P:(n + 1) * P], ns[("g_hi", "g_lo")[z]][:, :],
                                  z == 0, z == 1)
                last.then_inc(pe_done, 1)
                pe.wait_ge(vec_done, V.after(name, "q1lo", i))
                for j in range(2):
                    for t in range(TT):
                        tok = slice(t * P, (t + 1) * P)
                        k = [ns[z][:, bass.ds(i, 1), :, :].rearrange("p o h n -> p (o h n)") for z in ("kc_hi", "kc_lo")]
                        at = (j * TT + t) * 2 * NCMPCOL
                        last = mm3(bank[0][:, at:at + 2 * NCMPCOL], (ns["q_hi"][j][:, tok], ns["q_lo"][j][:, tok]), k,
                                   True, True)
                last.then_inc(pe_done, 1)
                pe.wait_ge(act_done, A.after(name, "g5", i))

                def compressed():
                    pe.wait_ge(vec_done, V.after(name, "cp", i))
                    for j in range(2):
                        for t in range(TT):
                            at = (j * TT + t) * 2 * NCMPCOL
                            last = mm(bank[j][0:2 * NCMPCOL, t * P:(t + 1) * P], ns["cmp"][:, at:at + 2 * NCMPCOL], ident,
                                      True, True)
                    last.then_inc(pe_done, 1)
                    for j in range(2):
                        pe.wait_ge(act_done, A.after(name, f"pt{j}", i))
                        mm(bank[j][:, :], ns["vcg"][:, :], turned[j], True, True).then_inc(pe_done, 1)

                def pv(u, h_):
                    values(bank[h_][:, :], lambda n: ns["v"][:, n, u % 2, h_, :], ns["prob"][h_])\
                        .then_inc(pe_done, 1)

                for u in range(5):
                    j, b = u // 2, u % 2
                    if u:
                        pe.wait_ge(act_done, A.after(name, f"exp1t2.{u - 1}", i))
                        pe.wait_ge(vec_done, V.after(name, f"on1.{u - 1}" if u > 1 else "acc1", i))
                        if u == 1:
                            pe.wait_ge(pool_done, G.after(name, "vz1", i))
                        pv(u - 1, 0)
                    if u < 4:
                        pe.wait_ge(vec_done, V.after(name, f"sel1.{u - u % 2}", i))
                        for h_ in range(2):
                            max_scores(ns, h_, [ns["q_hi"][j]], [ns["k_hi"][b][h_]], ns["table"])
                    if u:
                        pv(u - 1, 1)
                    if u < 4:
                        for h_ in range(2):
                            pe.wait_ge(vec_done, V.after(name, f"dg{h_}.{u}", i))
                            scores(ns, h_, [((ns["k_hi"][b][h_], ns["k_lo"][b][h_]), (ns["q_hi"][j], ns["q_lo"][j]))])
                    if u == 0:
                        compressed()

            pe.wait_ge(act_done, A.end("nsa_cmp"))
            pe.wait_ge(pool_done, G.after("nsa_attn.zero", "k7"))
            with pe.Fori(0, 2) as i:
                nsa_group(i)
            out_layer("nsa_out", ob, lambda k: (vec_done, V.end("nsa_attn")) if k == 0 else None)
            glu_in("sw0_in", h, normed("nsa_out"), ("sw0", "nsa_out"))
            out_layer("sw0_out", (act_hi, act_lo), glu("sw0_in"))

            s = SLAB_AT["pw1"]

            def pw1_tiles(c, turn, first=False):
                for n in range(2):
                    if not first:
                        pe.wait_ge(vec_done, V.after("pw1", ("ua", "ug")[n] + str(c), turn) - len(V.steps["pw1"]))
                    tile_of("pw1", bank[2 * c + n][:, :], s + 2 * c + n, h, (KD,), turn, 4,
                            normed("sw0_out") if first and n == 0 else None)
                    if first and n == 0:
                        stats("pw1", "sw0_out")

            def pw1_taps(c, turn):
                pe.wait_ge(vec_done, V.after("pw1", f"zl{c}", turn))
                pe.wait_ge(pool_done, G.after("pw1", f"dl{c}", turn))
                for k in range(PE_TAPS):
                    t = TAPS - PE_TAPS + k
                    last = mm3(bank[4 + c][:, :], [d[:, k, :] for d in cf["diag"][c]],
                               [cf[z][c][:, t:t + T] for z in ("z_hi", "z_lo")], k == 0, k == PE_TAPS - 1)
                last.then_inc(pe_done, 1)

            pw1_tiles(0, 0, True)
            with pe.Fori(0, KD // 2 - 1) as i:
                pw1_tiles(1, i)
                pw1_taps(0, i)
                pw1_tiles(0, i + 1)
                pw1_taps(1, i)
            pw1_tiles(1, KD // 2 - 1)
            pw1_taps(0, KD // 2 - 1)
            pw1_taps(1, KD // 2 - 1)
            pe.wait_ge(pool_done, G.end("pw1"))
            mm(bank[7][:, :], ones[:, :], sq_sum[:, :], True, True).then_inc(pe_done, 1)
            for n in range(KD):
                pe.wait_ge(act_done, A.after("ln", f"sq{n}"))
                mm(bank[7][:, :], ones[:, :], sq[n % 2][:, :], n == 0, n == KD - 1).then_inc(pe_done, 1)
            out_layer("pw2", (cf["o_hi"], cf["o_lo"]), lambda k: (vec_done, V.after("ln", f"lo{k}")))
            glu_in("sw1_in", h, normed("pw2"), ("sw1", "pw2"))
            out_layer("sw1_out", (act_hi, act_lo), glu("sw1_in"))
            stats("final", "sw1_out")


OUT = {
    "fox_out": (KD,), "ffn0_out": HID_SPLIT, "mla_out_a": (KD,),
    "mla_out_b": (KD,), "ffn1_out": HID_SPLIT, "nsa_out": (KD,),
    "sw0_out": HID_SPLIT, "pw2": (KD,), "sw1_out": HID_SPLIT,
}


def tiles_in_order(w):
    k, n = w.shape
    return [w[a:a + P, b:b + P] for b in range(0, n, P) for a in range(0, k, P)]


def pack(tiles, per_slab):
    out, at = [], 0
    for n in per_slab:
        slab = np.zeros((P, SLAB), np.float32)
        part = np.concatenate([np.ascontiguousarray(x) for x in tiles[at:at + n]], axis=1)
        slab[:, :part.shape[1]] = part
        out.append(slab)
        at += n
    assert at == len(tiles)
    return out


def interleave(a, b, n=1):
    return [s for i in range(0, len(a), n) for s in a[i:i + n] + b[i:i + n]]


def weight_stream(w):
    ws = {}
    fin = w["w_fox_in"][0]
    v = fin[:, 2048:3072]
    ws["fox_v"] = pack([v[k * P:(k + 1) * P, h * T:(h + 1) * T] for h in range(2) for k in range(KD)], [2] * 8)
    q, k = pack(tiles_in_order(fin[:, 0:1024]), [8] * 8), pack(tiles_in_order(fin[:, 1024:2048]), [8] * 8)
    ws["fox_qk"] = interleave(q, k)
    ws["fox_out"] = pack(tiles_in_order(w["w_fox_out"][0]), [8] * 8)
    ckv, half = w["w_dkv"], ROPE // 2
    x1, x2 = ckv[:, LAT:LAT + half], ckv[:, LAT + half:]
    ws["mla_kvq"] = pack(tiles_in_order(ckv[:, :LAT]) + tiles_in_order(np.concatenate([x1, x1, x2, x2], axis=1))
                         + tiles_in_order(w["w_dq"][0]), [6] * 12)
    uq = w["w_uq"][0].reshape(QLAT, MLA_H, NOPE + ROPE)
    pairs = []
    for p in range(0, MLA_H, 2):
        for h in (p, p + 1):
            pairs += pack(tiles_in_order(uq[:, h, :NOPE]), [KQ])
        rope = [uq[:, h, NOPE + o:NOPE + o + half] for o in (0, half) for h in (p, p + 1)]
        pairs += pack(tiles_in_order(np.concatenate(rope, axis=1)), [KQ])
        v = w["w_uv"][:, p * P:(p + 2) * P]
        pairs += pack(tiles_in_order(w["w_uk"][:, p * P:(p + 2) * P]) + [v[:P], v[P:]], [3 * KL])
    ws["mla_a"], ws["mla_b"] = pairs[:16], pairs[16:]
    o = w["w_mla_out"][0]
    ws["mla_out_a"] = pack(tiles_in_order(o[:D]), [8] * 8)
    ws["mla_out_b"] = pack(tiles_in_order(o[D:]), [8] * 8)
    a = w["nsa_w_in_2"][0]

    def piece(at, n):
        return tiles_in_order(a[:, at:at + n])

    ws["nsa_in"] = pack(piece(512, 2 * P) + piece(1304, T), [8] * 6)
    ws["nsa_cmp"] = pack([t for z in "kv" for t in tiles_in_order(w[f"cmp_{z}_w1_2"][0])], [8] * 4) \
        + pack([w["pool_w_2"][0, g] for g in range(4)], [2, 2])
    ws["pw1"] = interleave(pack(tiles_in_order(w["conv_w_pw1_2"][0][:, :D]), [8] * 8),
                           pack(tiles_in_order(w["conv_w_pw1_2"][0][:, D:]), [8] * 8))
    ws["pw2"] = pack(tiles_in_order(w["conv_w_pw2_2"][0]), [8] * 8)
    def both(at, g):
        return np.concatenate([a[:, at + g * DH:at + (g + 1) * DH], a[:, at + 2 * P + g * DH:at + 2 * P + (g + 1) * DH]], axis=1)

    v = np.concatenate([both(896, 0), both(896, 1)], axis=1)
    ws["nsa_proj"] = pack(piece(0, 4 * P) + tiles_in_order(both(768, 0)) + tiles_in_order(both(768, 1)), [8] * 6) \
        + pack([v[k * P:(k + 1) * P] for k in range(KD)], [4, 4])
    ws["nsa_out"] = pack(tiles_in_order(w["mix_w_out_2"][0]), [8] * 8)
    for n in range(2):
        a = w["w_ffn_in"][n]
        ws[f"ffn{n}_in"] = interleave(pack(tiles_in_order(a[:, :HID]), [8] * KH), pack(tiles_in_order(a[:, HID:]), [8] * KH))
        ws[f"ffn{n}_out"] = pack(tiles_in_order(w["w_ffn_out"][n]), list(HID_SPLIT) * 8)
        a, b = w["ffn_w_gate_2"][n], w["ffn_w_up_2"][n]
        ws[f"sw{n}_in"] = interleave(pack(tiles_in_order(a), [8] * KH), pack(tiles_in_order(b), [8] * KH))
        ws[f"sw{n}_out"] = pack(tiles_in_order(w["ffn_w_down_2"][n]), list(HID_SPLIT) * 8)
    return ws


def by_chunk(a):
    return np.ascontiguousarray(a.reshape(-1, P).T)


def conv_cols(w, b):
    return np.stack([by_chunk(w[0]), by_chunk(w[1]), by_chunk(w[2]), by_chunk(b)], axis=2).reshape(P, -1)


def constants(w):
    cols = np.zeros((P, NCOLS), np.float32)

    def put(name, a):
        cols[:a.shape[0], COLS[name]:COLS[name] + a.shape[1]] = a

    for name, a in [
        ("fox_norm", w["fox_norm"][0]), ("kv_in_norm", w["kv_in_norm"]), ("kv_norm", w["kv_norm"]),
        ("mla_norm", w["mla_norm"][0]), ("q_norm", w["q_norm"][0]), ("ffn_norm0", w["ffn_norm"][0]),
        ("ffn_norm1", w["ffn_norm"][1]), ("final_norm", w["final_norm"]), ("mix_norm0", w["mix_norm_2"][0]),
        ("mix_norm1", w["mix_norm_2"][1]), ("ffn2_norm0", w["ffn_norm_2"][0]), ("ffn2_norm1", w["ffn_norm_2"][1]),
        ("final2", w["final_norm_2"]), ("pool_scale", w["pool_scale_2"][0]), ("b_pw1", w["conv_b_pw1_2"][0]),
        ("b_dw", w["conv_b_dw_2"][0]), ("ln_g", w["conv_ln_g_2"][0]), ("ln_b", w["conv_ln_b_2"][0]),
        ("b_pw2", w["conv_b_pw2_2"][0]),
    ]:
        put(name, by_chunk(a))
    put("b_fox", w["b_fox_f"][0][:, None])
    for n in range(2):
        put(f"conv{n}", conv_cols(w["ffn_conv_w"][n], w["ffn_conv_b"][n]))
    put("w_dw", w["conv_w_dw_2"][0].reshape(TAPS, KD, P).transpose(2, 1, 0).reshape(P, -1))
    put("cmp_pos_k", by_chunk(w["cmp_pos_k_2"][0].reshape(-1)))
    put("cmp_pos_v", by_chunk(w["cmp_pos_v_2"][0].reshape(-1)))
    f = np.arange(P)
    put("rope_pick", np.stack([(f // 32) % 2 == 0, (f // 32) % 2 == 1], axis=1).astype(np.float32))
    slope = 2.0 ** -np.arange(1, NSA_H + 1, dtype=np.float32)
    pos = np.arange(T).reshape(TT, P).T
    a = (pos[:, :, None] * slope).reshape(P, TT, 2, NSA_H // 2).transpose(0, 2, 1, 3)
    put("alibi", a.reshape(P, -1).astype(np.float32))
    tok = np.arange(STRIDE)
    inv = np.concatenate([1.0 / np.minimum(tok + 1, 2 ** (g + 1)) for g in range(4)]).astype(np.float32)
    put("pool_inv", np.tile(inv, (P, 1)))
    put("eps", np.full((P, 1), 1e-6, np.float32))
    put("eps_ln", np.full((P, 1), 1e-5, np.float32))

    mats = np.zeros((P, 3, P), np.float32)
    q, k = np.arange(P)[:, None], np.arange(P)[None, :]
    mats[:, 0] = np.eye(P)
    mats[:, 1] = np.where(k > q, NEG, 0)
    mats[:, 2] = np.where(k >= (q // SEL + 1) * SEL, NEG, 0)
    end = np.arange(NCMPCOL) * STRIDE + CMP - 1
    tok = np.arange(T).reshape(TT, P).T
    hidden = (end[None, None, :] > tok[:, :, None]) | (np.arange(NCMPCOL) >= NCMP)
    tab = np.where(hidden[:, None, :, None, :], NEG, slope.reshape(1, NSA_H // 2, 1, 2, 1) * end).astype(np.float32)
    tab = np.ascontiguousarray(tab.reshape(P, -1))

    pos = np.arange(T, dtype=np.float32)
    inv = (10000.0 ** (-np.arange(0, ROPE, 2, dtype=np.float32) / ROPE)).astype(np.float32)
    ang = inv[:, None] * pos[None, :]
    cos, sin = np.cos(ang).astype(np.float32), np.sin(ang).astype(np.float32)
    rows = np.zeros((P, 3, T), np.float32)
    rows[:, 0, :T] = np.concatenate([cos] * 4)
    rows[:, 1, :T] = np.concatenate([-sin, -sin, sin, sin])
    rows[:NSA_H, 2, :] = slope[:, None] * np.arange(T)[None, :]
    return cols, mats, rows, tab


def side_weights(w):
    side = np.zeros((P, NSIDE), np.float32)

    def put(name, a):
        side[:, SIDE[name]:SIDE[name] + a.shape[1]] = a

    f = w["w_fox_in"][0][:, 3072:]
    put("w_f", f.reshape(KD, P, FOX_H).transpose(1, 0, 2).reshape(P, -1))
    g = w["nsa_w_in_2"][0][:, 1280:1304]
    put("w_gate", g.reshape(KD, P, 24).transpose(1, 0, 2).reshape(P, -1))
    side[:, SIDE["w2"]:SIDE["w2"] + P + DH] = np.concatenate([w["cmp_k_w2_2"][0]] * 2 + [w["cmp_v_w2_2"][0]], axis=1)
    return side


def kernel(**inputs):
    import concourse.bacc as bacc
    from concourse.bass_utils import run_bass_kernel_spmd

    w = {k: np.asarray(v) for k, v in inputs.items()}
    arrays = layout(w)
    nc = bacc.Bacc("TRN2", target_bir_lowering=False, num_devices=1)
    aps = [nc.dram_tensor(n, a.shape, F, kind="ExternalInput").ap() for n, a in arrays.items()]
    out = nc.dram_tensor("out_t", (P, KD, T), F, kind="ExternalOutput").ap()
    build(nc, *aps, out)
    r = run_bass_kernel_spmd(nc, [arrays], core_ids=[0])
    y = r.results[0]["out_t"]
    return np.ascontiguousarray(y.transpose(2, 1, 0).reshape(1, T, D))


def layout(w):
    ws = weight_stream(w)
    stream = np.zeros((NSLABS, P, SLAB), np.float32)
    for name, slabs in ws.items():
        assert len(slabs) == dict(SLABS)[name], (name, len(slabs))
        for n, slab in enumerate(slabs):
            stream[SLAB_AT[name] + n] = slab
    cols, mats, rows, tab = constants(w)
    xt = np.ascontiguousarray(w["x"][0].reshape(T, KD, P).transpose(2, 1, 0))
    return {"stream_dram": stream, "x_dram": xt, "cols_dram": cols, "mats_dram": mats,
            "side_dram": side_weights(w), "rows_dram": rows, "tab_dram": tab}
```
